# Optimizing a Trainium2 kernel written in Bass

```python
import math
import jax
import jax.numpy as jnp
from jax import lax
import numpy as np

D_MODEL = 2048
BATCH = 1
SEQ = 256
DEPTH = 1
DEC_BATCH = 8
DEC_SEQ = 8
PAST_LEN = 256
PAGE_SIZE = 128

HEAD_DIM = 128
N_HEADS = 8
N_KV = 2
HPG = N_HEADS // N_KV
ATTN_DIM = N_HEADS * HEAD_DIM
KV_DIM = N_KV * HEAD_DIM
MIX_DIM = D_MODEL
CONV_DIM = MIX_DIM - ATTN_DIM
CONV_WIDTH = 3
CMP_BLOCK = 32
CMP_STRIDE = 16
CMP_HID = 2 * HEAD_DIM
SEL_BLOCK = 64
TOP_N = 8
WINDOW = 512
Q_BLOCK = 64
N_BUCKETS = 32
MAX_DIST = 128
N_KEYS = 128
N_EXPERTS = N_KEYS * N_KEYS
PEER_HEADS = 8
PEER_TOPK = 16
PEER_DK = 256
PEER_CHUNK = 128
PLE_DIM = 256
N_SLOTS = 4
N_BRANCH = 3
IN_COLS = ATTN_DIM + 6 * KV_DIM + N_BRANCH * N_HEADS + 3 * CONV_DIM
SPLITS = [ATTN_DIM, ATTN_DIM + 6 * KV_DIM, ATTN_DIM + 6 * KV_DIM + N_BRANCH * N_HEADS]
EPS = 1e-6
NEG = -1e30
FORCE = 1e4

kernel_name = "hybrid_nsa_shortconv_peer_step"

def rmsnorm(x, g):
    x32 = x.astype(jnp.float32)
    y = x32 * lax.rsqrt(jnp.mean(x32 * x32, axis=-1, keepdims=True) + EPS)
    return (y * g.astype(jnp.float32)).astype(x.dtype)

def rel_bucket(dist):
    n = jnp.maximum(dist, 0)
    exact = N_BUCKETS // 2
    nf = jnp.maximum(n, 1).astype(jnp.float32)
    large = exact + (jnp.log(nf / exact) / math.log(MAX_DIST / exact) * (N_BUCKETS - exact)).astype(jnp.int32)
    return jnp.where(n < exact, n, jnp.minimum(large, N_BUCKETS - 1))

def mix_inputs(h, g_norm, w_in, qk_gain):
    b, L, _ = h.shape
    z = rmsnorm(h, g_norm) @ w_in
    q, kv, gt, cv = jnp.split(z, SPLITS, axis=-1)
    q = rmsnorm(q.reshape(b, L, N_HEADS, HEAD_DIM), qk_gain[0])
    kv = kv.reshape(b, L, 6, N_KV, HEAD_DIM)
    rows = jnp.stack([kv[:, :, 0], kv[:, :, 1], rmsnorm(kv[:, :, 2], qk_gain[2]), kv[:, :, 3]], axis=2)
    wrows = jnp.stack([rmsnorm(kv[:, :, 4], qk_gain[3]), kv[:, :, 5]], axis=2)
    gates = jax.nn.sigmoid(gt.reshape(b, L, N_BRANCH, N_HEADS))
    b_gate, c_gate, hc = jnp.split(cv, 3, axis=-1)
    return q, rows, wrows, gates, b_gate, c_gate * hc

def compress(raw, pe, w1, w2):
    b, T = raw.shape[:2]
    m = CMP_BLOCK // CMP_STRIDE
    nch = T // CMP_STRIDE
    ncmp = nch - m + 1
    ch = raw[:, :nch * CMP_STRIDE].reshape(b, nch, CMP_STRIDE, N_KV, HEAD_DIM)
    part = jnp.einsum("bcsgd,msdh->bcmgh", ch, w1.reshape(m, CMP_STRIDE, HEAD_DIM, CMP_HID))
    hid = pe.reshape(-1) @ w1
    for i in range(m):
        hid = hid + part[:, i:i + ncmp, i]
    return jax.nn.gelu(hid) @ w2

def to_blocks(k):
    b, T = k.shape[:2]
    ns = max(-(-T // SEL_BLOCK), TOP_N)
    k = jnp.pad(k, ((0, 0), (0, ns * SEL_BLOCK - T), (0, 0), (0, 0)))
    return k.reshape(b, ns, SEL_BLOCK, N_KV, HEAD_DIM).transpose(0, 3, 1, 2, 4)

def nsa_keys(rows, pe, w1, w2, kc_gain):
    kc = rmsnorm(compress(rows[:, :, 0], pe[0], w1[0], w2[0]), kc_gain)
    vc = compress(rows[:, :, 1], pe[1], w1[1], w2[1])
    kc_end = jnp.arange(kc.shape[1]) * CMP_STRIDE + CMP_BLOCK - 1
    return kc, vc, kc_end, to_blocks(rows[:, :, 2]), to_blocks(rows[:, :, 3])

def nsa_attend(q, q_pos, gates, kc, vc, kc_end, ks_blk, vs_blk, kw, vw, kw_pos, rel_bias):
    b, nq = q.shape[:2]
    ns = ks_blk.shape[2]
    scale = HEAD_DIM ** -0.5
    qg = q.reshape(b, nq, N_KV, HPG, HEAD_DIM)
    tab = rel_bias.astype(jnp.float32)

    def dense(k, v, dist, valid):
        logits = jnp.einsum("bqgrd,bkgd->bgrqk", qg, k).astype(jnp.float32) * scale
        bias = tab[rel_bucket(dist)].transpose(2, 0, 1).reshape(N_KV, HPG, nq, -1)
        pr = jax.nn.softmax(jnp.where(valid, logits + bias, NEG), axis=-1)
        pr = jnp.where(valid, pr, 0.0)
        return jnp.einsum("bgrqk,bkgd->bqgrd", pr.astype(v.dtype), v), pr

    dist_c = q_pos[:, None] - kc_end[None, :]
    out_c, pr_c = dense(kc, vc, dist_c, dist_c >= 0)

    c_start = kc_end - CMP_BLOCK + 1
    s_start = jnp.arange(ns) * SEL_BLOCK
    inter = ((c_start[:, None] < s_start[None, :] + SEL_BLOCK) & (kc_end[:, None] >= s_start[None, :])).astype(jnp.float32)
    imp = jnp.einsum("bgrqn,ns->bgqs", pr_c, inter)
    cur = (q_pos // SEL_BLOCK)[:, None]
    sid = jnp.arange(ns)[None, :]
    imp = jnp.where((sid == 0) | (sid == cur) | (sid == cur - 1), FORCE, imp)
    imp = jnp.where(sid > cur, -jnp.inf, imp)
    _, top = lax.top_k(imp, TOP_N)
    take = jax.vmap(jax.vmap(lambda blk, ix: blk[ix]))
    nk = TOP_N * SEL_BLOCK
    ksel = take(ks_blk, top).reshape(b, N_KV, nq, nk, HEAD_DIM)
    vsel = take(vs_blk, top).reshape(b, N_KV, nq, nk, HEAD_DIM)
    kpos = (top[..., None] * SEL_BLOCK + jnp.arange(SEL_BLOCK)).reshape(b, N_KV, nq, nk)
    dist_s = q_pos[None, None, :, None] - kpos
    valid_s = (dist_s >= 0)[:, :, None]
    logits = jnp.einsum("bqgrd,bgqkd->bgrqk", qg, ksel).astype(jnp.float32) * scale
    bias_s = tab.reshape(N_BUCKETS, N_KV, HPG)[rel_bucket(dist_s), jnp.arange(N_KV)[None, :, None, None]]
    logits = logits + bias_s.transpose(0, 1, 4, 2, 3)
    pr_s = jax.nn.softmax(jnp.where(valid_s, logits, NEG), axis=-1)
    out_s = jnp.einsum("bgrqk,bgqkd->bqgrd", pr_s.astype(vsel.dtype), vsel)

    dist_w = q_pos[:, None] - kw_pos[None, :]
    valid_w = (kw_pos[None, :] >= 0) & (dist_w >= 0) & (dist_w < WINDOW)
    out_w, _ = dense(kw, vw, dist_w, valid_w)

    o = jnp.stack([out_c, out_s, out_w], axis=2)
    g = gates.reshape(b, nq, N_BRANCH, N_KV, HPG, 1).astype(o.dtype)
    return (o * g).sum(axis=2).reshape(b, nq, ATTN_DIM)

def nsa_prompt(q, gates, keys, wrows, rel_bias):
    kc, vc, kc_end, ks_blk, vs_blk = keys
    b, L = q.shape[:2]
    wpad = jnp.pad(wrows, ((0, 0), (WINDOW, 0), (0, 0), (0, 0), (0, 0)))

    def block(i):
        s = i * Q_BLOCK
        qb = lax.dynamic_slice_in_dim(q, s, Q_BLOCK, axis=1)
        gb = lax.dynamic_slice_in_dim(gates, s, Q_BLOCK, axis=1)
        wb = lax.dynamic_slice_in_dim(wpad, s, WINDOW + Q_BLOCK, axis=1)
        q_pos = s + jnp.arange(Q_BLOCK)
        kw_pos = s - WINDOW + jnp.arange(WINDOW + Q_BLOCK)
        return nsa_attend(qb, q_pos, gb, kc, vc, kc_end, ks_blk, vs_blk, wb[:, :, 0], wb[:, :, 1], kw_pos, rel_bias)

    out = lax.map(block, jnp.arange(L // Q_BLOCK))
    return out.transpose(1, 0, 2, 3).reshape(b, L, ATTN_DIM)

def short_conv(u, b_gate, prev, w, bias):
    ctx = jnp.concatenate([prev, u], axis=1)
    y = lax.conv_general_dilated(ctx, w[:, None, :], window_strides=(1,), padding="VALID",
                                 dimension_numbers=("NWC", "WIO", "NWC"), feature_group_count=CONV_DIM)
    return b_gate * (y + bias), ctx[:, -(CONV_WIDTH - 1):]

def merge_out(attn, conv, gain, w_out):
    a = rmsnorm(attn, gain[:ATTN_DIM])
    c = rmsnorm(conv, gain[ATTN_DIM:])
    return jnp.concatenate([a, c], axis=-1) @ w_out

def peer_ffn(n, wq, sub_keys, u_tab, v_tab):
    ntok = n.shape[0]
    nc = -(-ntok // PEER_CHUNK)
    xs = jnp.pad(n, ((0, nc * PEER_CHUNK - ntok), (0, 0))).reshape(nc, PEER_CHUNK, D_MODEL)
    ncand = PEER_TOPK * PEER_TOPK

    def chunk(xc):
        qh = (xc @ wq).reshape(PEER_CHUNK, PEER_HEADS, 2, PEER_DK // 2)
        s = jnp.einsum("trhk,hnk->trhn", qh, sub_keys).astype(jnp.float32)
        sv, si = lax.top_k(s, PEER_TOPK)
        cand = (sv[:, :, 0, :, None] + sv[:, :, 1, None, :]).reshape(PEER_CHUNK, PEER_HEADS, ncand)
        cidx = (si[:, :, 0, :, None] * N_KEYS + si[:, :, 1, None, :]).reshape(PEER_CHUNK, PEER_HEADS, ncand)
        fv, fi = lax.top_k(cand, PEER_TOPK)
        eidx = jnp.take_along_axis(cidx, fi, axis=-1)
        g = jax.nn.softmax(fv, axis=-1)
        act = jax.nn.gelu(jnp.einsum("td,trkd->trk", xc, u_tab[eidx]).astype(jnp.float32))
        return jnp.einsum("trk,trkd->td", (g * act).astype(xc.dtype), v_tab[eidx])

    return lax.map(chunk, xs).reshape(nc * PEER_CHUNK, D_MODEL)[:ntok]

def channel_ple(h, p, g2, wq, sub_keys, u_tab, v_tab, g3, w_gate, w_ple):
    b, L, _ = h.shape
    n = rmsnorm(h, g2).reshape(b * L, D_MODEL)
    h = h + peer_ffn(n, wq, sub_keys, u_tab, v_tab).reshape(b, L, D_MODEL)
    gate = jax.nn.sigmoid((rmsnorm(h, g3) @ w_gate).astype(jnp.float32)).astype(h.dtype)
    return h + gate * (p @ w_ple)

def setup_inputs(seed: int = 0) -> dict:
    key = jax.random.key(seed)
    ks = jax.random.split(key, 27)
    f32 = jnp.float32
    n_pages = PAST_LEN // PAGE_SIZE
    n_used = DEC_BATCH * n_pages
    n_pool = n_used + (n_used + 3) // 4
    win_len = min(WINDOW, PAST_LEN)

    def nrm(k, shape, scale):
        return jax.random.normal(k, shape, f32) * scale

    def gain(k, shape):
        return 1.0 + 0.05 * jax.random.normal(k, shape, f32)

    page_table = jax.random.permutation(ks[7], n_pool)[:n_used].reshape(DEC_BATCH, n_pages).astype(jnp.int32)
    return {
        "x_prompt": nrm(ks[0], (BATCH, SEQ, D_MODEL), 1.0),
        "x_sample": nrm(ks[1], (DEC_BATCH, DEC_SEQ, D_MODEL), 1.0),
        "p_prompt": nrm(ks[2], (DEPTH, BATCH, SEQ, PLE_DIM), 1.0),
        "p_sample": nrm(ks[3], (DEPTH, DEC_BATCH, DEC_SEQ, PLE_DIM), 1.0),
        "cache_kv": nrm(ks[4], (DEPTH, n_pool, PAGE_SIZE, N_SLOTS, N_KV, HEAD_DIM), 1.0),
        "state_win": nrm(ks[5], (DEPTH, DEC_BATCH, win_len, 2, N_KV, HEAD_DIM), 1.0),
        "state_conv": nrm(ks[6], (DEPTH, DEC_BATCH, CONV_WIDTH - 1, CONV_DIM), 1.0),
        "page_table": page_table,
        "rel_bias": nrm(ks[8], (N_BUCKETS, N_HEADS), 0.5),
        "norm1": gain(ks[9], (DEPTH, D_MODEL)),
        "w_in": nrm(ks[10], (DEPTH, D_MODEL, IN_COLS), D_MODEL ** -0.5),
        "qk_gain": gain(ks[11], (DEPTH, 4, HEAD_DIM)),
        "cmp_pe": nrm(ks[12], (DEPTH, 2, CMP_BLOCK, HEAD_DIM), 0.5),
        "cmp_w1": nrm(ks[13], (DEPTH, 2, CMP_BLOCK * HEAD_DIM, CMP_HID), (CMP_BLOCK * HEAD_DIM) ** -0.5),
        "cmp_w2": nrm(ks[14], (DEPTH, 2, CMP_HID, HEAD_DIM), CMP_HID ** -0.5),
        "conv_w": nrm(ks[15], (DEPTH, CONV_WIDTH, CONV_DIM), CONV_WIDTH ** -0.5),
        "conv_b": nrm(ks[16], (DEPTH, CONV_DIM), 0.02),
        "out_gain": gain(ks[17], (DEPTH, MIX_DIM)),
        "w_out": nrm(ks[18], (DEPTH, MIX_DIM, D_MODEL), MIX_DIM ** -0.5),
        "norm2": gain(ks[19], (DEPTH, D_MODEL)),
        "peer_wq": nrm(ks[20], (DEPTH, D_MODEL, PEER_HEADS * PEER_DK), D_MODEL ** -0.5),
        "peer_keys": nrm(ks[21], (DEPTH, 2, N_KEYS, PEER_DK // 2), (PEER_DK // 2) ** -0.5),
        "peer_u": nrm(ks[22], (DEPTH, N_EXPERTS, D_MODEL), D_MODEL ** -0.5),
        "peer_v": nrm(ks[23], (DEPTH, N_EXPERTS, D_MODEL), 0.3),
        "norm3": gain(ks[24], (DEPTH, D_MODEL)),
        "ple_gate": nrm(ks[25], (DEPTH, D_MODEL, D_MODEL), D_MODEL ** -0.5),
        "ple_proj": nrm(ks[26], (DEPTH, PLE_DIM, D_MODEL), PLE_DIM ** -0.5),
    }

def reference(x_prompt, x_sample, p_prompt, p_sample, cache_kv, state_win, state_conv, page_table,
              rel_bias, norm1, w_in, qk_gain, cmp_pe, cmp_w1, cmp_w2, conv_w, conv_b, out_gain, w_out,
              norm2, peer_wq, peer_keys, peer_u, peer_v, norm3, ple_gate, ple_proj):
    h_p, h_s = x_prompt, x_sample
    kv_p, win_p, conv_p, kv_s, win_s, conv_s = [], [], [], [], [], []
    n_dec = x_sample.shape[0]
    past_len = page_table.shape[1] * cache_kv.shape[2]
    win_len = state_win.shape[2]
    for l in range(DEPTH):
        b, L = h_p.shape[:2]
        q, rows, wrows, gates, bg, u = mix_inputs(h_p, norm1[l], w_in[l], qk_gain[l])
        keys = nsa_keys(rows, cmp_pe[l], cmp_w1[l], cmp_w2[l], qk_gain[l, 1])
        attn = nsa_prompt(q, gates, keys, wrows, rel_bias)
        prev0 = jnp.zeros((b, CONV_WIDTH - 1, CONV_DIM), u.dtype)
        conv, cst = short_conv(u, bg, prev0, conv_w[l], conv_b[l])
        h = h_p + merge_out(attn, conv, out_gain[l], w_out[l])
        h_p = channel_ple(h, p_prompt[l], norm2[l], peer_wq[l], peer_keys[l], peer_u[l], peer_v[l],
                          norm3[l], ple_gate[l], ple_proj[l])
        kv_p.append(rows)
        win_p.append(wrows[:, L - min(WINDOW, L):])
        conv_p.append(cst)

        Ls = h_s.shape[1]
        q, rows, wrows, gates, bg, u = mix_inputs(h_s, norm1[l], w_in[l], qk_gain[l])
        past = cache_kv[l][page_table].reshape(n_dec, past_len, N_SLOTS, N_KV, HEAD_DIM)
        keys = nsa_keys(jnp.concatenate([past, rows], axis=1), cmp_pe[l], cmp_w1[l], cmp_w2[l], qk_gain[l, 1])
        wctx = jnp.concatenate([state_win[l], wrows], axis=1)
        q_pos = past_len + jnp.arange(Ls)
        kw_pos = past_len - win_len + jnp.arange(win_len + Ls)
        attn = nsa_attend(q, q_pos, gates, *keys, wctx[:, :, 0], wctx[:, :, 1], kw_pos, rel_bias)
        conv, cst = short_conv(u, bg, state_conv[l], conv_w[l], conv_b[l])
        h = h_s + merge_out(attn, conv, out_gain[l], w_out[l])
        h_s = channel_ple(h, p_sample[l], norm2[l], peer_wq[l], peer_keys[l], peer_u[l], peer_v[l],
                          norm3[l], ple_gate[l], ple_proj[l])
        kv_s.append(rows)
        win_s.append(wctx[:, -win_len:])
        conv_s.append(cst)
    return (h_p, h_s, jnp.stack(kv_p), jnp.stack(win_p), jnp.stack(conv_p), jnp.stack(kv_s), jnp.stack(win_s), jnp.stack(conv_s))


_drawn_inputs = setup_inputs


def setup_inputs(seed=0):
    import zlib

    import numpy as np

    out = dict(_drawn_inputs(seed))
    spreads = {}
    factors = {'conv_b': 3.846, 'norm3': 8.0}
    for name, (base, spread) in spreads.items():
        noise = np.random.default_rng([zlib.crc32(name.encode()), seed]).standard_normal(out[name].shape)
        drawn = base * np.exp(spread * noise) if base else spread * noise
        out[name] = jnp.asarray(drawn.astype(out[name].dtype))
    for name, factor in factors.items():
        out[name] = (out[name] * factor).astype(out[name].dtype)
    return out
```

```python
import math
from contextlib import ExitStack

import numpy as np
import concourse.bass as bass
from concourse import mybir

D = 2048
KC = D // 128
NP, NB, NT = 256, 8, 8
PAST, PAGE = 256, 128
HD, NH, NG = 128, 8, 2
HPG = NH // NG
ATT = NH * HD
CONV = D - ATT
KVC = 6 * NG * HD
QKV = ATT + KVC
GATES = 3 * NH
BLK, STRIDE, HID = 32, 16, 256
NWIN = PAST // STRIDE - 1
SEQS = (1 + NB) * NG
PH, PK, NKEY = 8, 16, 128
PLE = 256
EPS, NEG = 1e-6, -1e30
ROWS = (128, 128, NB * NT)
TOK = sum(ROWS)
NBUCKET, MAXDIST = 32, 128
DMAX = PAST + NT - 1
NBIAS = DMAX + 128

C_ID = 0
C_IOTA = C_ID + 128
C_PAIR = C_IOTA + PK * PK
C_SELG = C_PAIR + 64
C_HM = C_SELG + 4 * 128
C_VM = C_HM + GATES
C_OH = C_VM + 1
NCST = C_OH + NBIAS


def shape_constants():
    c = np.zeros((128, NCST), np.float32)
    p = np.arange(128)
    c[:, C_ID:C_ID + 128] = np.eye(128, dtype=np.float32)
    c[:, C_IOTA:C_IOTA + PK * PK] = np.arange(PK * PK) % PK
    c[p, C_PAIR + p % 64] = 1.0
    for s in range(4):
        tok = (2 * s + p // 64) * NT + p % NT
        c[tok, C_SELG + s * 128 + p] = 1.0
    for br in range(3):
        c[p, C_HM + br * NH + (p % 64) // NT] = 1.0
    c[BLK - 1:, C_VM] = 1.0
    dist = DMAX - np.arange(NBIAS)
    n = np.maximum(dist, 0)
    exact = NBUCKET // 2
    nf = np.maximum(n, 1).astype(np.float32)
    large = exact + (np.log(nf / np.float32(exact)) / np.float32(math.log(MAXDIST / exact))
                     * np.float32(NBUCKET - exact)).astype(np.int32)
    bucket = np.where(n < exact, n, np.minimum(large, NBUCKET - 1))
    bucket = np.where(dist >= 0, bucket, NBUCKET)
    c[bucket, C_OH + np.arange(NBIAS)] = 1.0
    return c


def build(nc, I, O):
    fp32, i32, u32 = mybir.dt.float32, mybir.dt.int32, mybir.dt.uint32
    ALU, ACT, AX = mybir.AluOpType, mybir.ActivationFunctionType, mybir.AxisListType
    ctx = ExitStack()
    PITCH = 53200
    arena = ctx.enter_context(nc.sbuf_tensor("arena", [128, PITCH], fp32))
    bank = [ctx.enter_context(nc.psum_tensor(f"bank{i}", [128, 512], fp32)) for i in range(8)]
    bias_dram = nc.dram_tensor("bias_rows", (NH, 128, NBIAS), fp32, kind="Internal").ap()

    def sem(name):
        return ctx.enter_context(nc.semaphore(name))

    def buf(off, *dims):
        n = math.prod(dims)
        assert off + n <= PITCH
        a = arena[:, off:off + n]
        if len(dims) == 1:
            return a
        names = "abcde"[:len(dims)]
        return a.rearrange(f"p ({' '.join(names)}) -> p {' '.join(names)}",
                           **{x: d for x, d in zip(names[1:], dims[1:])})

    def rep(ap, *dims):
        return bass.AP(ap.tensor, ap.offset, [list(ap.ap[0])] + [list(d) for d in dims])

    T0 = 0
    W0 = T0 + KC * 384
    Z0 = W0 + 4 * 8 * 512
    ZC0 = Z0 + 3 * 2560
    X0 = ZC0 + 9 * 1024
    K0 = X0 + 3 * 1024

    xT = buf(T0, KC, 384)
    ring = [buf(W0 + s * 4096, 8, 512) for s in range(4)]
    z = buf(Z0, 3, 2560)
    h = buf(Z0, 3, D)
    n_tok = buf(Z0 + 3 * D, 3, D)
    bg, cu, sh1 = (buf(ZC0 + i * 3072, 3, 1024) for i in range(3))
    sh2 = buf(X0, 3, 1024)
    att = buf(X0, 3, 1024)

    cst = buf(K0, NCST)
    ident = cst[:, C_ID:C_ID + 128]
    gT = buf(K0 + NCST, 4, KC)
    qg = buf(K0 + NCST + 64, 4, HD)
    gate = buf(K0 + NCST + 576, 3, GATES)
    bias_s = buf(K0 + NCST + 648, DMAX + 1)
    bias_p = buf(K0 + NCST + 912, NH, 256)
    g2 = buf(K0 + NCST + 912, D)
    cw = buf(K0 + NCST + 912 + 2048, 4, CONV)
    S0 = K0 + NCST + 912 + 2048 + 4096
    stats = buf(S0, 256)
    tab = buf(S0 + 256, NH)
    bias_row = buf(S0 + 264, NBIAS)
    g24 = buf(S0 + 264, 4, 3, NH)
    gs = buf(S0 + 368, 4, 3)
    pages = buf(S0 + 656, 2 * NB).bitcast(i32)
    w4 = buf(S0 + 672, 2, 4)
    a4 = buf(S0 + 680, 2, 4)
    idx4 = buf(S0 + 688, 2, 4).bitcast(i32)
    diag = buf(S0 + 700, 2, 4, 128)
    vn = buf(K0 + NCST + 912 + 2048, NB, 2, 256)
    qsT = buf(S0 + 1724, NB, NH, NT)

    qkT = buf(W0, 16, TOK)
    w1 = buf(W0 + 5120, BLK, HID)
    page_in = buf(W0 + 13312, 2, 2, 256)
    hid = buf(W0 + 13312 + 1024, 2, SEQS * NWIN)
    w2 = buf(W0 + 14880, 2, HD)
    kcT = buf(W0 + 15136, SEQS * NWIN)
    kct = buf(W0 + 15408, 3, HD)
    pe_in = buf(W0 + 15792, HD)
    pecol = buf(W0 + 15920, 2)
    raw = buf(T0, SEQS + 1, 256)
    vc = buf(T0 + 3840, SEQS, HD)

    def past_rows(s, bb, br, a):
        return buf(W0 + 5120 + (((s % 2) * 2 + bb) * 2 + br) * 1024 + a * 512, 512)

    pastT = buf(ZC0 + 3072, 2, 2, 2, 2, HD)
    pb = buf(T0, 2, 544)
    pT = buf(T0 + 1088, 2, 896)
    attT = buf(T0 + 2880, NH, NB * NT)
    mx, nm, sm, cf = (buf(S0 + 200 + 6 * i, 2, 3) for i in range(4))
    qT = buf(Z0 + 6 * D, KC, 384)
    keys_in = buf(K0 + NCST + 2960, 2, 128)
    keysT = buf(K0 + NCST + 2960 + 256, 2, 128)
    sv = buf(K0 + NCST + 2960 + 512, 16, PK)
    si = buf(K0 + NCST + 2960 + 768, 16, PK)
    fv = buf(K0 + NCST + 2960 + 1024, PH, PK)
    fi = buf(K0 + NCST + 2960 + 1152, PH, PK)
    fh = buf(K0 + NCST + 2960 + 1280, PH, PK)
    fl = buf(K0 + NCST + 2960 + 1408, PH, PK)
    e0 = buf(K0 + NCST + 2960 + 1536, PH, PK)
    e1 = buf(K0 + NCST + 2960 + 1664, PH, PK)
    wgt = buf(K0 + NCST + 2960 + 1792, 3, 128)
    idx = buf(K0 + NCST + 2960 + 2176, 3, 128).bitcast(i32)
    score = buf(T0, 3, D)
    cand = buf(Z0 + 6 * D, PH, PK, PK)
    scr = buf(Z0 + 7 * D, PH, PK, PK)
    u_row = [buf(W0 + j * D, D) for j in range(4)]
    v_row = [buf(W0 + (4 + j) * D, D) for j in range(4)]
    ple_w = buf(Z0 + 6 * D, 2, D)
    p_in = buf(K0 + NCST + 3984, 3, PLE)
    pleT = buf(K0 + NCST + 3984 + 768, 2, TOK)
    sig = buf(K0 + NCST + 912, 2, 3, 512)

    x_in, cst_in, small_in, cw_in, dve_step, hn_ready = map(sem, ("x_in", "cst_in", "small_in", "cw_in", "dve_step", "hn_ready"))
    v_ready, root_ready = sem("v_ready"), sem("root_ready")
    t_mm, t_ev = sem("t_mm"), [sem("t_ev_dve"), sem("t_ev_act")]
    bias_mm, bias_sb, bias_out, bias_in = map(sem, ("bias_mm", "bias_sb", "bias_out", "bias_in"))
    w_in = [sem(f"w_in{s}") for s in range(4)]
    w_used, mm_done, mm_ev = map(sem, ("w_used", "mm_done", "mm_ev"))
    gate_ready = sem("gate_ready")
    u_ready, shift_a, shift_b, out_done = map(sem, ("u_ready", "shift_a", "shift_b", "out_done"))
    qkv_ready, vn_in = sem("qkv_ready"), sem("vn_in")
    w1_in, w2_in, pe_in_s, page_s, page_used = sem("w1_in"), sem("w2_in"), sem("pe_in"), [sem("page_in0"), sem("page_in1")], sem("page_used")
    raw_ready, cmp_mm, hid_ready, kc_mm, kc_ready, kcT_mm, cmp_done = map(sem, (
        "raw_ready", "cmp_mm", "hid_ready", "kc_mm", "kc_ready", "kcT_mm", "cmp_done"))
    s_mm, biased, exp_done, p_scaled, pt_mm, pt_ev, o_mm, o_ev = map(sem, (
        "s_mm", "biased", "exp_done", "p_scaled", "pt_mm", "pt_ev", "o_mm", "o_ev"))
    past_in, gs_mm = [sem("past_in0"), sem("past_in1")], sem("gs_mm")
    attT_mm, attT_ev = sem("attT_mm"), sem("attT_ev")
    merged, dup_in, n2_ready = sem("merged"), sem("dup_in"), sem("n2_ready")
    h_ready = sem("h_ready")
    keys_s, keys_mm, keys_ev, sc_mm, sc_ev, qT_done = map(sem, ("keys_in", "keys_mm", "keys_ev", "sc_mm", "sc_ev", "qT_done"))
    e_in, e_out, idx_ready = sem("e_in"), sem("e_out"), sem("idx_ready")
    idx_set, u_used, v_used = sem("idx_set"), sem("u_used"), sem("v_used")
    u_in = [sem(f"u_in{j}") for j in range(4)]
    v_in = [sem(f"v_in{j}") for j in range(4)]
    dots, gelu_done, diag_ready, peer_mm = map(sem, ("dots", "gelu_done", "diag_ready", "peer_mm"))
    ple_in, pleT_mm, pleT_ev, ple_mm, sig_ready, y_ready = map(sem, ("ple_in", "pleT_mm", "pleT_ev", "ple_mm", "sig_ready", "y_ready"))
    loop_step, slot_seen = sem("loop_step"), sem("slot_seen")

    N_Z, N_OUT, N_WQ, N_GATE = 0, 12, 16, 20
    w_in_cols = [QKV + GATES + 512 * i for i in range(6)] + [512 * i for i in range(5)] + [QKV]
    TBLOCKS = [HD * i for i in range(NH)] + [1024, 1152, 1280, 1408, 1536, 1664, 2048, 2176]
    GROUPS = (PH * PK // 4, PH * PK // 4, PH * PK // 8)

    w_view = {
        "in": I["w_in"][0].rearrange("(k p) n -> p k n", p=128),
        "out": I["w_out"][0].rearrange("(k p) n -> p k n", p=128),
        "wq": I["peer_wq"][0].rearrange("(k p) n -> p k n", p=128),
        "gate": I["ple_gate"][0].rearrange("(k p) n -> p k n", p=128),
    }
    xp = I["x_prompt"][0].rearrange("(t p) d -> t p d", p=128)
    xs = I["x_sample"].rearrange("b t d -> (b t) d")
    cache = I["cache_kv"][0].rearrange("n p s g d -> n p (s g d)")
    swin = I["state_win"][0].rearrange("b (a p) s g d -> b p a (s g d)", p=128)
    kv_p = O[2][0].rearrange("b (t p) s g d -> (b t) p (s g d)", p=128)
    win_p = O[3][0].rearrange("b (t p) s g d -> (b t) p (s g d)", p=128)
    kv_s = O[5][0].rearrange("b t s g d -> (b t) (s g d)")
    win_s = O[6][0].rearrange("b t s g d -> b t (s g d)")

    block = ctx.enter_context(nc.Block())

    @block.sync
    def _(sp):
        def tiles_of(src_p, src_s, dst, s):
            for t in range(2):
                sp.dma_start(dst[:, t, :], src_p[t]).then_inc(s, 16)
            sp.dma_start(dst[0:64, 2, :], src_s).then_inc(s, 16)

        sp.dma_start(cst, I["cst"]).then_inc(cst_in, 16)
        tiles_of(xp, xs, h, x_in)
        for i, name in enumerate(("norm1", "norm2", "norm3", "out_gain")):
            with nc.allow_non_contiguous_dma(reason="a gain by channel"):
                sp.dma_start(gT[:, i, :], I[name][0].rearrange("(k p) -> p k", p=128)).then_inc(small_in, 16)
        sp.dma_start(tab[0:NBUCKET, :], I["rel_bias"]).then_inc(small_in, 16)
        sp.dma_start(pages[0:1, :], I["page_table"].rearrange("(o b) n -> o (b n)", o=1)).then_inc(small_in, 16)
        sp.dma_start(qg, bass.AP(I["qk_gain"].tensor, 0, [[0, 128], [HD, 4], [1, HD]])).then_inc(small_in, 16)
        sp.dma_start(cw[:, 0:3, :], bass.AP(I["conv_w"].tensor, 0, [[0, 128], [CONV, 3], [1, CONV]])).then_inc(cw_in, 16)
        sp.dma_start(cw[:, 3, :], bass.AP(I["conv_b"].tensor, 0, [[0, 128], [1, CONV]])).then_inc(cw_in, 16)

        def fill(f, src, n=512):
            sp.wait_ge(w_used, f + 1)
            sp.dma_start(ring[f % 4][:, :, 0:n], src).then_inc(w_in[f % 4], 16)

        for blk, c0 in enumerate(w_in_cols):
            n = GATES if blk == 11 else 512
            for half in range(2):
                fill(2 * blk + half, w_view["in"][:, 8 * half:8 * half + 8, c0:c0 + n], n)
        sp.dma_start(win_s[:, 0:PAST - NT, :], I["state_win"][0].rearrange("b t s g d -> b t (s g d)")[:, NT:, :])\
          .then_inc(out_done, 16)

        sp.wait_ge(bias_sb, 1)
        sp.dma_start(bias_dram, rep(bias_row[0:NH, :], [0, 128], [1, NBIAS])).then_inc(bias_out, 16)
        sp.wait_ge(bias_out, 16)
        bt = bias_dram.tensor
        sp.dma_start(bias_p, bass.AP(bt, DMAX - 128, [[NBIAS - 1, 128], [128 * NBIAS, NH], [1, 256]])).then_inc(bias_in, 16)
        for r in range(2 * NH):
            sp.dma_start(bias_s[NT * r:NT * r + NT, :],
                         bass.AP(bt, (r % NH) * 128 * NBIAS + DMAX - PAST, [[NBIAS - 1, NT], [1, DMAX + 1]])).then_inc(bias_in, 16)

        sp.wait_ge(u_ready, 1)
        sp.dma_start(O[4][0, 0], cu[126:128, 1, :]).then_inc(out_done, 16)
        for w in range(2):
            sp.dma_start(O[7][0][:, w, :], cu[NT - 2 + w:64:NT, 2, :]).then_inc(out_done, 16)
        for d, dst in ((1, sh1), (2, sh2)):
            for t in range(3):
                sp.dma_start(dst[d:ROWS[t], t, :], cu[0:ROWS[t] - d, t, :]).then_inc(shift_a, 16)
            sp.dma_start(dst[0:d, 1, :], cu[128 - d:128, 0, :]).then_inc(shift_a, 16)
        sp.wait_ge(shift_a, 8 * 16)
        sc = I["state_conv"][0]
        sp.dma_start(sh1[0:64:NT, 2, :], sc[:, 1, :]).then_inc(shift_b, 16)
        sp.dma_start(sh2[0:64:NT, 2, :], sc[:, 0, :]).then_inc(shift_b, 16)
        sp.dma_start(sh2[1:64:NT, 2, :], sc[:, 1, :]).then_inc(shift_b, 16)

        sp.wait_ge(qkv_ready, 1)
        for t in range(2):
            sp.dma_start(kv_p[t], z[:, t, 1024:2048]).then_inc(out_done, 16)
            sp.dma_start(win_p[t], z[:, t, 2048:2560]).then_inc(out_done, 16)
        sp.dma_start(kv_s, z[0:64, 2, 1024:2048]).then_inc(out_done, 16)
        for b in range(NB):
            sp.dma_start(win_s[b, PAST - NT:PAST, :], z[b * NT:b * NT + NT, 2, 2048:2560]).then_inc(out_done, 16)
            for i, c0 in enumerate((1792, 2304)):
                sp.dma_start(vn[0:NT, b, i, :], z[b * NT:b * NT + NT, 2, c0:c0 + 256]).then_inc(vn_in, 16)

        def page(b, a):
            return sp.value_load(pages[0:1, 2 * b + a:2 * b + a + 1], min_val=0, max_val=I["cache_kv"].shape[1] - 1)

        sp.wait_ge(mm_done, 12)
        for kind in range(2):
            if kind:
                sp.wait_ge(cmp_mm, 2)
                sp.wait_ge(kc_mm, 1)
            sp.dma_start(w1, I["cmp_w1"][0, kind].rearrange("(m d) h -> d m h", d=HD)).then_inc(w1_in, 16)
            sp.dma_start(w2, I["cmp_w2"][0, kind].rearrange("(a p) h -> p a h", p=128)).then_inc(w2_in, 16)
            sp.dma_start(pe_in[0:BLK, :], I["cmp_pe"][0, kind]).then_inc(pe_in_s, 16)
            for b in range(NB):
                if NB * kind + b >= 2:
                    sp.wait_ge(page_used, NB * kind + b - 1)
                for a in range(2):
                    sp.dma_start(page_in[:, b % 2, a, :],
                                 cache[bass.ds(page(b, a), 1), :, 256 * kind:256 * kind + 256]
                                 .rearrange("o p n -> p (o n)")).then_inc(page_s[b % 2], 16)

        sp.wait_ge(cmp_mm, 4)
        for s in range(NB // 2):
            if s >= 2:
                sp.wait_ge(o_mm, 16 + s - 1)
            for bb in range(2):
                b = 2 * s + bb
                for a in range(2):
                    sp.dma_start(past_rows(s, bb, 0, a),
                                 cache[bass.ds(page(b, a), 1), :, 512:1024].rearrange("o p n -> p (o n)"))\
                      .then_inc(past_in[s % 2], 16)
                sp.dma_start(buf(W0 + 5120 + (((s % 2) * 2 + bb) * 2 + 1) * 1024, 2, 512), swin[b]).then_inc(past_in[s % 2], 16)

        sp.wait_ge(merged, 1)
        tiles_of(xp, xs, h, x_in)
        for blk in range(4):
            for half in range(2):
                fill(2 * (N_OUT + blk) + half, w_view["out"][:, 8 * half:8 * half + 8, 512 * blk:512 * blk + 512])
        sp.dma_start(g2, bass.AP(I["norm2"].tensor, 0, [[0, 128], [1, D]])).then_inc(dup_in, 16)
        sp.dma_start(keys_in, I["peer_keys"][0].rearrange("a n k -> n a k")).then_inc(keys_s, 16)
        sp.wait_ge(h_ready, 1)
        sp.dma_start(h[64:128, 2, :], h[0:64, 2, :]).then_inc(dup_in, 16)
        for blk in range(4):
            for half in range(2):
                fill(2 * (N_WQ + blk) + half, w_view["wq"][:, 8 * half:8 * half + 8, 512 * blk:512 * blk + 512])
        sp.wait_ge(idx_ready, 3)
        sp.dma_start(ple_w, I["ple_proj"][0].rearrange("(k p) n -> p k n", p=128)).then_inc(ple_in, 16)
        sp.wait_ge(h_ready, 2)
        tiles_of(I["p_prompt"][0, 0].rearrange("(t p) d -> t p d", p=128),
                 I["p_sample"][0].rearrange("b t d -> (b t) d"), p_in, ple_in)
        for blk in range(4):
            for half in range(2):
                fill(2 * (N_GATE + blk) + half, w_view["gate"][:, 8 * half:8 * half + 8, 512 * blk:512 * blk + 512])
        yp = O[0][0].rearrange("(t p) d -> t p d", p=128)
        ys = O[1].rearrange("b t d -> (b t) d")
        for blk in range(4):
            sp.wait_ge(y_ready, blk + 1)
            cols = slice(512 * blk, 512 * blk + 512)
            for t in range(3):
                dst = yp[t][:, cols] if t < 2 else ys[:, cols]
                sp.dma_start(dst, h[0:ROWS[t], t, cols]).then_inc(out_done, 16)
        sp.wait_ge(out_done, 16 * (1 + 3 + 5 + NB + 12))

    @block.gpsimd
    def _(pool):
        def gathers(k, par):
            pool.wait_ge(idx_set, k + 1)
            for j in range(4):
                pool.wait_ge(u_used, 4 * k + j + 1)
                pool.sem_inc(slot_seen, 1)
                pool.indirect_dma_start(u_row[j], None, I["peer_u"][0],
                                        bass.IndirectOffsetOnAxis(idx4[:, par, j:j + 1], 0)).then_inc(u_in[j], 16)
            for j in range(4):
                pool.wait_ge(v_used, 4 * k + j + 1)
                pool.sem_inc(slot_seen, 1)
                pool.indirect_dma_start(v_row[j], None, I["peer_v"][0],
                                        bass.IndirectOffsetOnAxis(idx4[:, par, j:j + 1], 0)).then_inc(v_in[j], 16)

        base = 0
        for t in range(3):
            gathers(base, 0)
            with pool.Fori(0, (GROUPS[t] - 2) // 2) as i:
                for jj in range(2):
                    gathers(i * 2 + (base + 1 + jj), (1 + jj) % 2)
            gathers(base + GROUPS[t] - 1, 1)
            base += GROUPS[t]

    @block.scalar
    def _(act):
        act.sem_inc(mm_ev, 2)
        roots = [0]

        def root(src, dst):
            roots[0] += 1
            act.wait_ge(v_ready, roots[0])
            act.activation(dst, src, ACT.Sqrt).then_inc(root_ready, 1)

        tcount = [0]

        def odd_transposes(n, put):
            for c in range(1, n, 2):
                act.wait_ge(t_mm, tcount[0] + c + 1)
                put(act, c).then_inc(t_ev[1], 1)
            tcount[0] += n

        root(stats[:, 0:3], stats[:, 3:6])
        act.wait_ge(small_in, 16 * 7)
        odd_transposes(KC, lambda e, c: e.activation(xT[:, c, 0:TOK], bank[7][:, 0:TOK], ACT.Copy, scale=gT[:, 0, c:c + 1]))

        def z_out(n, wait, dst):
            act.wait_ge(mm_done, wait)
            for t in range(3):
                ins = act.activation(dst(t), bank[3 * (n % 2) + t][0:ROWS[t], :], ACT.Copy)
            ins.then_inc(mm_ev, 1)

        for part, region in enumerate((bg, cu, sh1)):
            with act.Fori(part, part + 1) as i:
                for j in range(2):
                    z_out(j, i * 2 + j + 1, lambda t: region[0:ROWS[t], t, 512 * j:512 * j + 512])
        with act.Fori(0, 2) as i:
            for j in range(2):
                z_out(j, i * 2 + 6 + j + 1, lambda t: z[0:ROWS[t], t, bass.ds(i * 1024 + 512 * j, 512)])
        z_out(10, 11, lambda t: z[0:ROWS[t], t, 2048:2560])
        act.wait_ge(mm_done, 12)
        for t in range(3):
            ins = act.activation(gate[0:ROWS[t], t, :], bank[3 + t][0:ROWS[t], 0:GATES], ACT.Sigmoid)
        ins.then_inc(mm_ev, 1)
        root(stats[:, 36:72], stats[:, 72:108])

        def heads_out(e, c):
            ins = e.activation(qkT[:, c, :], bank[7][:, 0:TOK], ACT.Copy)
            if c < NH:
                ins = e.activation(qsT[:, :, c, :], bank[7][:, 256:TOK].rearrange("p (b t) -> p b t", b=NB), ACT.Copy)
            return ins
        odd_transposes(16, heads_out)

        for kind in range(2):
            if kind:
                act.wait_ge(cmp_mm, 2)
            act.activation(raw[:, 0:NG, :], qkT[:, 8 + 2 * kind:10 + 2 * kind, 0:256], ACT.Copy).then_inc(raw_ready, 1)

            def raw_out(e, c):
                dst = raw[:, 2 + 2 * c:4 + 2 * c, :].rearrange("p g (a x) -> p a g x", a=2)
                return e.activation(dst, bank[7][:, :].rearrange("p (a g x) -> p a g x", a=2, g=2), ACT.Copy)
            odd_transposes(NB, raw_out)
            odd_transposes(1, raw_out)
            for hb in range(2):
                act.wait_ge(cmp_mm, 2 * kind + hb + 1)
                act.activation(pecol[:, hb:hb + 1], bank[hb][:, SEQS * NWIN:SEQS * NWIN + 1], ACT.Copy).then_inc(e_out, 1)
                act.wait_ge(e_out, 2 * kind + hb + 1)
                act.activation(hid[:, hb, :], bank[hb][:, 0:SEQS * NWIN], ACT.Gelu_apprx_tanh,
                               bias=pecol[:, hb:hb + 1]).then_inc(hid_ready, 1)
            if kind == 0:
                root(stats[:, 108:111], stats[:, 111:114])

        def softmax_exp(u, rows_list, par):
            act.wait_ge(biased, u + 1)
            for br, ap in rows_list:
                ins = act.activation(ap, ap, ACT.Exp, bias=nm[:, par, br:br + 1], accum_out=sm[:, par, br:br + 1])
            ins.then_inc(exp_done, 1)

        def prompt_pt(u):
            t = u // NH
            act.wait_ge(pt_mm, u + 1)
            if t:
                act.activation(pT[:, u % 2, 0:512], bank[4 + u % 2][:, :], ACT.Copy)
            else:
                act.activation(pT[:, u % 2, 0:512].rearrange("p (a b) -> p a b", a=2)[:, :, 0:128],
                               bank[4 + u % 2][:, :].rearrange("p (a b) -> p a b", a=2)[:, :, 0:128], ACT.Copy)
            nc_ = NWIN if t else 7
            act.activation(pT[0:nc_, u % 2, 512:640], bank[2 + u % 2][0:nc_, 128:256], ACT.Copy).then_inc(pt_ev, 1)

        def prompt_o(u):
            t, hh = u // NH, u % NH
            act.wait_ge(o_mm, u + 1)
            act.activation(att[:, t, hh * HD:hh * HD + HD], bank[6 + u % 2][:, 0:HD], ACT.Copy).then_inc(o_ev, 1)

        def prompt_rows(u):
            t = u // NH
            nk = 128 * (t + 1)
            return [(0, pb[:, u % 2, 512:512 + (NWIN if t else 7)]), (1, pb[:, u % 2, 0:nk]), (2, pb[:, u % 2, 256:256 + nk])]

        for u in range(17):
            if u < 16:
                softmax_exp(u, prompt_rows(u), u % 2)
            if u:
                prompt_pt(u - 1)
            if u > 1:
                prompt_o(u - 2)
        prompt_o(15)

        for s in range(4):
            u = 16 + s
            odd_transposes(4, lambda e, c: e.activation(
                pastT[:, c // 2, c % 2].rearrange("p a b d -> p (a b d)"), bank[7][:, :], ACT.Copy))
            softmax_exp(u, [(0, pb[:, 0, 528:528 + NWIN]), (1, pb[:, 0, 0:264]), (2, pb[:, 0, 264:528])], 0)
            act.wait_ge(pt_mm, u + 1)
            act.activation(pT[:, 0, 0:512], bank[4][:, :], ACT.Copy)
            act.activation(pT[0:NT, 0, 512:768], bank[5][0:NT, 0:256], ACT.Copy)
            act.activation(pT[0:NWIN, 0, 768:896], bank[5][0:NWIN, 256:384], ACT.Copy).then_inc(pt_ev, 1)
            act.wait_ge(o_mm, u + 1)
            for bb in range(2):
                ins = act.activation(attT[:, :, (2 * s + bb) * NT:(2 * s + bb) * NT + NT],
                                     bank[5][:, 384 + 64 * bb:448 + 64 * bb].rearrange("p (h t) -> p h t", h=NH), ACT.Copy)
            ins.then_inc(o_ev, 1)
        for i in range(2):
            act.wait_ge(attT_mm, i + 1)
            act.activation(att[0:64, 2, 512 * i:512 * i + 512], bank[i][0:64, :], ACT.Copy).then_inc(attT_ev, 1)
        root(stats[:, 120:126], stats[:, 126:132])
        odd_transposes(KC, lambda e, c: e.activation(xT[:, c, 0:TOK], bank[7][:, 0:TOK], ACT.Copy, scale=gT[:, 3, c:c + 1]))

        root(stats[:, 136:139], stats[:, 139:142])
        odd_transposes(KC, lambda e, c: e.activation(xT[:, c, :], bank[7][:, 0:384], ACT.Copy))
        for blk in range(4):
            act.wait_ge(mm_done, N_WQ + blk + 1)
            for sub in range(4):
                ins = act.activation(qT[:, 4 * blk + sub, :], bank[4 * (blk % 2) + sub][:, 0:384], ACT.Copy)
            ins.then_inc(qT_done, 1)
        act.wait_ge(keys_mm, 1)
        act.activation(keysT, bank[0][:, 0:256].rearrange("p (a b) -> p a b", a=2), ACT.Copy).then_inc(keys_ev, 1)
        for t in range(3):
            for q in range(4):
                act.wait_ge(sc_mm, 4 * t + q + 1)
                act.activation(score[:, t, 512 * q:512 * q + 512], bank[4 * (t % 2) + q][:, :], ACT.Copy).then_inc(sc_ev, 1)
        for t in range(3):
            act.wait_ge(e_in, t + 1)
            act.activation(fv, fv, ACT.Exp).then_inc(e_out, 1)

        def gelu(k, par):
            act.wait_ge(dots, k + 1)
            act.activation(w4[:, par, :], a4[:, par, :], ACT.Gelu_apprx_tanh).then_inc(gelu_done, 1)

        base = 0
        for t in range(3):
            gelu(base, 0)
            with act.Fori(0, (GROUPS[t] - 2) // 2) as i:
                for jj in range(2):
                    gelu(i * 2 + (base + 1 + jj), (1 + jj) % 2)
            gelu(base + GROUPS[t] - 1, 1)
            base += GROUPS[t]

        root(stats[:, 144:147], stats[:, 147:150])
        odd_transposes(KC, lambda e, c: e.activation(xT[:, c, 0:TOK], bank[7][:, 0:TOK], ACT.Copy, scale=gT[:, 2, c:c + 1]))
        for blk in range(4):
            act.wait_ge(mm_done, N_GATE + blk + 1)
            if blk >= 2:
                act.wait_ge(y_ready, blk - 1)
            for t in range(3):
                ins = act.activation(sig[0:ROWS[t], blk % 2, t, :], bank[t][0:ROWS[t], :], ACT.Sigmoid)
            ins.then_inc(sig_ready, 1)

    @block.vector
    def _(dve):
        steps = [0]

        def step(ins):
            steps[0] += 1
            ins.then_inc(dve_step, 1)
            dve.wait_ge(dve_step, steps[0])

        roots = [0]

        def inv_rms(ss, v, y, t, width):
            step(dve.tensor_scalar(v, ss, 1.0 / width, EPS, ALU.mult, ALU.add))
            dve.sem_inc(v_ready, 1)
            roots[0] += 1
            dve.wait_ge(root_ready, roots[0])
            step(dve.reciprocal(y, y))
            step(dve.tensor_tensor(t, y, y, ALU.mult))
            step(dve.tensor_tensor(t, t, v, ALU.mult))
            step(dve.tensor_scalar(t, t, -0.5, 1.5, ALU.mult, ALU.add))
            step(dve.tensor_tensor(y, y, t, ALU.mult))

        tcount = [0]

        def even_transposes(n, put):
            for c in range(0, n, 2):
                dve.wait_ge(t_mm, tcount[0] + c + 1)
                put(dve, c).then_inc(t_ev[0], 1)
            tcount[0] += n

        def squares(src, junk, acc):
            return dve.tensor_tensor_reduce(out=junk, in0=src, in1=src, scale=1.0, scalar=0.0,
                                            op0=ALU.mult, op1=ALU.add, accum_out=acc)

        step(dve.memset(stats, 1.0))
        step(dve.memset(tab[NBUCKET:NBUCKET + 1, :], NEG))
        dve.wait_ge(x_in, 48)
        for t in range(3):
            ins = squares(h[0:ROWS[t], t, :], n_tok[0:ROWS[t], t, :], stats[0:ROWS[t], t:t + 1])
        step(ins)
        inv_rms(stats[:, 0:3], stats[:, 0:3], stats[:, 3:6], stats[:, 6:9], D)
        for t in range(3):
            ins = dve.tensor_scalar(h[0:ROWS[t], t, :], h[0:ROWS[t], t, :], stats[0:ROWS[t], 3 + t:4 + t], None, ALU.mult)
        ins.then_inc(hn_ready, 1)
        dve.wait_ge(small_in, 16 * 7)
        even_transposes(KC, lambda e, c: e.tensor_scalar(xT[:, c, 0:TOK], bank[6][:, 0:TOK], gT[:, 0, c:c + 1], None, ALU.mult))
        dve.wait_ge(bias_mm, 1)
        dve.tensor_copy(bias_row[0:NH, :], bank[0][0:NH, 0:NBIAS]).then_inc(bias_sb, 1)

        dve.wait_ge(mm_ev, 2 + 6)
        for t in range(3):
            r = ROWS[t]
            ins = dve.tensor_tensor(cu[0:r, t, :], cu[0:r, t, :], sh1[0:r, t, :], ALU.mult)
        step(ins)
        dve.memset(sh2[0:2, 0, :], 0.0)
        step(dve.memset(sh1[0:1, 0, :], 0.0))
        dve.sem_inc(u_ready, 1)
        dve.wait_ge(shift_a, 8 * 16)
        dve.wait_ge(shift_b, 3 * 16)
        dve.wait_ge(cw_in, 32)
        for op in range(7):
            for t in range(3):
                r = ROWS[t]
                a, b, c, g = sh1[0:r, t, :], sh2[0:r, t, :], cu[0:r, t, :], bg[0:r, t, :]
                out, x, y, alu = ((a, a, cw[0:r, 1, :], ALU.mult), (b, b, cw[0:r, 0, :], ALU.mult), (a, a, b, ALU.add),
                                  (b, c, cw[0:r, 2, :], ALU.mult), (a, a, b, ALU.add), (a, a, cw[0:r, 3, :], ALU.add),
                                  (g, g, a, ALU.mult))[op]
                ins = dve.tensor_tensor(out, x, y, alu)
            step(ins)
        for t in range(3):
            r = ROWS[t]
            ins = squares(bg[0:r, t, :], sh1[0:r, t, :], stats[0:r, 123 + t:124 + t])
        step(ins)

        dve.wait_ge(mm_ev, 2 + 12)
        HEADS = ((0, 8, 0, 0), (1536, 2, 8, 2), (2048, 2, 10, 3))
        for t in range(3):
            r = ROWS[t]
            for c0, nh, s0, _ in HEADS:
                v = z[0:r, t, c0:c0 + nh * HD]
                step(dve.tensor_tensor(sh2[0:r, t, 0:nh * HD], v, v, ALU.mult))
                step(dve.tensor_reduce(stats[0:r, 36 + 12 * t + s0:36 + 12 * t + s0 + nh],
                                       sh2[0:r, t, 0:nh * HD].rearrange("p (n d) -> p n d", d=HD), AX.X, ALU.add))
        inv_rms(stats[:, 36:72], stats[:, 36:72], stats[:, 72:108], stats[:, 160:196], HD)
        qs = stats[:, 72:108].rearrange("p (t n) -> p t n", t=3)[:, :, 0:NH]
        step(dve.tensor_scalar(qs, qs, HD ** -0.5, None, ALU.mult))
        for t in range(3):
            r = ROWS[t]
            for c0, nh, s0, gi in HEADS:
                for n in range(nh):
                    v = z[0:r, t, c0 + n * HD:c0 + n * HD + HD]
                    k = 72 + 12 * t + s0 + n
                    ins = dve.scalar_tensor_tensor(out=v, in0=v, scalar=stats[0:r, k:k + 1], in1=qg[0:r, gi, :],
                                                   op0=ALU.mult, op1=ALU.mult)
        step(ins)
        dve.sem_inc(qkv_ready, 1)

        def heads_out(e, c):
            ins = e.tensor_copy(qkT[:, c, :], bank[6][:, 0:TOK])
            if c < NH:
                ins = e.tensor_copy(qsT[:, :, c, :], bank[6][:, 256:TOK].rearrange("p (b t) -> p b t", b=NB))
            return ins
        even_transposes(16, heads_out)

        step(dve.memset(raw[:, SEQS, :], 0.0))
        for kind in range(2):
            if kind:
                dve.wait_ge(cmp_mm, 2)
            even_transposes(NB, lambda e, c: e.tensor_copy(
                raw[:, 2 + 2 * c:4 + 2 * c, :].rearrange("p g (a x) -> p a g x", a=2),
                bank[6][:, :].rearrange("p (a g x) -> p a g x", a=2, g=2)))
            dve.wait_ge(raw_ready, 2 * kind + 1)
            dve.wait_ge(t_mm, tcount[0] + 1)
            dve.tensor_copy(raw[:, SEQS, 0:BLK], bank[6][:, 0:BLK]).then_inc(t_ev[0], 1)
            tcount[0] += 1
            dve.sem_inc(raw_ready, 1)
            if kind == 0:
                dve.wait_ge(kc_mm, 1)
                for i in range(3):
                    ins = dve.tensor_copy(kct[0:90, i, :], bank[2][0:90, i * HD:i * HD + HD])
                step(ins)
                for i in range(3):
                    ins = squares(kct[0:90, i, :], scr[0:90, 0].rearrange("p a b -> p (a b)")[:, 0:HD], stats[0:90, 108 + i:109 + i])
                    step(ins)
                inv_rms(stats[:, 108:111], stats[:, 108:111], stats[:, 111:114], stats[:, 114:117], HD)
                for i in range(3):
                    ins = dve.scalar_tensor_tensor(out=kct[0:90, i, :], in0=kct[0:90, i, :], scalar=stats[0:90, 111 + i:112 + i],
                                                   in1=qg[0:90, 1, :], op0=ALU.mult, op1=ALU.mult)
                ins.then_inc(kc_ready, 1)
                dve.wait_ge(kcT_mm, 1)
                dve.tensor_copy(kcT, bank[3][:, 0:SEQS * NWIN]).then_inc(cmp_done, 1)
            else:
                for q in range(5):
                    dve.wait_ge(kc_mm, 2 + q)
                    n = min(4, SEQS - 4 * q)
                    dve.tensor_copy(vc[0:NWIN, 4 * q:4 * q + n, :],
                                    bank[(2, 3, 4, 5, 0)[q]][0:NWIN, 0:n * HD].rearrange("p (a b) -> p a b", a=n))\
                       .then_inc(cmp_done, 1)
        dve.wait_ge(gs_mm, 1)
        step(dve.tensor_tensor(g24, bank[1][:, 0:96].rearrange("p (s c h) -> p s c h", s=4, c=3),
                               rep(cst[:, C_HM:], [0, 4], [NH, 3], [1, NH]), ALU.mult))
        dve.sem_inc(cmp_done, 1)
        step(dve.tensor_reduce(gs, g24, AX.X, ALU.add))

        def bias_max(u, par, parts):
            dve.wait_ge(s_mm, u + 1)
            for br, out, src, bias in parts:
                ins = dve.tensor_tensor_reduce(out=out, in0=src, in1=bias, scale=1.0, scalar=-3.0e38,
                                               op0=ALU.add, op1=ALU.max, accum_out=mx[:, par, br:br + 1])
            step(ins)
            step(dve.tensor_scalar(nm[:, par, :], mx[:, par, :], -1.0, None, ALU.mult))
            dve.sem_inc(biased, 1)

        def weigh(u, par, parts, gates_, mask):
            dve.wait_ge(exp_done, u + 1)
            step(dve.reciprocal(cf[:, par, :], sm[:, par, :]))
            step(dve.tensor_tensor(cf[:, par, :], cf[:, par, :], gates_, ALU.mult))
            if mask:
                step(dve.tensor_tensor(cf[:, par, 0:1], cf[:, par, 0:1], cst[:, C_VM:C_VM + 1], ALU.mult))
            for br, out, _, _ in parts:
                ins = dve.tensor_scalar(out, out, cf[:, par, br:br + 1], None, ALU.mult)
            step(ins)
            dve.sem_inc(p_scaled, 1)

        def prompt_parts(u):
            t, hh, par = u // NH, u % NH, u % 2
            nk = 128 * (t + 1)
            s, c = bank[par], bank[2 + par]
            ncmp = NWIN if t else 7
            c0 = BLK - 1 if t else BLK - 1 + 128
            return [(0, pb[:, par, 512:512 + ncmp], c[:, 0:ncmp], bias_p[:, hh, c0:256:STRIDE][:, 0:ncmp]),
                    (1, pb[:, par, 0:nk], s[:, 0:nk], bias_p[:, hh, 256 - nk:256]),
                    (2, pb[:, par, 256:256 + nk], s[:, 256:256 + nk], bias_p[:, hh, 256 - nk:256])]

        dve.wait_ge(bias_in, 17 * 16)
        for u in range(17):
            if u < 16:
                if u >= 2:
                    dve.wait_ge(pt_mm, u - 1)
                bias_max(u, u % 2, prompt_parts(u))
            if u:
                v = u - 1
                weigh(v, v % 2, prompt_parts(v), gate[:, v // NH, v % NH:GATES:NH], v < NH)
        for s in range(4):
            u = 16 + s
            if s:
                dve.wait_ge(s_mm, u)
            even_transposes(4, lambda e, c: e.tensor_copy(
                pastT[:, c // 2, c % 2].rearrange("p a b d -> p (a b d)"), bank[6][:, :]))
            dve.wait_ge(pt_mm, u)
            parts = [(0, pb[:, 0, 528:528 + NWIN], bank[0][:, 264:264 + NWIN], bias_s[:, BLK - 1:256:STRIDE]),
                     (1, pb[:, 0, 0:264], bank[0][:, 0:264], bias_s),
                     (2, pb[:, 0, 264:528], bank[1][:, 0:264], bias_s)]
            bias_max(u, 0, parts)
            weigh(u, 0, parts, gs[:, s, :], False)

        dve.wait_ge(attT_ev, 2)
        dve.wait_ge(o_ev, 20)
        for t in range(3):
            r = ROWS[t]
            ins = squares(att[0:r, t, :], cu[0:r, t, :], stats[0:r, 120 + t:121 + t])
        step(ins)
        inv_rms(stats[:, 120:126], stats[:, 120:126], stats[:, 126:132], stats[:, 160:166], ATT)
        for t in range(3):
            r = ROWS[t]
            for src, k in ((att, 126 + t), (bg, 129 + t)):
                ins = dve.tensor_scalar(src[0:r, t, :], src[0:r, t, :], stats[0:r, k:k + 1], None, ALU.mult)
        ins.then_inc(hn_ready, 1)
        even_transposes(KC, lambda e, c: e.tensor_scalar(xT[:, c, 0:TOK], bank[6][:, 0:TOK], gT[:, 3, c:c + 1], None, ALU.mult))

        dve.wait_ge(x_in, 96)
        for blk in range(4):
            dve.wait_ge(mm_done, N_OUT + blk + 1)
            for t in range(3):
                v = h[0:ROWS[t], t, 512 * blk:512 * blk + 512]
                ins = dve.tensor_tensor(v, bank[3 * (blk % 2) + t][0:ROWS[t], :], v, ALU.add)
            ins.then_inc(mm_ev, 1)
        step(dve.memset(stats[:, 136:139], 0.0))
        dve.wait_ge(mm_ev, 2 + 16)
        dve.sem_inc(h_ready, 1)
        dve.wait_ge(dup_in, 32)
        for t in range(3):
            ins = squares(h[:, t, :], n_tok[:, t, :], stats[:, 136 + t:137 + t])
        step(ins)
        inv_rms(stats[:, 136:139], stats[:, 136:139], stats[:, 139:142], stats[:, 160:163], D)
        for t in range(3):
            ins = dve.scalar_tensor_tensor(out=n_tok[:, t, :], in0=h[:, t, :], scalar=stats[:, 139 + t:140 + t],
                                           in1=g2, op0=ALU.mult, op1=ALU.mult)
        ins.then_inc(hn_ready, 1)
        even_transposes(KC, lambda e, c: e.tensor_copy(xT[:, c, :], bank[6][:, 0:384]))

        iota = cst[:, C_IOTA:C_IOTA + PK * PK]
        for t in range(3):
            dve.wait_ge(sc_ev, 4 * t + 4)
            if t == 0:
                dve.wait_ge(sc_ev, 12)
            cut = scr.rearrange("p a b c -> p (a b c)")

            def top16(n, width, src, val, ix):
                for half in range(2):
                    o = slice(8 * half, 8 * half + 8)
                    for r in range(n):
                        ins = dve.max(val[:, r, o], (cut if half else src)[:, r * width:r * width + width])
                    step(ins)
                    for r in range(n):
                        ins = dve.max_index(ix[:, r, o].bitcast(u32), val[:, r, o],
                                            (cut if half else src)[:, r * width:r * width + width])
                    step(ins)
                    if half == 0:
                        for r in range(n):
                            ins = dve.match_replace(cut[:, r * width:r * width + width], val[:, r, o],
                                                    src[:, r * width:r * width + width], -3.0e38)
                        step(ins)

            top16(16, NKEY, score[:, t, :], sv, si)
            step(dve.tensor_copy(si, si.bitcast(u32)))
            for r in range(PH):
                ins = dve.tensor_tensor(cand[:, r], rep(sv[:, 2 * r, :], [1, PK], [0, PK]),
                                        rep(sv[:, 2 * r + 1, :], [0, PK], [1, PK]), ALU.add)
            step(ins)
            top16(PH, PK * PK, cand.rearrange("p a b c -> p (a b c)"), fv, fi)
            fiu = fi.bitcast(u32)
            dve.tensor_scalar(fh.bitcast(u32), fiu, 4, None, ALU.logical_shift_right)
            step(dve.tensor_scalar(fl.bitcast(u32), fiu, PK - 1, None, ALU.bitwise_and))
            dve.tensor_copy(fh, fh.bitcast(u32))
            step(dve.tensor_copy(fl, fl.bitcast(u32)))
            for side, (pos, e) in enumerate(((fh, e0), (fl, e1))):
                step(dve.tensor_tensor(cand, rep(pos, [PK, PH], [1, PK], [0, PK]),
                                       rep(iota, [0, PH], [PK, PK], [1, PK]), ALU.is_equal))
                step(dve.tensor_tensor(cand, cand, rep(si[:, side, :], [2 * PK, PH], [0, PK], [1, PK]), ALU.mult))
                step(dve.tensor_reduce(e, cand, AX.X, ALU.add))
            step(dve.scalar_tensor_tensor(out=e0, in0=e0, scalar=float(NKEY), in1=e1, op0=ALU.mult, op1=ALU.add))
            step(dve.tensor_copy(idx[:, t, :], e0.rearrange("p a b -> p (a b)")))
            step(dve.tensor_copy(e1[:, :, 0], fv[:, :, 0]))
            step(dve.tensor_tensor(fv, fv, rep(e1, [PK, PH], [0, PK]), ALU.subtract))
            dve.sem_inc(e_in, 1)
            dve.wait_ge(e_out, 4 + t + 1)
            step(dve.tensor_reduce(e1[:, :, 0], fv, AX.X, ALU.add))
            step(dve.reciprocal(e1[:, :, 1], e1[:, :, 0]))
            step(dve.tensor_tensor(wgt[:, t, :].rearrange("p (a b) -> p a b", a=PH), fv,
                                   rep(e1[:, :, 1], [PK, PH], [0, PK]), ALU.mult))
            if t == 2:
                step(dve.tensor_copy(wgt[64:128, 2, 0:64], wgt[64:128, 2, 64:128]))
                step(dve.tensor_copy(idx[64:128, 2, 0:64], idx[64:128, 2, 64:128]))
            dve.sem_inc(idx_ready, 1)

        dve.sem_inc(u_used, 4)
        dve.sem_inc(v_used, 4)
        loop_steps = [0]

        def group(k, par, t, c0):
            dve.tensor_copy(idx4[:, par, :], idx[:, t, c0]).then_inc(idx_set, 1)
            for j in range(4):
                dve.wait_ge(u_in[j], (k + 1) * 16)
                ins = dve.tensor_tensor_reduce(out=u_row[j], in0=u_row[j], in1=n_tok[:, t, :], scale=1.0, scalar=0.0,
                                               op0=ALU.mult, op1=ALU.add, accum_out=a4[:, par, j:j + 1])
                ins.then_inc(u_used, 1)
            dve.wait_ge(u_used, k * 4 + 8)
            dve.sem_inc(dots, 1)
            dve.wait_ge(gelu_done, k + 1)
            dve.tensor_tensor(w4[:, par, :], w4[:, par, :], wgt[:, t, c0], ALU.mult).then_inc(loop_step, 1)
            dve.wait_ge(loop_step, k + 1)
            for j in range(4):
                src = ident if t < 2 else cst[:, C_PAIR:C_PAIR + 64]
                ins = dve.tensor_scalar(diag[:, par, j, 0:(128 if t < 2 else 64)], src, w4[:, par, j:j + 1], None, ALU.mult)
            ins.then_inc(diag_ready, 1)

        def add_peer(t):
            dve.wait_ge(peer_mm, t + 1)
            for q in range(4):
                v = h[0:ROWS[t], t, 512 * q:512 * q + 512]
                ins = dve.tensor_tensor(v, bank[4 * (t % 2) + q][0:ROWS[t], :], v, ALU.add)
            return ins

        base = 0
        for t in range(3):
            group(base, 0, t, slice(0, 4))
            if t:
                step(add_peer(t - 1))
            with dve.Fori(0, (GROUPS[t] - 2) // 2) as i:
                for jj in range(2):
                    k = i * 2 + (base + 1 + jj)
                    dve.wait_ge(v_used, k * 4 - 0)
                    group(k, (1 + jj) % 2, t, bass.ds(i * 8 + 4 * (1 + jj), 4))
            group(base + GROUPS[t] - 1, 1, t, slice(4 * GROUPS[t] - 4, 4 * GROUPS[t]))
            base += GROUPS[t]
        step(add_peer(2))
        dve.sem_inc(h_ready, 1)

        for t in range(3):
            ins = squares(h[0:ROWS[t], t, :], n_tok[0:ROWS[t], t, :], stats[0:ROWS[t], 144 + t:145 + t])
        step(ins)
        inv_rms(stats[:, 144:147], stats[:, 144:147], stats[:, 147:150], stats[:, 160:163], D)
        for t in range(3):
            ins = dve.tensor_scalar(n_tok[0:ROWS[t], t, :], h[0:ROWS[t], t, :], stats[0:ROWS[t], 147 + t:148 + t], None, ALU.mult)
        ins.then_inc(hn_ready, 1)
        even_transposes(KC, lambda e, c: e.tensor_scalar(xT[:, c, 0:TOK], bank[6][:, 0:TOK], gT[:, 2, c:c + 1], None, ALU.mult))
        for c in range(2):
            dve.wait_ge(pleT_mm, c + 1)
            dve.tensor_copy(pleT[:, c, :], bank[c][:, 0:TOK]).then_inc(pleT_ev, 1)
        for blk in range(4):
            dve.wait_ge(sig_ready, blk + 1)
            for t in range(3):
                r = ROWS[t]
                s = sig[0:r, blk % 2, t, :]
                ins = dve.tensor_tensor(s, s, bank[3 + t][0:r, :], ALU.mult)
            step(ins)
            dve.sem_inc(ple_mm, 1)
            for t in range(3):
                r = ROWS[t]
                v = h[0:r, t, 512 * blk:512 * blk + 512]
                ins = dve.tensor_tensor(v, v, sig[0:r, blk % 2, t, :], ALU.add)
            step(ins)
            dve.sem_inc(y_ready, 1)

    @block.tensor
    def _(pe):
        pe.sem_inc(w_used, 4)
        runs = [0]
        evs = [0, 0]

        def transposes(n, src_of):
            for c in range(n):
                par = c % 2
                if evs[par] >= 1:
                    pe.wait_ge(t_ev[par], evs[par])
                for dst, src, rows in src_of(c):
                    ins = pe.transpose(bank[6 + par][0:src.shape[1], dst:dst + rows], src, ident[0:rows, 0:rows])
                ins.then_inc(t_mm, 1)
                evs[par] += 1

        def tok_tiles(src, rows=ROWS):
            return lambda c: [(128 * t, src(t, c)[0:rows[t], :], rows[t]) for t in range(3)]

        pe.wait_ge(cst_in, 16)
        pe.wait_ge(small_in, 16 * 7)
        pe.wait_ge(dve_step, 2)
        pe.matmul(bank[0][0:NH, 0:NBIAS], tab[0:NBUCKET + 1, :], cst[0:NBUCKET + 1, C_OH:C_OH + NBIAS],
                  start=True, stop=True).then_inc(bias_mm, 1)
        pe.wait_ge(hn_ready, 1)
        transposes(KC, tok_tiles(lambda t, c: h[:, t, 128 * c:128 * c + 128]))
        pe.wait_ge(t_ev[0], 8)
        pe.wait_ge(t_ev[1], 8)
        pe.wait_ge(bias_sb, 1)

        def product(n, done, f, par, width=512):
            pe.wait_ge(mm_ev, done)
            for half in range(2):
                slot = (2 * par + half) % 4
                pe.wait_ge(w_in[slot], f)
                for t in range(3):
                    for k in range(8):
                        ins = pe.matmul(bank[3 * par + t][0:ROWS[t], 0:width], xT[:, 8 * half + k, 128 * t:128 * t + ROWS[t]],
                                        ring[slot][:, k, 0:width], start=(half == 0 and k == 0), stop=(half == 1 and k == 7))
                ins.then_inc(w_used, 1)

        def blocks(first, count):
            with pe.Fori(0, count // 2) as i:
                for par in range(2):
                    product(None, i * 2 + (first + par + 1), i * 16 + (8 * first + 16), par)
                    pe.wait_ge(w_used, i * 4 + (4 + 2 * (first + par + 1)))
                    pe.sem_inc(mm_done, 1)

        blocks(0, 6)
        blocks(6, 4)
        for n in (10, 11):
            product(None, n + 1, 16 * (n // 2) + 16, n % 2, 512 if n == 10 else GATES)
            pe.wait_ge(w_used, 4 + 2 * (n + 1))
            pe.sem_inc(mm_done, 1)

        pe.wait_ge(qkv_ready, 1)
        transposes(16, tok_tiles(lambda t, c: z[:, t, TBLOCKS[c]:TBLOCKS[c] + 128]))
        pe.wait_ge(t_ev[0], evs[0])
        pe.wait_ge(t_ev[1], evs[1])

        for kind in range(2):
            def page_blocks(b):
                return [(128 * (2 * a + g), page_in[:, b % 2, a, g * HD:g * HD + HD], 128) for a in range(2) for g in range(2)]
            for b in range(NB):
                par = b % 2
                pe.wait_ge(page_s[par], 32 * (NB // 2 * kind + b // 2 + 1))
                pe.wait_ge(t_ev[par], evs[par])
                for dst, src, rows in page_blocks(b):
                    ins = pe.transpose(bank[6 + par][:, dst:dst + 128], src, ident)
                ins.then_inc(t_mm, 1)
                evs[par] += 1
                pe.wait_ge(t_mm, sum(evs))
                pe.sem_inc(page_used, 1)
            pe.wait_ge(pe_in_s, 16 * (kind + 1))
            transposes(1, lambda c: [(0, pe_in[0:BLK, :], BLK)])
            pe.wait_ge(t_ev[0], evs[0])
            pe.wait_ge(t_ev[1], evs[1])
            pe.wait_ge(raw_ready, 2 * kind + 2)
            pe.wait_ge(w1_in, 16 * (kind + 1))
            for hb in range(2):
                if kind:
                    pe.wait_ge(hid_ready, hb + 1)
                for m in range(BLK):
                    view = raw[:, :, m:m + STRIDE * (NWIN - 1) + 1:STRIDE]
                    ins = pe.matmul(bank[hb][:, 0:(SEQS + 1) * NWIN], w1[:, m, hb * 128:hb * 128 + 128], view,
                                    start=(m == 0), stop=(m == BLK - 1))
                ins.then_inc(cmp_mm, 1)
            pe.wait_ge(hid_ready, 2 * kind + 2)
            pe.wait_ge(w2_in, 16 * (kind + 1))
            if kind == 0:
                for i in range(3):
                    for hb in range(2):
                        ins = pe.matmul(bank[2][0:90, i * HD:i * HD + HD], hid[:, hb, 90 * i:90 * i + 90], w2[:, hb, :],
                                        start=(hb == 0), stop=(hb == 1))
                ins.then_inc(kc_mm, 1)
                pe.wait_ge(kc_ready, 1)
                for i in range(3):
                    ins = pe.transpose(bank[3][:, 90 * i:90 * i + 90], kct[0:90, i, :], ident[0:90, 0:90])
                ins.then_inc(kcT_mm, 1)
                pe.wait_ge(cmp_done, 1)
            else:
                for sg in range(SEQS):
                    q = sg // 4
                    for hb in range(2):
                        ins = pe.matmul(bank[(2, 3, 4, 5, 0)[q]][0:NWIN, (sg % 4) * HD:(sg % 4) * HD + HD],
                                        hid[:, hb, NWIN * sg:NWIN * sg + NWIN], w2[:, hb, :], start=(hb == 0), stop=(hb == 1))
                    if sg % 4 == 3 or sg == SEQS - 1:
                        ins.then_inc(kc_mm, 1)
        for s in range(4):
            ins = pe.matmul(bank[1][:, GATES * s:GATES * s + GATES], cst[0:64, C_SELG + 128 * s:C_SELG + 128 * s + 128],
                            gate[0:64, 2, :], start=True, stop=True)
        ins.then_inc(gs_mm, 1)
        pe.wait_ge(cmp_done, 7)

        def scores(u):
            t, hh, par = u // NH, u % NH, u % 2
            g = hh // HPG
            nk = 128 * (t + 1)
            if u >= 2:
                pe.wait_ge(biased, u - 1)
            q = qkT[:, hh, 128 * t:128 * t + 128]
            pe.matmul(bank[par][:, 0:nk], q, qkT[:, 12 + g, 0:nk], start=True, stop=True)
            pe.matmul(bank[par][:, 256:256 + nk], q, qkT[:, 14 + g, 0:nk], start=True, stop=True)
            ncmp = NWIN if t else 7
            pe.matmul(bank[2 + par][:, 0:ncmp], q, kcT[:, g * NWIN:g * NWIN + ncmp], start=True, stop=True).then_inc(s_mm, 1)

        def values(u):
            t, hh, par = u // NH, u % NH, u % 2
            g = hh // HPG
            ncmp = NWIN if t else 7
            pe.wait_ge(p_scaled, u + 1)
            if u >= 2:
                pe.wait_ge(pt_ev, u - 1)
            for w in range(2):
                for k in range(t + 1):
                    pe.transpose(bank[4 + par][:, 256 * w + 128 * k:256 * w + 128 * k + 128],
                                 pb[:, par, 256 * w + 128 * k:256 * w + 128 * k + 128], ident)
            pe.transpose(bank[2 + par][0:ncmp, 128:256], pb[:, par, 512:512 + ncmp], ident).then_inc(pt_mm, 1)
            pe.wait_ge(pt_ev, u + 1)
            if u >= 2:
                pe.wait_ge(o_ev, u - 1)
            first = True
            for w in range(2):
                for k in range(t + 1):
                    pe.matmul(bank[6 + par][:, 0:HD], pT[:, par, 256 * w + 128 * k:256 * w + 128 * k + 128],
                              z[:, k, (1792, 2304)[w] + g * HD:(1792, 2304)[w] + g * HD + HD], start=first, stop=False)
                    first = False
            pe.matmul(bank[6 + par][:, 0:HD], pT[0:ncmp, par, 512:640], vc[0:ncmp, g, :], start=False, stop=True)\
              .then_inc(o_mm, 1)

        for u in range(17):
            if u < 16:
                scores(u)
            if u:
                values(u - 1)
        pe.wait_ge(o_ev, 16)

        for s in range(4):
            u = 16 + s
            pe.wait_ge(past_in[s % 2], 96 * (s // 2 + 1))

            transposes(4, lambda c: [(128 * (2 * a + g), past_rows(s, c // 2, c % 2, a)[:, g * HD:g * HD + HD], 128)
                                     for a in range(2) for g in range(2)])
            pe.wait_ge(t_ev[0], evs[0])
            pe.wait_ge(t_ev[1], evs[1])
            pe.wait_ge(biased, u)
            for bb in range(2):
                b = 2 * s + bb
                for g in range(NG):
                    p0 = 64 * bb + 32 * g
                    q = qsT[:, b, HPG * g:HPG * g + HPG, :].rearrange("p h t -> p (h t)")
                    for br in range(2):
                        for a in range(2):
                            pe.matmul(bank[br][p0:p0 + 32, 128 * a:128 * a + 128], q, pastT[:, bb, br, a, g, :],
                                      start=True, stop=True)
                        pe.matmul(bank[br][p0:p0 + 32, 256:264], q, qkT[:, 12 + 2 * br + g, 256 + b * NT:256 + b * NT + NT],
                                  start=True, stop=True)
                    sg = 2 * (1 + b) + g
                    ins = pe.matmul(bank[0][p0:p0 + 32, 264:264 + NWIN], q, kcT[:, sg * NWIN:sg * NWIN + NWIN],
                                    start=True, stop=True)
            ins.then_inc(s_mm, 1)
            pe.wait_ge(p_scaled, u + 1)
            for w in range(2):
                for k in range(2):
                    pe.transpose(bank[4][:, 256 * w + 128 * k:256 * w + 128 * k + 128],
                                 pb[:, 0, 264 * w + 128 * k:264 * w + 128 * k + 128], ident)
                pe.transpose(bank[5][0:NT, 128 * w:128 * w + 128], pb[:, 0, 264 * w + 256:264 * w + 264], ident)
            pe.transpose(bank[5][0:NWIN, 256:384], pb[:, 0, 528:528 + NWIN], ident).then_inc(pt_mm, 1)
            pe.wait_ge(pt_ev, u + 1)
            if s == 0:
                pe.wait_ge(vn_in, 16 * 2 * NB)
            for bb in range(2):
                b = 2 * s + bb
                for g in range(NG):
                    r = slice(64 * bb + 32 * g, 64 * bb + 32 * g + 32)
                    o = bank[5][:, 384 + r.start:384 + r.stop]
                    for w in range(2):
                        for k in range(2):
                            pe.matmul(o, past_rows(s, bb, w, k)[:, 256 + g * HD:256 + g * HD + HD],
                                      pT[:, 0, 256 * w + 128 * k + r.start:256 * w + 128 * k + r.stop],
                                      start=(w == 0 and k == 0), stop=False)
                        pe.matmul(o, vn[0:NT, b, w, g * HD:g * HD + HD],
                                  pT[0:NT, 0, 512 + 128 * w + r.start:512 + 128 * w + r.stop], start=False, stop=False)
                    ins = pe.matmul(o, vc[0:NWIN, 2 * (1 + b) + g, :], pT[0:NWIN, 0, 768 + r.start:768 + r.stop],
                                    start=False, stop=True)
            ins.then_inc(o_mm, 1)
            pe.wait_ge(o_ev, u + 1)
        for i in range(2):
            for j in range(4):
                ins = pe.transpose(bank[i][0:64, 128 * j:128 * j + 128], attT[:, 4 * i + j, :], ident)
            ins.then_inc(attT_mm, 1)

        pe.wait_ge(hn_ready, 2)
        pe.sem_inc(merged, 1)
        transposes(KC, tok_tiles(lambda t, c: (att if c < 8 else bg)[:, t, 128 * (c % 8):128 * (c % 8) + 128]))
        pe.wait_ge(t_ev[0], evs[0])
        pe.wait_ge(t_ev[1], evs[1])
        blocks(N_OUT, 4)

        pe.wait_ge(hn_ready, 3)
        transposes(KC, tok_tiles(lambda t, c: n_tok[:, t, 128 * c:128 * c + 128], (128, 128, 128)))
        pe.wait_ge(t_ev[0], evs[0])
        pe.wait_ge(t_ev[1], evs[1])
        for blk in range(4):
            if blk >= 2:
                pe.wait_ge(qT_done, blk - 1)
            n = N_WQ + blk
            for half in range(2):
                slot = (2 * blk + half) % 4
                pe.wait_ge(w_in[slot], 16 * (n // 2) + 16)
                for sub in range(4):
                    for k in range(8):
                        ins = pe.matmul(bank[4 * (blk % 2) + sub][:, 0:384], ring[slot][:, k, 128 * sub:128 * sub + 128],
                                        xT[:, 8 * half + k, :], start=(half == 0 and k == 0), stop=(half == 1 and k == 7))
                ins.then_inc(w_used, 1)
            pe.wait_ge(w_used, 4 + 2 * (n + 1))
            pe.sem_inc(mm_done, 1)
        pe.wait_ge(qT_done, 4)
        pe.wait_ge(keys_s, 16)
        for a in range(2):
            ins = pe.transpose(bank[0][:, 128 * a:128 * a + 128], keys_in[:, a, :], ident)
        ins.then_inc(keys_mm, 1)
        pe.wait_ge(keys_ev, 1)
        for t in range(3):
            for q in range(4):
                if t == 2:
                    pe.wait_ge(sc_ev, q + 1)
                for j in range(4):
                    c = 4 * q + j
                    ins = pe.matmul(bank[4 * (t % 2) + q][:, 128 * j:128 * j + 128], qT[:, c, 128 * t:128 * t + 128],
                                    keysT[:, c % 2, :], start=True, stop=True)
                ins.then_inc(sc_mm, 1)
        pe.wait_ge(sc_ev, 12)

        def weighted_rows(k, par, t, first, last):
            m = 128 if t < 2 else 64
            pe.wait_ge(diag_ready, k + 1)
            for j in range(4):
                pe.wait_ge(v_in[j], (k + 1) * 16)
                for q in range(4):
                    ins = pe.matmul(bank[4 * (t % 2) + q][0:m, :], diag[:, par, j, 0:m], v_row[j][:, 512 * q:512 * q + 512],
                                    start=(first and j == 0), stop=(last and j == 3))
                ins.then_inc(v_used, 1)

        base = 0
        for t in range(3):
            weighted_rows(base, 0, t, True, False)
            with pe.Fori(0, (GROUPS[t] - 2) // 2) as i:
                for jj in range(2):
                    weighted_rows(i * 2 + (base + 1 + jj), (1 + jj) % 2, t, False, False)
            weighted_rows(base + GROUPS[t] - 1, 1, t, False, True)
            base += GROUPS[t]
            pe.wait_ge(v_used, 4 * base + 4)
            pe.sem_inc(peer_mm, 1)

        pe.wait_ge(hn_ready, 4)
        transposes(KC, tok_tiles(lambda t, c: n_tok[:, t, 128 * c:128 * c + 128]))
        pe.wait_ge(ple_in, 64)
        for c in range(2):
            for t in range(3):
                ins = pe.transpose(bank[c][:, 128 * t:128 * t + ROWS[t]], p_in[0:ROWS[t], t, 128 * c:128 * c + 128],
                                   ident[0:ROWS[t], 0:ROWS[t]])
            ins.then_inc(pleT_mm, 1)
        pe.wait_ge(pleT_ev, 2)
        pe.wait_ge(t_ev[0], evs[0])
        pe.wait_ge(t_ev[1], evs[1])
        for blk in range(4):
            n = N_GATE + blk
            if blk:
                pe.wait_ge(ple_mm, blk)
            for t in range(3):
                for c in range(2):
                    pe.matmul(bank[3 + t][0:ROWS[t], :], pleT[:, c, 128 * t:128 * t + ROWS[t]],
                              ple_w[:, c, 512 * blk:512 * blk + 512], start=(c == 0), stop=(c == 1))
            for half in range(2):
                slot = (2 * blk + half) % 4
                pe.wait_ge(w_in[slot], 16 * (n // 2) + 16)
                for t in range(3):
                    for k in range(8):
                        ins = pe.matmul(bank[t][0:ROWS[t], :], xT[:, 8 * half + k, 128 * t:128 * t + ROWS[t]],
                                        ring[slot][:, k, :], start=(half == 0 and k == 0), stop=(half == 1 and k == 7))
                ins.then_inc(w_used, 1)
            pe.wait_ge(w_used, 4 + 2 * (n + 1))
            pe.sem_inc(mm_done, 1)

    ctx.close()


_INS = ["x_prompt", "x_sample", "p_prompt", "p_sample", "cache_kv", "state_win", "state_conv", "page_table", "rel_bias",
        "norm1", "w_in", "qk_gain", "cmp_pe", "cmp_w1", "cmp_w2", "conv_w", "conv_b", "out_gain", "w_out", "norm2",
        "peer_wq", "peer_keys", "peer_u", "peer_v", "norm3", "ple_gate", "ple_proj"]
_OUTS = [(1, NP, D), (NB, NT, D), (1, 1, NP, 4, NG, HD), (1, 1, NP, 2, NG, HD), (1, 1, 2, CONV),
         (1, NB, NT, 4, NG, HD), (1, NB, PAST, 2, NG, HD), (1, NB, 2, CONV)]


def kernel(**inputs):
    import concourse.bacc as bacc
    from concourse.bass_utils import run_bass_kernel_spmd

    nc = bacc.Bacc("TRN2", target_bir_lowering=False, num_devices=1)
    arrays, ins = {}, {}
    for name in _INS:
        a = np.ascontiguousarray(inputs[name])
        arrays[f"in_{name}"] = a
        ins[name] = nc.dram_tensor(f"in_{name}", a.shape, mybir.dt.from_np(a.dtype), kind="ExternalInput").ap()
    arrays["in_cst"] = shape_constants()
    ins["cst"] = nc.dram_tensor("in_cst", (128, NCST), mybir.dt.float32, kind="ExternalInput").ap()
    outs = [nc.dram_tensor(f"out_{i}", s, mybir.dt.float32, kind="ExternalOutput").ap() for i, s in enumerate(_OUTS)]
    build(nc, ins, outs)
    r = run_bass_kernel_spmd(nc, [arrays], core_ids=[0])
    return tuple(r.results[0][f"out_{i}"] for i in range(len(_OUTS)))
```

```python
import math
from contextlib import ExitStack

import numpy as np
import concourse.bass as bass
from concourse import mybir

D = 2048
KC = D // 128
NP, NB, NT = 256, 8, 8
PAST, PAGE = 256, 128
HD, NH, NG = 128, 8, 2
HPG = NH // NG
ATT = NH * HD
CONV = D - ATT
KVC = 6 * NG * HD
QKV = ATT + KVC
GATES = 3 * NH
BLK, STRIDE, HID = 32, 16, 256
NWIN = PAST // STRIDE - 1
SEQS = (1 + NB) * NG
PH, PK, NKEY = 8, 16, 128
PLE = 256
EPS, NEG = 1e-6, -1e30
ROWS = (128, 128, NB * NT)
TOK = sum(ROWS)
NBUCKET, MAXDIST = 32, 128
DMAX = PAST + NT - 1
NBIAS = DMAX + 128

C_ID = 0
C_IOTA = C_ID + 128
C_PAIR = C_IOTA + PK * PK
C_SELG = C_PAIR + 64
C_HM = C_SELG + 4 * 128
C_VM = C_HM + GATES
C_OH = C_VM + 1
NCST = C_OH + NBIAS


def shape_constants():
    c = np.zeros((128, NCST), np.float32)
    p = np.arange(128)
    c[:, C_ID:C_ID + 128] = np.eye(128, dtype=np.float32)
    c[:, C_IOTA:C_IOTA + PK * PK] = np.arange(PK * PK) % PK
    c[p, C_PAIR + p % 64] = 1.0
    for s in range(4):
        tok = (2 * s + p // 64) * NT + p % NT
        c[tok, C_SELG + s * 128 + p] = 1.0
    for br in range(3):
        c[p, C_HM + br * NH + (p % 64) // NT] = 1.0
    c[BLK - 1:, C_VM] = 1.0
    dist = DMAX - np.arange(NBIAS)
    n = np.maximum(dist, 0)
    exact = NBUCKET // 2
    nf = np.maximum(n, 1).astype(np.float32)
    large = exact + (np.log(nf / np.float32(exact)) / np.float32(math.log(MAXDIST / exact))
                     * np.float32(NBUCKET - exact)).astype(np.int32)
    bucket = np.where(n < exact, n, np.minimum(large, NBUCKET - 1))
    bucket = np.where(dist >= 0, bucket, NBUCKET)
    c[bucket, C_OH + np.arange(NBIAS)] = 1.0
    return c


def build(nc, I, O):
    fp32, i32, u32 = mybir.dt.float32, mybir.dt.int32, mybir.dt.uint32
    ALU, ACT, AX = mybir.AluOpType, mybir.ActivationFunctionType, mybir.AxisListType
    ctx = ExitStack()
    PITCH = 53200
    arena = ctx.enter_context(nc.sbuf_tensor("arena", [128, PITCH], fp32))
    bank = [ctx.enter_context(nc.psum_tensor(f"bank{i}", [128, 512], fp32)) for i in range(8)]
    bias_dram = nc.dram_tensor("bias_rows", (NH, 128, NBIAS), fp32, kind="Internal").ap()

    def sem(name):
        return ctx.enter_context(nc.semaphore(name))

    def buf(off, *dims):
        n = math.prod(dims)
        assert off + n <= PITCH
        a = arena[:, off:off + n]
        if len(dims) == 1:
            return a
        names = "abcde"[:len(dims)]
        return a.rearrange(f"p ({' '.join(names)}) -> p {' '.join(names)}",
                           **{x: d for x, d in zip(names[1:], dims[1:])})

    def rep(ap, *dims):
        return bass.AP(ap.tensor, ap.offset, [list(ap.ap[0])] + [list(d) for d in dims])

    T0 = 0
    W0 = T0 + KC * 384
    Z0 = W0 + 4 * 8 * 512
    ZC0 = Z0 + 3 * 2560
    X0 = ZC0 + 9 * 1024
    K0 = X0 + 3 * 1024

    xT = buf(T0, KC, 384)
    ring = [buf(W0 + s * 4096, 8, 512) for s in range(4)]
    z = buf(Z0, 3, 2560)
    h = buf(Z0, 3, D)
    n_tok = buf(Z0 + 3 * D, 3, D)
    bg, cu, sh1 = (buf(ZC0 + i * 3072, 3, 1024) for i in range(3))
    sh2 = buf(X0, 3, 1024)
    att = buf(X0, 3, 1024)

    cst = buf(K0, NCST)
    ident = cst[:, C_ID:C_ID + 128]
    gT = buf(K0 + NCST, 4, KC)
    qg = buf(K0 + NCST + 64, 4, HD)
    gate = buf(K0 + NCST + 576, 3, GATES)
    bias_s = buf(K0 + NCST + 648, DMAX + 1)
    bias_p = buf(K0 + NCST + 912, NH, 256)
    g2 = buf(K0 + NCST + 912, D)
    cw = buf(K0 + NCST + 912 + 2048, 4, CONV)
    S0 = K0 + NCST + 912 + 2048 + 4096
    stats = buf(S0, 256)
    tab = buf(S0 + 256, NH)
    bias_row = buf(S0 + 264, NBIAS)
    g24 = buf(S0 + 264, 4, 3, NH)
    gs = buf(S0 + 368, 4, 3)
    pages = buf(S0 + 656, 2 * NB).bitcast(i32)
    w4 = buf(S0 + 672, 2, 4)
    a4 = buf(S0 + 680, 2, 4)
    idx4 = buf(S0 + 688, 2, 4).bitcast(i32)
    diag = buf(S0 + 700, 2, 4, 128)
    vn = buf(K0 + NCST + 912 + 2048, NB, 2, 256)
    qsT = buf(S0 + 1724, NB, NH, NT)

    qkT = buf(W0, 16, TOK)
    w1 = buf(W0 + 5120, BLK, HID)
    page_in = buf(W0 + 13312, 2, 2, 256)
    hid = buf(W0 + 13312 + 1024, 2, SEQS * NWIN)
    w2 = buf(W0 + 14880, 2, HD)
    kcT = buf(W0 + 15136, SEQS * NWIN)
    kct = buf(W0 + 15408, 3, HD)
    pe_in = buf(W0 + 15792, HD)
    pecol = buf(W0 + 15920, 2)
    raw = buf(T0, SEQS + 1, 256)
    vc = buf(T0 + 3840, SEQS, HD)

    def past_rows(s, bb, br, a):
        return buf(W0 + 5120 + (((s % 2) * 2 + bb) * 2 + br) * 1024 + a * 512, 512)

    pastT = buf(ZC0 + 3072, 2, 2, 2, 2, HD)
    pb = buf(T0, 2, 544)
    pT = buf(T0 + 1088, 2, 896)
    attT = buf(T0 + 2880, NH, NB * NT)
    mx, nm, sm, cf = (buf(S0 + 200 + 6 * i, 2, 3) for i in range(4))
    qT = buf(Z0 + 6 * D, KC, 384)
    keys_in = buf(K0 + NCST + 2960, 2, 128)
    keysT = buf(K0 + NCST + 2960 + 256, 2, 128)
    sv = buf(K0 + NCST + 2960 + 512, 16, PK)
    si = buf(K0 + NCST + 2960 + 768, 16, PK)
    fv = buf(K0 + NCST + 2960 + 1024, PH, PK)
    fi = buf(K0 + NCST + 2960 + 1152, PH, PK)
    fh = buf(K0 + NCST + 2960 + 1280, PH, PK)
    fl = buf(K0 + NCST + 2960 + 1408, PH, PK)
    e0 = buf(K0 + NCST + 2960 + 1536, PH, PK)
    e1 = buf(K0 + NCST + 2960 + 1664, PH, PK)
    wgt = buf(K0 + NCST + 2960 + 1792, 3, 128)
    idx = buf(K0 + NCST + 2960 + 2176, 3, 128).bitcast(i32)
    score = buf(T0, 3, D)
    cand = buf(Z0 + 6 * D, PH, PK, PK)
    scr = buf(Z0 + 7 * D, PH, PK, PK)
    u_row = [buf(W0 + j * D, D) for j in range(4)]
    v_row = [buf(W0 + (4 + j) * D, D) for j in range(4)]
    ple_w = buf(Z0 + 6 * D, 2, D)
    p_in = buf(K0 + NCST + 5520, 3, PLE)
    pleT = buf(K0 + NCST + 6288, 2, TOK)
    sig = buf(K0 + NCST + 912, 2, 512)
    hT = buf(T0, KC, 256)
    hT_s = buf(T0, KC, 64)
    gate_w = [n_tok[:, 0, :], n_tok[:, 1, :], buf(T0 + KC * 256, D)]
    gate_w = [g.rearrange("p (k n) -> p k n", k=4) for g in gate_w]

    x_in, cst_in, small_in, cw_in, dve_step, hn_ready = map(sem, ("x_in", "cst_in", "small_in", "cw_in", "dve_step", "hn_ready"))
    v_ready, root_ready = sem("v_ready"), sem("root_ready")
    t_mm, t_ev = sem("t_mm"), [sem("t_ev_dve"), sem("t_ev_act")]
    bias_mm, bias_sb, bias_out, bias_in = map(sem, ("bias_mm", "bias_sb", "bias_out", "bias_in"))
    w_in = [sem(f"w_in{s}") for s in range(4)]
    w_used, mm_done, mm_ev = map(sem, ("w_used", "mm_done", "mm_ev"))
    gate_ready = sem("gate_ready")
    u_ready, shift_a, shift_b, out_done = map(sem, ("u_ready", "shift_a", "shift_b", "out_done"))
    qkv_ready, vn_in = sem("qkv_ready"), sem("vn_in")
    w1_in, w2_in, pe_in_s, page_s, page_used = sem("w1_in"), sem("w2_in"), sem("pe_in"), [sem("page_in0"), sem("page_in1")], sem("page_used")
    raw_ready, cmp_mm, hid_ready, kc_mm, kc_ready, kcT_mm, cmp_done = map(sem, (
        "raw_ready", "cmp_mm", "hid_ready", "kc_mm", "kc_ready", "kcT_mm", "cmp_done"))
    s_mm, biased, exp_done, p_scaled, pt_mm, pt_ev, o_mm, o_ev = map(sem, (
        "s_mm", "biased", "exp_done", "p_scaled", "pt_mm", "pt_ev", "o_mm", "o_ev"))
    past_in, gs_mm = [sem("past_in0"), sem("past_in1")], sem("gs_mm")
    attT_mm, attT_ev = sem("attT_mm"), sem("attT_ev")
    merged, dup_in, n2_ready = sem("merged"), sem("dup_in"), sem("n2_ready")
    h_ready = sem("h_ready")
    keys_s, keys_mm, keys_ev, sc_mm, sc_ev, qT_done = map(sem, ("keys_in", "keys_mm", "keys_ev", "sc_mm", "sc_ev", "qT_done"))
    e_in, e_out, idx_ready = sem("e_in"), sem("e_out"), sem("idx_ready")
    idx_set, u_used, v_used = sem("idx_set"), sem("u_used"), sem("v_used")
    u_in = [sem(f"u_in{j}") for j in range(4)]
    v_in = [sem(f"v_in{j}") for j in range(4)]
    dots, gelu_done, diag_ready, peer_mm = map(sem, ("dots", "gelu_done", "diag_ready", "peer_mm"))
    ple_in, pleT_mm, pleT_ev, ple_mm, sig_ready, y_ready = map(sem, ("ple_in", "pleT_mm", "pleT_ev", "ple_mm", "sig_ready", "y_ready"))
    loop_step, slot_seen = sem("loop_step"), sem("slot_seen")
    h_seen = sem("h_seen")
    gw_in = [sem(f"gate_w_in{j}") for j in range(3)]
    gw_used, p_in_s, hT_mm, hT_ev, gate_mm = map(sem, ("gate_w_used", "p_in", "hT_mm", "hT_ev", "gate_mm"))

    N_Z, N_OUT, N_WQ, N_GATE = 0, 12, 16, 20
    w_in_cols = [QKV + GATES + 512 * i for i in range(6)] + [512 * i for i in range(5)] + [QKV]
    TBLOCKS = [HD * i for i in range(NH)] + [1024, 1152, 1280, 1408, 1536, 1664, 2048, 2176]
    GROUPS = (PH * PK // 4, PH * PK // 4, PH * PK // 8)
    LAST = GROUPS[0] + GROUPS[1]
    PICKING = 16

    def gate_quarters(i):
        if i < 4:
            return []
        b, j = divmod(i - 4, 3)
        return [4 * b + q for q in ((0,), (1,), (2, 3))[j]]

    w_view = {
        "in": I["w_in"][0].rearrange("(k p) n -> p k n", p=128),
        "out": I["w_out"][0].rearrange("(k p) n -> p k n", p=128),
        "wq": I["peer_wq"][0].rearrange("(k p) n -> p k n", p=128),
        "gate": I["ple_gate"][0].rearrange("(k p) n -> p k n", p=128),
    }
    xp = I["x_prompt"][0].rearrange("(t p) d -> t p d", p=128)
    xs = I["x_sample"].rearrange("b t d -> (b t) d")
    cache = I["cache_kv"][0].rearrange("n p s g d -> n p (s g d)")
    swin = I["state_win"][0].rearrange("b (a p) s g d -> b p a (s g d)", p=128)
    kv_p = O[2][0].rearrange("b (t p) s g d -> (b t) p (s g d)", p=128)
    win_p = O[3][0].rearrange("b (t p) s g d -> (b t) p (s g d)", p=128)
    kv_s = O[5][0].rearrange("b t s g d -> (b t) (s g d)")
    win_s = O[6][0].rearrange("b t s g d -> b t (s g d)")

    block = ctx.enter_context(nc.Block())

    @block.sync
    def _(sp):
        def tiles_of(src_p, src_s, dst, s):
            for t in range(2):
                sp.dma_start(dst[:, t, :], src_p[t]).then_inc(s, 16)
            sp.dma_start(dst[0:64, 2, :], src_s).then_inc(s, 16)

        sp.dma_start(cst, I["cst"]).then_inc(cst_in, 16)
        tiles_of(xp, xs, h, x_in)
        for i, name in enumerate(("norm1", "norm2", "norm3", "out_gain")):
            with nc.allow_non_contiguous_dma(reason="a gain by channel"):
                sp.dma_start(gT[:, i, :], I[name][0].rearrange("(k p) -> p k", p=128)).then_inc(small_in, 16)
        sp.dma_start(tab[0:NBUCKET, :], I["rel_bias"]).then_inc(small_in, 16)
        sp.dma_start(pages[0:1, :], I["page_table"].rearrange("(o b) n -> o (b n)", o=1)).then_inc(small_in, 16)
        sp.dma_start(qg, bass.AP(I["qk_gain"].tensor, 0, [[0, 128], [HD, 4], [1, HD]])).then_inc(small_in, 16)
        sp.dma_start(cw[:, 0:3, :], bass.AP(I["conv_w"].tensor, 0, [[0, 128], [CONV, 3], [1, CONV]])).then_inc(cw_in, 16)
        sp.dma_start(cw[:, 3, :], bass.AP(I["conv_b"].tensor, 0, [[0, 128], [1, CONV]])).then_inc(cw_in, 16)

        def fill(f, src, n=512):
            sp.wait_ge(w_used, f + 1)
            sp.dma_start(ring[f % 4][:, :, 0:n], src).then_inc(w_in[f % 4], 16)

        for blk, c0 in enumerate(w_in_cols):
            n = GATES if blk == 11 else 512
            for half in range(2):
                fill(2 * blk + half, w_view["in"][:, 8 * half:8 * half + 8, c0:c0 + n], n)
        sp.dma_start(win_s[:, 0:PAST - NT, :], I["state_win"][0].rearrange("b t s g d -> b t (s g d)")[:, NT:, :])\
          .then_inc(out_done, 16)

        sp.wait_ge(bias_sb, 1)
        sp.dma_start(bias_dram, rep(bias_row[0:NH, :], [0, 128], [1, NBIAS])).then_inc(bias_out, 16)
        sp.wait_ge(bias_out, 16)
        bt = bias_dram.tensor
        sp.dma_start(bias_p, bass.AP(bt, DMAX - 128, [[NBIAS - 1, 128], [128 * NBIAS, NH], [1, 256]])).then_inc(bias_in, 16)
        for r in range(2 * NH):
            sp.dma_start(bias_s[NT * r:NT * r + NT, :],
                         bass.AP(bt, (r % NH) * 128 * NBIAS + DMAX - PAST, [[NBIAS - 1, NT], [1, DMAX + 1]])).then_inc(bias_in, 16)

        sp.wait_ge(u_ready, 1)
        sp.dma_start(O[4][0, 0], cu[126:128, 1, :]).then_inc(out_done, 16)
        for w in range(2):
            sp.dma_start(O[7][0][:, w, :], cu[NT - 2 + w:64:NT, 2, :]).then_inc(out_done, 16)
        for d, dst in ((1, sh1), (2, sh2)):
            for t in range(3):
                sp.dma_start(dst[d:ROWS[t], t, :], cu[0:ROWS[t] - d, t, :]).then_inc(shift_a, 16)
            sp.dma_start(dst[0:d, 1, :], cu[128 - d:128, 0, :]).then_inc(shift_a, 16)
        sp.wait_ge(shift_a, 8 * 16)
        sc = I["state_conv"][0]
        sp.dma_start(sh1[0:64:NT, 2, :], sc[:, 1, :]).then_inc(shift_b, 16)
        sp.dma_start(sh2[0:64:NT, 2, :], sc[:, 0, :]).then_inc(shift_b, 16)
        sp.dma_start(sh2[1:64:NT, 2, :], sc[:, 1, :]).then_inc(shift_b, 16)

        sp.wait_ge(qkv_ready, 1)
        for t in range(2):
            sp.dma_start(kv_p[t], z[:, t, 1024:2048]).then_inc(out_done, 16)
            sp.dma_start(win_p[t], z[:, t, 2048:2560]).then_inc(out_done, 16)
        sp.dma_start(kv_s, z[0:64, 2, 1024:2048]).then_inc(out_done, 16)
        for b in range(NB):
            sp.dma_start(win_s[b, PAST - NT:PAST, :], z[b * NT:b * NT + NT, 2, 2048:2560]).then_inc(out_done, 16)
            for i, c0 in enumerate((1792, 2304)):
                sp.dma_start(vn[0:NT, b, i, :], z[b * NT:b * NT + NT, 2, c0:c0 + 256]).then_inc(vn_in, 16)

        def page(b, a):
            return sp.value_load(pages[0:1, 2 * b + a:2 * b + a + 1], min_val=0, max_val=I["cache_kv"].shape[1] - 1)

        sp.wait_ge(mm_done, 12)
        for kind in range(2):
            if kind:
                sp.wait_ge(cmp_mm, 2)
                sp.wait_ge(kc_mm, 1)
            sp.dma_start(w1, I["cmp_w1"][0, kind].rearrange("(m d) h -> d m h", d=HD)).then_inc(w1_in, 16)
            sp.dma_start(w2, I["cmp_w2"][0, kind].rearrange("(a p) h -> p a h", p=128)).then_inc(w2_in, 16)
            sp.dma_start(pe_in[0:BLK, :], I["cmp_pe"][0, kind]).then_inc(pe_in_s, 16)
            for b in range(NB):
                if NB * kind + b >= 2:
                    sp.wait_ge(page_used, NB * kind + b - 1)
                for a in range(2):
                    sp.dma_start(page_in[:, b % 2, a, :],
                                 cache[bass.ds(page(b, a), 1), :, 256 * kind:256 * kind + 256]
                                 .rearrange("o p n -> p (o n)")).then_inc(page_s[b % 2], 16)

        sp.wait_ge(cmp_mm, 4)
        for s in range(NB // 2):
            if s >= 2:
                sp.wait_ge(o_mm, 16 + s - 1)
            for bb in range(2):
                b = 2 * s + bb
                for a in range(2):
                    sp.dma_start(past_rows(s, bb, 0, a),
                                 cache[bass.ds(page(b, a), 1), :, 512:1024].rearrange("o p n -> p (o n)"))\
                      .then_inc(past_in[s % 2], 16)
                sp.dma_start(buf(W0 + 5120 + (((s % 2) * 2 + bb) * 2 + 1) * 1024, 2, 512), swin[b]).then_inc(past_in[s % 2], 16)

        sp.wait_ge(merged, 1)
        tiles_of(xp, xs, h, x_in)
        for blk in range(4):
            for half in range(2):
                fill(2 * (N_OUT + blk) + half, w_view["out"][:, 8 * half:8 * half + 8, 512 * blk:512 * blk + 512])
        sp.dma_start(g2, bass.AP(I["norm2"].tensor, 0, [[0, 128], [1, D]])).then_inc(dup_in, 16)
        sp.dma_start(keys_in, I["peer_keys"][0].rearrange("a n k -> n a k")).then_inc(keys_s, 16)
        sp.wait_ge(h_ready, 1)
        sp.dma_start(h[64:128, 2, :], h[0:64, 2, :]).then_inc(dup_in, 16)
        for blk in range(4):
            for half in range(2):
                fill(2 * (N_WQ + blk) + half, w_view["wq"][:, 8 * half:8 * half + 8, 512 * blk:512 * blk + 512])
        tiles_of(I["p_prompt"][0, 0].rearrange("(t p) d -> t p d", p=128),
                 I["p_sample"][0].rearrange("b t d -> (b t) d"), p_in, p_in_s)
        sp.wait_ge(idx_ready, 3)
        sp.dma_start(ple_w, I["ple_proj"][0].rearrange("(k p) n -> p k n", p=128)).then_inc(ple_in, 16)
        sp.wait_ge(u_used, 4 + 4 * LAST)
        yp = O[0][0].rearrange("(t p) d -> t p d", p=128)
        ys = O[1].rearrange("b t d -> (b t) d")

        def y_out(b):
            sp.wait_ge(y_ready, b + 1)
            cols = slice(512 * b, 512 * b + 512)
            for t in range(2):
                sp.dma_start(yp[t][:, cols], h[:, t, cols]).then_inc(out_done, 16)

        for q in range(16):
            if q >= 3:
                sp.wait_ge(gw_used, q - 2)
            sp.dma_start(gate_w[q % 3], w_view["gate"][:, 4 * (q % 4):4 * (q % 4) + 4, 512 * (q // 4):512 * (q // 4) + 512])\
              .then_inc(gw_in[q % 3], 16)
            if q >= 8 and q % 4 == 0:
                y_out(q // 4 - 2)
        y_out(2)
        sp.wait_ge(u_used, 4 + 4 * (LAST + GROUPS[2]))
        sp.wait_ge(v_used, 4 + 4 * (LAST + GROUPS[2]))
        for blk in range(4):
            for half in range(2):
                fill(2 * (N_GATE + blk) + half, w_view["gate"][:, 8 * half:8 * half + 8, 512 * blk:512 * blk + 512])
        y_out(3)
        for blk in range(4):
            sp.wait_ge(y_ready, 4 + blk + 1)
            cols = slice(512 * blk, 512 * blk + 512)
            sp.dma_start(ys[:, cols], h[0:64, 2, cols]).then_inc(out_done, 16)
        sp.wait_ge(out_done, 16 * (1 + 3 + 5 + NB + 12))

    @block.gpsimd
    def _(pool):
        def gathers(k, par):
            pool.wait_ge(idx_set, k + 1)
            for j in range(4):
                pool.wait_ge(u_used, 4 * k + j + 1)
                pool.sem_inc(slot_seen, 1)
                pool.indirect_dma_start(u_row[j], None, I["peer_u"][0],
                                        bass.IndirectOffsetOnAxis(idx4[:, par, j:j + 1], 0)).then_inc(u_in[j], 16)
            for j in range(4):
                pool.wait_ge(v_used, 4 * k + j + 1)
                pool.sem_inc(slot_seen, 1)
                pool.indirect_dma_start(v_row[j], None, I["peer_v"][0],
                                        bass.IndirectOffsetOnAxis(idx4[:, par, j:j + 1], 0)).then_inc(v_in[j], 16)

        with pool.Fori(0, sum(GROUPS) // 2) as i:
            for par in range(2):
                gathers(i * 2 + par, par)

    @block.scalar
    def _(act):
        act.sem_inc(mm_ev, 2)
        roots = [0]

        def root(src, dst):
            roots[0] += 1
            act.wait_ge(v_ready, roots[0])
            act.activation(dst, src, ACT.Sqrt).then_inc(root_ready, 1)

        tcount = [0]

        def odd_transposes(n, put):
            for c in range(1, n, 2):
                act.wait_ge(t_mm, tcount[0] + c + 1)
                put(act, c).then_inc(t_ev[1], 1)
            tcount[0] += n

        root(stats[:, 0:3], stats[:, 3:6])
        act.wait_ge(small_in, 16 * 7)
        odd_transposes(KC, lambda e, c: e.activation(xT[:, c, 0:TOK], bank[7][:, 0:TOK], ACT.Copy, scale=gT[:, 0, c:c + 1]))

        def z_out(n, wait, dst):
            act.wait_ge(mm_done, wait)
            for t in range(3):
                ins = act.activation(dst(t), bank[3 * (n % 2) + t][0:ROWS[t], :], ACT.Copy)
            ins.then_inc(mm_ev, 1)

        for part, region in enumerate((bg, cu, sh1)):
            with act.Fori(part, part + 1) as i:
                for j in range(2):
                    z_out(j, i * 2 + j + 1, lambda t: region[0:ROWS[t], t, 512 * j:512 * j + 512])
        with act.Fori(0, 2) as i:
            for j in range(2):
                z_out(j, i * 2 + 6 + j + 1, lambda t: z[0:ROWS[t], t, bass.ds(i * 1024 + 512 * j, 512)])
        z_out(10, 11, lambda t: z[0:ROWS[t], t, 2048:2560])
        act.wait_ge(mm_done, 12)
        for t in range(3):
            ins = act.activation(gate[0:ROWS[t], t, :], bank[3 + t][0:ROWS[t], 0:GATES], ACT.Sigmoid)
        ins.then_inc(mm_ev, 1)
        root(stats[:, 36:72], stats[:, 72:108])

        def heads_out(e, c):
            ins = e.activation(qkT[:, c, :], bank[7][:, 0:TOK], ACT.Copy)
            if c < NH:
                ins = e.activation(qsT[:, :, c, :], bank[7][:, 256:TOK].rearrange("p (b t) -> p b t", b=NB), ACT.Copy)
            return ins
        odd_transposes(16, heads_out)

        for kind in range(2):
            if kind:
                act.wait_ge(cmp_mm, 2)
            act.activation(raw[:, 0:NG, :], qkT[:, 8 + 2 * kind:10 + 2 * kind, 0:256], ACT.Copy).then_inc(raw_ready, 1)

            def raw_out(e, c):
                dst = raw[:, 2 + 2 * c:4 + 2 * c, :].rearrange("p g (a x) -> p a g x", a=2)
                return e.activation(dst, bank[7][:, :].rearrange("p (a g x) -> p a g x", a=2, g=2), ACT.Copy)
            odd_transposes(NB, raw_out)
            odd_transposes(1, raw_out)
            for hb in range(2):
                act.wait_ge(cmp_mm, 2 * kind + hb + 1)
                act.activation(pecol[:, hb:hb + 1], bank[hb][:, SEQS * NWIN:SEQS * NWIN + 1], ACT.Copy).then_inc(e_out, 1)
                act.wait_ge(e_out, 2 * kind + hb + 1)
                act.activation(hid[:, hb, :], bank[hb][:, 0:SEQS * NWIN], ACT.Gelu_apprx_tanh,
                               bias=pecol[:, hb:hb + 1]).then_inc(hid_ready, 1)
            if kind == 0:
                root(stats[:, 108:111], stats[:, 111:114])

        def softmax_exp(u, rows_list, par):
            act.wait_ge(biased, u + 1)
            for br, ap in rows_list:
                ins = act.activation(ap, ap, ACT.Exp, bias=nm[:, par, br:br + 1], accum_out=sm[:, par, br:br + 1])
            ins.then_inc(exp_done, 1)

        def prompt_pt(u):
            t = u // NH
            act.wait_ge(pt_mm, u + 1)
            if t:
                act.activation(pT[:, u % 2, 0:512], bank[4 + u % 2][:, :], ACT.Copy)
            else:
                act.activation(pT[:, u % 2, 0:512].rearrange("p (a b) -> p a b", a=2)[:, :, 0:128],
                               bank[4 + u % 2][:, :].rearrange("p (a b) -> p a b", a=2)[:, :, 0:128], ACT.Copy)
            nc_ = NWIN if t else 7
            act.activation(pT[0:nc_, u % 2, 512:640], bank[2 + u % 2][0:nc_, 128:256], ACT.Copy).then_inc(pt_ev, 1)

        def prompt_o(u):
            t, hh = u // NH, u % NH
            act.wait_ge(o_mm, u + 1)
            act.activation(att[:, t, hh * HD:hh * HD + HD], bank[6 + u % 2][:, 0:HD], ACT.Copy).then_inc(o_ev, 1)

        def prompt_rows(u):
            t = u // NH
            nk = 128 * (t + 1)
            return [(0, pb[:, u % 2, 512:512 + (NWIN if t else 7)]), (1, pb[:, u % 2, 0:nk]), (2, pb[:, u % 2, 256:256 + nk])]

        for u in range(17):
            if u < 16:
                softmax_exp(u, prompt_rows(u), u % 2)
            if u:
                prompt_pt(u - 1)
            if u > 1:
                prompt_o(u - 2)
        prompt_o(15)

        for s in range(4):
            u = 16 + s
            odd_transposes(4, lambda e, c: e.activation(
                pastT[:, c // 2, c % 2].rearrange("p a b d -> p (a b d)"), bank[7][:, :], ACT.Copy))
            softmax_exp(u, [(0, pb[:, 0, 528:528 + NWIN]), (1, pb[:, 0, 0:264]), (2, pb[:, 0, 264:528])], 0)
            act.wait_ge(pt_mm, u + 1)
            act.activation(pT[:, 0, 0:512], bank[4][:, :], ACT.Copy)
            act.activation(pT[0:NT, 0, 512:768], bank[5][0:NT, 0:256], ACT.Copy)
            act.activation(pT[0:NWIN, 0, 768:896], bank[5][0:NWIN, 256:384], ACT.Copy).then_inc(pt_ev, 1)
            act.wait_ge(o_mm, u + 1)
            for bb in range(2):
                ins = act.activation(attT[:, :, (2 * s + bb) * NT:(2 * s + bb) * NT + NT],
                                     bank[5][:, 384 + 64 * bb:448 + 64 * bb].rearrange("p (h t) -> p h t", h=NH), ACT.Copy)
            ins.then_inc(o_ev, 1)
        for i in range(2):
            act.wait_ge(attT_mm, i + 1)
            act.activation(att[0:64, 2, 512 * i:512 * i + 512], bank[i][0:64, :], ACT.Copy).then_inc(attT_ev, 1)
        root(stats[:, 120:126], stats[:, 126:132])
        odd_transposes(KC, lambda e, c: e.activation(xT[:, c, 0:TOK], bank[7][:, 0:TOK], ACT.Copy, scale=gT[:, 3, c:c + 1]))

        root(stats[:, 136:139], stats[:, 139:142])
        odd_transposes(KC, lambda e, c: e.activation(xT[:, c, :], bank[7][:, 0:384], ACT.Copy))
        for blk in range(4):
            act.wait_ge(mm_done, N_WQ + blk + 1)
            for sub in range(4):
                ins = act.activation(qT[:, 4 * blk + sub, :], bank[4 * (blk % 2) + sub][:, 0:384], ACT.Copy)
            ins.then_inc(qT_done, 1)
        act.wait_ge(keys_mm, 1)
        act.activation(keysT, bank[0][:, 0:256].rearrange("p (a b) -> p a b", a=2), ACT.Copy).then_inc(keys_ev, 1)
        for t in range(3):
            for q in range(4):
                act.wait_ge(sc_mm, 4 * t + q + 1)
                act.activation(score[:, t, 512 * q:512 * q + 512], bank[4 * (t % 2) + q][:, :], ACT.Copy).then_inc(sc_ev, 1)
        act.wait_ge(pleT_mm, 1)
        for c in range(2):
            ins = act.activation(pleT[:, c, :], bank[c][:, 0:TOK], ACT.Copy)
        ins.then_inc(pleT_ev, 1)

        def pick_exp(t):
            act.wait_ge(e_in, t + 1)
            act.activation(fv, fv, ACT.Exp).then_inc(e_out, 1)

        def gate_sigmoid(b):
            act.wait_ge(gate_mm, b + 1)
            if b:
                act.wait_ge(y_ready, b)
            for t in range(2):
                ins = act.activation(sig[:, t, :], bank[4 + t][:, :], ACT.Sigmoid, scale=stats[:, 147 + t:148 + t])
            ins.then_inc(sig_ready, 1)

        def gelu(k, par):
            act.wait_ge(dots, k + 1)
            act.activation(w4[:, par, :], a4[:, par, :], ACT.Gelu_apprx_tanh).then_inc(gelu_done, 1)

        pick_exp(0)
        for i in range(PICKING):
            if i == 7:
                pick_exp(1)
            if i == 14:
                pick_exp(2)
            gelu(i, i % 2)
        with act.Fori(0, (GROUPS[0] - PICKING) // 2) as i:
            for jj in range(2):
                gelu(i * 2 + (PICKING + jj), jj)
        with act.Fori(0, GROUPS[1] // 2) as i:
            for jj in range(2):
                gelu(i * 2 + (GROUPS[0] + jj), jj)
        for i in range(GROUPS[2]):
            if i == 2:
                root(stats[:, 144:146], stats[:, 147:149])
            if i in (3, 4):
                act.wait_ge(hT_mm, i - 2)
                for j in range(4):
                    c = 8 * (i - 3) + 4 + j
                    ins = act.activation(hT[:, c, :], bank[6 + j // 2][:, 256 * (j % 2):256 * (j % 2) + 256], ACT.Copy,
                                         scale=gT[:, 2, c:c + 1])
                ins.then_inc(hT_ev, 1)
            if i in (7, 10, 13):
                gate_sigmoid((i - 7) // 3)
            gelu(LAST + i, i % 2)
        gate_sigmoid(3)
        root(stats[:, 146:147], stats[:, 149:150])
        odd_transposes(KC, lambda e, c: e.activation(hT_s[:, c, :], bank[7][:, 0:64], ACT.Copy, scale=gT[:, 2, c:c + 1]))
        for blk in range(4):
            act.wait_ge(mm_done, N_GATE + blk + 1)
            if blk >= 2:
                act.wait_ge(y_ready, 4 + blk - 1)
            act.activation(sig[0:64, blk % 2, :], bank[blk % 2][0:64, :], ACT.Sigmoid, scale=stats[0:64, 149:150])\
               .then_inc(sig_ready, 1)

    @block.vector
    def _(dve):
        steps = [0]

        def step(ins):
            steps[0] += 1
            ins.then_inc(dve_step, 1)
            dve.wait_ge(dve_step, steps[0])

        roots = [0]

        def inv_rms(ss, v, y, t, width):
            step(dve.tensor_scalar(v, ss, 1.0 / width, EPS, ALU.mult, ALU.add))
            dve.sem_inc(v_ready, 1)
            roots[0] += 1
            dve.wait_ge(root_ready, roots[0])
            step(dve.reciprocal(y, y))
            step(dve.tensor_tensor(t, y, y, ALU.mult))
            step(dve.tensor_tensor(t, t, v, ALU.mult))
            step(dve.tensor_scalar(t, t, -0.5, 1.5, ALU.mult, ALU.add))
            step(dve.tensor_tensor(y, y, t, ALU.mult))

        tcount = [0]

        def even_transposes(n, put):
            for c in range(0, n, 2):
                dve.wait_ge(t_mm, tcount[0] + c + 1)
                put(dve, c).then_inc(t_ev[0], 1)
            tcount[0] += n

        def squares(src, junk, acc):
            return dve.tensor_tensor_reduce(out=junk, in0=src, in1=src, scale=1.0, scalar=0.0,
                                            op0=ALU.mult, op1=ALU.add, accum_out=acc)

        step(dve.memset(stats, 1.0))
        step(dve.memset(tab[NBUCKET:NBUCKET + 1, :], NEG))
        dve.wait_ge(x_in, 48)
        for t in range(3):
            ins = squares(h[0:ROWS[t], t, :], n_tok[0:ROWS[t], t, :], stats[0:ROWS[t], t:t + 1])
        step(ins)
        inv_rms(stats[:, 0:3], stats[:, 0:3], stats[:, 3:6], stats[:, 6:9], D)
        for t in range(3):
            ins = dve.tensor_scalar(h[0:ROWS[t], t, :], h[0:ROWS[t], t, :], stats[0:ROWS[t], 3 + t:4 + t], None, ALU.mult)
        ins.then_inc(hn_ready, 1)
        dve.wait_ge(small_in, 16 * 7)
        even_transposes(KC, lambda e, c: e.tensor_scalar(xT[:, c, 0:TOK], bank[6][:, 0:TOK], gT[:, 0, c:c + 1], None, ALU.mult))
        dve.wait_ge(bias_mm, 1)
        dve.tensor_copy(bias_row[0:NH, :], bank[0][0:NH, 0:NBIAS]).then_inc(bias_sb, 1)

        dve.wait_ge(mm_ev, 2 + 6)
        for t in range(3):
            r = ROWS[t]
            ins = dve.tensor_tensor(cu[0:r, t, :], cu[0:r, t, :], sh1[0:r, t, :], ALU.mult)
        step(ins)
        dve.memset(sh2[0:2, 0, :], 0.0)
        step(dve.memset(sh1[0:1, 0, :], 0.0))
        dve.sem_inc(u_ready, 1)
        dve.wait_ge(shift_a, 8 * 16)
        dve.wait_ge(shift_b, 3 * 16)
        dve.wait_ge(cw_in, 32)
        for op in range(7):
            for t in range(3):
                r = ROWS[t]
                a, b, c, g = sh1[0:r, t, :], sh2[0:r, t, :], cu[0:r, t, :], bg[0:r, t, :]
                out, x, y, alu = ((a, a, cw[0:r, 1, :], ALU.mult), (b, b, cw[0:r, 0, :], ALU.mult), (a, a, b, ALU.add),
                                  (b, c, cw[0:r, 2, :], ALU.mult), (a, a, b, ALU.add), (a, a, cw[0:r, 3, :], ALU.add),
                                  (g, g, a, ALU.mult))[op]
                ins = dve.tensor_tensor(out, x, y, alu)
            step(ins)
        for t in range(3):
            r = ROWS[t]
            ins = squares(bg[0:r, t, :], sh1[0:r, t, :], stats[0:r, 123 + t:124 + t])
        step(ins)

        dve.wait_ge(mm_ev, 2 + 12)
        HEADS = ((0, 8, 0, 0), (1536, 2, 8, 2), (2048, 2, 10, 3))
        for t in range(3):
            r = ROWS[t]
            for c0, nh, s0, _ in HEADS:
                v = z[0:r, t, c0:c0 + nh * HD]
                step(dve.tensor_tensor(sh2[0:r, t, 0:nh * HD], v, v, ALU.mult))
                step(dve.tensor_reduce(stats[0:r, 36 + 12 * t + s0:36 + 12 * t + s0 + nh],
                                       sh2[0:r, t, 0:nh * HD].rearrange("p (n d) -> p n d", d=HD), AX.X, ALU.add))
        inv_rms(stats[:, 36:72], stats[:, 36:72], stats[:, 72:108], stats[:, 160:196], HD)
        qs = stats[:, 72:108].rearrange("p (t n) -> p t n", t=3)[:, :, 0:NH]
        step(dve.tensor_scalar(qs, qs, HD ** -0.5, None, ALU.mult))
        for t in range(3):
            r = ROWS[t]
            for c0, nh, s0, gi in HEADS:
                for n in range(nh):
                    v = z[0:r, t, c0 + n * HD:c0 + n * HD + HD]
                    k = 72 + 12 * t + s0 + n
                    ins = dve.scalar_tensor_tensor(out=v, in0=v, scalar=stats[0:r, k:k + 1], in1=qg[0:r, gi, :],
                                                   op0=ALU.mult, op1=ALU.mult)
        step(ins)
        dve.sem_inc(qkv_ready, 1)

        def heads_out(e, c):
            ins = e.tensor_copy(qkT[:, c, :], bank[6][:, 0:TOK])
            if c < NH:
                ins = e.tensor_copy(qsT[:, :, c, :], bank[6][:, 256:TOK].rearrange("p (b t) -> p b t", b=NB))
            return ins
        even_transposes(16, heads_out)

        step(dve.memset(raw[:, SEQS, :], 0.0))
        for kind in range(2):
            if kind:
                dve.wait_ge(cmp_mm, 2)
            even_transposes(NB, lambda e, c: e.tensor_copy(
                raw[:, 2 + 2 * c:4 + 2 * c, :].rearrange("p g (a x) -> p a g x", a=2),
                bank[6][:, :].rearrange("p (a g x) -> p a g x", a=2, g=2)))
            dve.wait_ge(raw_ready, 2 * kind + 1)
            dve.wait_ge(t_mm, tcount[0] + 1)
            dve.tensor_copy(raw[:, SEQS, 0:BLK], bank[6][:, 0:BLK]).then_inc(t_ev[0], 1)
            tcount[0] += 1
            dve.sem_inc(raw_ready, 1)
            if kind == 0:
                dve.wait_ge(kc_mm, 1)
                for i in range(3):
                    ins = dve.tensor_copy(kct[0:90, i, :], bank[2][0:90, i * HD:i * HD + HD])
                step(ins)
                for i in range(3):
                    ins = squares(kct[0:90, i, :], scr[0:90, 0].rearrange("p a b -> p (a b)")[:, 0:HD], stats[0:90, 108 + i:109 + i])
                    step(ins)
                inv_rms(stats[:, 108:111], stats[:, 108:111], stats[:, 111:114], stats[:, 114:117], HD)
                for i in range(3):
                    ins = dve.scalar_tensor_tensor(out=kct[0:90, i, :], in0=kct[0:90, i, :], scalar=stats[0:90, 111 + i:112 + i],
                                                   in1=qg[0:90, 1, :], op0=ALU.mult, op1=ALU.mult)
                ins.then_inc(kc_ready, 1)
                dve.wait_ge(kcT_mm, 1)
                dve.tensor_copy(kcT, bank[3][:, 0:SEQS * NWIN]).then_inc(cmp_done, 1)
            else:
                for q in range(5):
                    dve.wait_ge(kc_mm, 2 + q)
                    n = min(4, SEQS - 4 * q)
                    dve.tensor_copy(vc[0:NWIN, 4 * q:4 * q + n, :],
                                    bank[(2, 3, 4, 5, 0)[q]][0:NWIN, 0:n * HD].rearrange("p (a b) -> p a b", a=n))\
                       .then_inc(cmp_done, 1)
        dve.wait_ge(gs_mm, 1)
        step(dve.tensor_tensor(g24, bank[1][:, 0:96].rearrange("p (s c h) -> p s c h", s=4, c=3),
                               rep(cst[:, C_HM:], [0, 4], [NH, 3], [1, NH]), ALU.mult))
        dve.sem_inc(cmp_done, 1)
        step(dve.tensor_reduce(gs, g24, AX.X, ALU.add))

        def bias_max(u, par, parts):
            dve.wait_ge(s_mm, u + 1)
            for br, out, src, bias in parts:
                ins = dve.tensor_tensor_reduce(out=out, in0=src, in1=bias, scale=1.0, scalar=-3.0e38,
                                               op0=ALU.add, op1=ALU.max, accum_out=mx[:, par, br:br + 1])
            step(ins)
            step(dve.tensor_scalar(nm[:, par, :], mx[:, par, :], -1.0, None, ALU.mult))
            dve.sem_inc(biased, 1)

        def weigh(u, par, parts, gates_, mask):
            dve.wait_ge(exp_done, u + 1)
            step(dve.reciprocal(cf[:, par, :], sm[:, par, :]))
            step(dve.tensor_tensor(cf[:, par, :], cf[:, par, :], gates_, ALU.mult))
            if mask:
                step(dve.tensor_tensor(cf[:, par, 0:1], cf[:, par, 0:1], cst[:, C_VM:C_VM + 1], ALU.mult))
            for br, out, _, _ in parts:
                ins = dve.tensor_scalar(out, out, cf[:, par, br:br + 1], None, ALU.mult)
            step(ins)
            dve.sem_inc(p_scaled, 1)

        def prompt_parts(u):
            t, hh, par = u // NH, u % NH, u % 2
            nk = 128 * (t + 1)
            s, c = bank[par], bank[2 + par]
            ncmp = NWIN if t else 7
            c0 = BLK - 1 if t else BLK - 1 + 128
            return [(0, pb[:, par, 512:512 + ncmp], c[:, 0:ncmp], bias_p[:, hh, c0:256:STRIDE][:, 0:ncmp]),
                    (1, pb[:, par, 0:nk], s[:, 0:nk], bias_p[:, hh, 256 - nk:256]),
                    (2, pb[:, par, 256:256 + nk], s[:, 256:256 + nk], bias_p[:, hh, 256 - nk:256])]

        dve.wait_ge(bias_in, 17 * 16)
        for u in range(17):
            if u < 16:
                if u >= 2:
                    dve.wait_ge(pt_mm, u - 1)
                bias_max(u, u % 2, prompt_parts(u))
            if u:
                v = u - 1
                weigh(v, v % 2, prompt_parts(v), gate[:, v // NH, v % NH:GATES:NH], v < NH)
        for s in range(4):
            u = 16 + s
            if s:
                dve.wait_ge(s_mm, u)
            even_transposes(4, lambda e, c: e.tensor_copy(
                pastT[:, c // 2, c % 2].rearrange("p a b d -> p (a b d)"), bank[6][:, :]))
            dve.wait_ge(pt_mm, u)
            parts = [(0, pb[:, 0, 528:528 + NWIN], bank[0][:, 264:264 + NWIN], bias_s[:, BLK - 1:256:STRIDE]),
                     (1, pb[:, 0, 0:264], bank[0][:, 0:264], bias_s),
                     (2, pb[:, 0, 264:528], bank[1][:, 0:264], bias_s)]
            bias_max(u, 0, parts)
            weigh(u, 0, parts, gs[:, s, :], False)

        dve.wait_ge(attT_ev, 2)
        dve.wait_ge(o_ev, 20)
        for t in range(3):
            r = ROWS[t]
            ins = squares(att[0:r, t, :], cu[0:r, t, :], stats[0:r, 120 + t:121 + t])
        step(ins)
        inv_rms(stats[:, 120:126], stats[:, 120:126], stats[:, 126:132], stats[:, 160:166], ATT)
        for t in range(3):
            r = ROWS[t]
            for src, k in ((att, 126 + t), (bg, 129 + t)):
                ins = dve.tensor_scalar(src[0:r, t, :], src[0:r, t, :], stats[0:r, k:k + 1], None, ALU.mult)
        ins.then_inc(hn_ready, 1)
        even_transposes(KC, lambda e, c: e.tensor_scalar(xT[:, c, 0:TOK], bank[6][:, 0:TOK], gT[:, 3, c:c + 1], None, ALU.mult))

        dve.wait_ge(x_in, 96)
        for blk in range(4):
            dve.wait_ge(mm_done, N_OUT + blk + 1)
            for t in range(3):
                v = h[0:ROWS[t], t, 512 * blk:512 * blk + 512]
                ins = dve.tensor_tensor(v, bank[3 * (blk % 2) + t][0:ROWS[t], :], v, ALU.add)
            ins.then_inc(mm_ev, 1)
        step(dve.memset(stats[:, 136:139], 0.0))
        dve.wait_ge(mm_ev, 2 + 16)
        dve.sem_inc(h_ready, 1)
        dve.wait_ge(dup_in, 32)
        for t in range(3):
            ins = squares(h[:, t, :], n_tok[:, t, :], stats[:, 136 + t:137 + t])
        step(ins)
        inv_rms(stats[:, 136:139], stats[:, 136:139], stats[:, 139:142], stats[:, 160:163], D)
        for t in range(3):
            ins = dve.scalar_tensor_tensor(out=n_tok[:, t, :], in0=h[:, t, :], scalar=stats[:, 139 + t:140 + t],
                                           in1=g2, op0=ALU.mult, op1=ALU.mult)
        ins.then_inc(hn_ready, 1)
        even_transposes(KC, lambda e, c: e.tensor_copy(xT[:, c, :], bank[6][:, 0:384]))

        iota = cst[:, C_IOTA:C_IOTA + PK * PK]
        cut = scr.rearrange("p a b c -> p (a b c)")

        def best8(half, n, width, src, val, ix):
            o = slice(8 * half, 8 * half + 8)
            src_ = cut if half else src
            for r in range(n):
                ins = dve.max(val[:, r, o], src_[:, r * width:r * width + width])
            step(ins)
            for r in range(n):
                ins = dve.max_index(ix[:, r, o].bitcast(u32), val[:, r, o], src_[:, r * width:r * width + width])
            step(ins)
            if half == 0:
                for r in range(n):
                    ins = dve.match_replace(cut[:, r * width:r * width + width], val[:, r, o],
                                            src[:, r * width:r * width + width], -3.0e38)
                step(ins)

        def pick(t, part):
            flat = cand.rearrange("p a b c -> p (a b c)")
            fiu = fi.bitcast(u32)
            if part == 0:
                best8(0, 16, NKEY, score[:, t, :], sv, si)
            elif part == 1:
                best8(1, 16, NKEY, score[:, t, :], sv, si)
                step(dve.tensor_copy(si, si.bitcast(u32)))
                for r in range(PH):
                    ins = dve.tensor_tensor(cand[:, r], rep(sv[:, 2 * r, :], [1, PK], [0, PK]),
                                            rep(sv[:, 2 * r + 1, :], [0, PK], [1, PK]), ALU.add)
                step(ins)
            elif part == 2:
                best8(0, PH, PK * PK, flat, fv, fi)
            elif part == 3:
                best8(1, PH, PK * PK, flat, fv, fi)
                dve.tensor_scalar(fh.bitcast(u32), fiu, 4, None, ALU.logical_shift_right)
                step(dve.tensor_scalar(fl.bitcast(u32), fiu, PK - 1, None, ALU.bitwise_and))
                dve.tensor_copy(fh, fh.bitcast(u32))
                step(dve.tensor_copy(fl, fl.bitcast(u32)))
            elif part < 6:
                side = part - 4
                pos, e = ((fh, e0), (fl, e1))[side]
                step(dve.tensor_tensor(cand, rep(pos, [PK, PH], [1, PK], [0, PK]),
                                       rep(iota, [0, PH], [PK, PK], [1, PK]), ALU.is_equal))
                step(dve.tensor_tensor(cand, cand, rep(si[:, side, :], [2 * PK, PH], [0, PK], [1, PK]), ALU.mult))
                step(dve.tensor_reduce(e, cand, AX.X, ALU.add))
            else:
                step(dve.scalar_tensor_tensor(out=e0, in0=e0, scalar=float(NKEY), in1=e1, op0=ALU.mult, op1=ALU.add))
                step(dve.tensor_copy(idx[:, t, :], e0.rearrange("p a b -> p (a b)")))
                step(dve.tensor_copy(e1[:, :, 0], fv[:, :, 0]))
                step(dve.tensor_tensor(fv, fv, rep(e1, [PK, PH], [0, PK]), ALU.subtract))
                dve.sem_inc(e_in, 1)
                dve.wait_ge(e_out, 4 + t + 1)
                step(dve.tensor_reduce(e1[:, :, 0], fv, AX.X, ALU.add))
                step(dve.reciprocal(e1[:, :, 1], e1[:, :, 0]))
                step(dve.tensor_tensor(wgt[:, t, :].rearrange("p (a b) -> p a b", a=PH), fv,
                                       rep(e1[:, :, 1], [PK, PH], [0, PK]), ALU.mult))
                if t == 2:
                    step(dve.tensor_copy(wgt[64:128, 2, 0:64], wgt[64:128, 2, 64:128]))
                    step(dve.tensor_copy(idx[64:128, 2, 0:64], idx[64:128, 2, 64:128]))
                dve.sem_inc(idx_ready, 1)

        dve.wait_ge(sc_ev, 12)
        for part in range(7):
            pick(0, part)
        dve.sem_inc(u_used, 4)
        dve.sem_inc(v_used, 4)

        def group(k, par, t, c0, between=None):
            dve.tensor_copy(idx4[:, par, :], idx[:, t, c0]).then_inc(idx_set, 1)
            for j in range(4):
                dve.wait_ge(u_in[j], (k + 1) * 16)
                ins = dve.tensor_tensor_reduce(out=u_row[j], in0=u_row[j], in1=n_tok[:, t, :], scale=1.0, scalar=0.0,
                                               op0=ALU.mult, op1=ALU.add, accum_out=a4[:, par, j:j + 1])
                ins.then_inc(u_used, 1)
            dve.wait_ge(u_used, k * 4 + 8)
            dve.sem_inc(dots, 1)
            if between:
                between()
            dve.wait_ge(gelu_done, k + 1)
            dve.tensor_tensor(w4[:, par, :], w4[:, par, :], wgt[:, t, c0], ALU.mult).then_inc(loop_step, 1)
            dve.wait_ge(loop_step, k + 1)
            for j in range(4):
                src = ident if t < 2 else cst[:, C_PAIR:C_PAIR + 64]
                ins = dve.tensor_scalar(diag[:, par, j, 0:(128 if t < 2 else 64)], src, w4[:, par, j:j + 1], None, ALU.mult)
            ins.then_inc(diag_ready, 1)

        def add_peer(t):
            dve.wait_ge(peer_mm, t + 1)
            for q in range(4):
                v = h[0:ROWS[t], t, 512 * q:512 * q + 512]
                ins = dve.tensor_tensor(v, bank[4 * (t % 2) + q][0:ROWS[t], :], v, ALU.add)
            step(ins)
            dve.sem_inc(h_seen, 1)

        def gate_rms():
            for t in range(2):
                step(squares(h[:, t, :], buf(Z0 + 8 * D, D), stats[:, 144 + t:145 + t]))
            inv_rms(stats[:, 144:146], stats[:, 144:146], stats[:, 147:149], stats[:, 160:162], D)

        def prompt_y(b):
            dve.wait_ge(sig_ready, b + 1)
            for t in range(2):
                ins = dve.tensor_tensor(sig[:, t, :], sig[:, t, :], bank[6 + t][:, :], ALU.mult)
            step(ins)
            for t in range(2):
                v = h[:, t, 512 * b:512 * b + 512]
                ins = dve.tensor_tensor(v, v, sig[:, t, :], ALU.add)
            step(ins)
            dve.sem_inc(y_ready, 1)

        def hT_out(rnd):
            dve.wait_ge(hT_mm, rnd + 1)
            for j in range(4):
                c = 8 * rnd + j
                ins = dve.tensor_scalar(hT[:, c, :], bank[4 + j // 2][:, 256 * (j % 2):256 * (j % 2) + 256],
                                        gT[:, 2, c:c + 1], None, ALU.mult)
            ins.then_inc(hT_ev, 1)

        def diag_free(k):
            dve.wait_ge(v_used, k * 4 - 4 + 4)

        for i in range(PICKING):
            if i >= 2:
                diag_free(i)
            group(i, i % 2, 0, slice(4 * i, 4 * i + 4),
                  (lambda: pick(1 + (i - 1) // 7, (i - 1) % 7)) if 1 <= i <= 14 else None)
        with dve.Fori(0, (GROUPS[0] - PICKING) // 2) as i:
            for jj in range(2):
                diag_free(i * 2 + (PICKING + jj))
                group(i * 2 + (PICKING + jj), jj, 0, bass.ds(i * 8 + 4 * (PICKING + jj), 4))
        with dve.Fori(0, GROUPS[1] // 2) as i:
            for jj in range(2):
                diag_free(i * 2 + (GROUPS[0] + jj))
                group(i * 2 + (GROUPS[0] + jj), jj, 1, bass.ds(i * 8 + 4 * jj, 4))
        extra = {0: lambda: add_peer(0), 1: lambda: add_peer(1), 2: gate_rms, 3: lambda: hT_out(0), 4: lambda: hT_out(1),
                 7: lambda: prompt_y(0), 10: lambda: prompt_y(1), 13: lambda: prompt_y(2)}
        for i in range(GROUPS[2]):
            diag_free(LAST + i)
            group(LAST + i, i % 2, 2, slice(4 * i, 4 * i + 4), extra.get(i))
        add_peer(2)
        ins = squares(h[0:64, 2, :], n_tok[0:64, 2, :], stats[0:64, 146:147])
        ins.then_inc(h_ready, 1)
        dve.wait_ge(h_ready, 2)
        inv_rms(stats[:, 146:147], stats[:, 146:147], stats[:, 149:150], stats[:, 160:161], D)
        prompt_y(3)
        even_transposes(KC, lambda e, c: e.tensor_scalar(hT_s[:, c, :], bank[6][:, 0:64], gT[:, 2, c:c + 1], None, ALU.mult))
        for blk in range(4):
            dve.wait_ge(sig_ready, 4 + blk + 1)
            s = sig[0:64, blk % 2, :]
            step(dve.tensor_tensor(s, s, bank[2 + blk % 2][0:64, :], ALU.mult))
            dve.sem_inc(ple_mm, 1)
            v = h[0:64, 2, 512 * blk:512 * blk + 512]
            step(dve.tensor_tensor(v, v, s, ALU.add))
            dve.sem_inc(y_ready, 1)

    @block.tensor
    def _(pe):
        pe.sem_inc(w_used, 4)
        runs = [0]
        evs = [0, 0]

        def transposes(n, src_of):
            for c in range(n):
                par = c % 2
                if evs[par] >= 1:
                    pe.wait_ge(t_ev[par], evs[par])
                for dst, src, rows in src_of(c):
                    ins = pe.transpose(bank[6 + par][0:src.shape[1], dst:dst + rows], src, ident[0:rows, 0:rows])
                ins.then_inc(t_mm, 1)
                evs[par] += 1

        def tok_tiles(src, rows=ROWS):
            return lambda c: [(128 * t, src(t, c)[0:rows[t], :], rows[t]) for t in range(3)]

        pe.wait_ge(cst_in, 16)
        pe.wait_ge(small_in, 16 * 7)
        pe.wait_ge(dve_step, 2)
        pe.matmul(bank[0][0:NH, 0:NBIAS], tab[0:NBUCKET + 1, :], cst[0:NBUCKET + 1, C_OH:C_OH + NBIAS],
                  start=True, stop=True).then_inc(bias_mm, 1)
        pe.wait_ge(hn_ready, 1)
        transposes(KC, tok_tiles(lambda t, c: h[:, t, 128 * c:128 * c + 128]))
        pe.wait_ge(t_ev[0], 8)
        pe.wait_ge(t_ev[1], 8)
        pe.wait_ge(bias_sb, 1)

        def product(n, done, f, par, width=512):
            pe.wait_ge(mm_ev, done)
            for half in range(2):
                slot = (2 * par + half) % 4
                pe.wait_ge(w_in[slot], f)
                for t in range(3):
                    for k in range(8):
                        ins = pe.matmul(bank[3 * par + t][0:ROWS[t], 0:width], xT[:, 8 * half + k, 128 * t:128 * t + ROWS[t]],
                                        ring[slot][:, k, 0:width], start=(half == 0 and k == 0), stop=(half == 1 and k == 7))
                ins.then_inc(w_used, 1)

        def blocks(first, count):
            with pe.Fori(0, count // 2) as i:
                for par in range(2):
                    product(None, i * 2 + (first + par + 1), i * 16 + (8 * first + 16), par)
                    pe.wait_ge(w_used, i * 4 + (4 + 2 * (first + par + 1)))
                    pe.sem_inc(mm_done, 1)

        blocks(0, 6)
        blocks(6, 4)
        for n in (10, 11):
            product(None, n + 1, 16 * (n // 2) + 16, n % 2, 512 if n == 10 else GATES)
            pe.wait_ge(w_used, 4 + 2 * (n + 1))
            pe.sem_inc(mm_done, 1)

        pe.wait_ge(qkv_ready, 1)
        transposes(16, tok_tiles(lambda t, c: z[:, t, TBLOCKS[c]:TBLOCKS[c] + 128]))
        pe.wait_ge(t_ev[0], evs[0])
        pe.wait_ge(t_ev[1], evs[1])

        for kind in range(2):
            def page_blocks(b):
                return [(128 * (2 * a + g), page_in[:, b % 2, a, g * HD:g * HD + HD], 128) for a in range(2) for g in range(2)]
            for b in range(NB):
                par = b % 2
                pe.wait_ge(page_s[par], 32 * (NB // 2 * kind + b // 2 + 1))
                pe.wait_ge(t_ev[par], evs[par])
                for dst, src, rows in page_blocks(b):
                    ins = pe.transpose(bank[6 + par][:, dst:dst + 128], src, ident)
                ins.then_inc(t_mm, 1)
                evs[par] += 1
                pe.wait_ge(t_mm, sum(evs))
                pe.sem_inc(page_used, 1)
            pe.wait_ge(pe_in_s, 16 * (kind + 1))
            transposes(1, lambda c: [(0, pe_in[0:BLK, :], BLK)])
            pe.wait_ge(t_ev[0], evs[0])
            pe.wait_ge(t_ev[1], evs[1])
            pe.wait_ge(raw_ready, 2 * kind + 2)
            pe.wait_ge(w1_in, 16 * (kind + 1))
            for hb in range(2):
                if kind:
                    pe.wait_ge(hid_ready, hb + 1)
                for m in range(BLK):
                    view = raw[:, :, m:m + STRIDE * (NWIN - 1) + 1:STRIDE]
                    ins = pe.matmul(bank[hb][:, 0:(SEQS + 1) * NWIN], w1[:, m, hb * 128:hb * 128 + 128], view,
                                    start=(m == 0), stop=(m == BLK - 1))
                ins.then_inc(cmp_mm, 1)
            pe.wait_ge(hid_ready, 2 * kind + 2)
            pe.wait_ge(w2_in, 16 * (kind + 1))
            if kind == 0:
                for i in range(3):
                    for hb in range(2):
                        ins = pe.matmul(bank[2][0:90, i * HD:i * HD + HD], hid[:, hb, 90 * i:90 * i + 90], w2[:, hb, :],
                                        start=(hb == 0), stop=(hb == 1))
                ins.then_inc(kc_mm, 1)
                pe.wait_ge(kc_ready, 1)
                for i in range(3):
                    ins = pe.transpose(bank[3][:, 90 * i:90 * i + 90], kct[0:90, i, :], ident[0:90, 0:90])
                ins.then_inc(kcT_mm, 1)
                pe.wait_ge(cmp_done, 1)
            else:
                for sg in range(SEQS):
                    q = sg // 4
                    for hb in range(2):
                        ins = pe.matmul(bank[(2, 3, 4, 5, 0)[q]][0:NWIN, (sg % 4) * HD:(sg % 4) * HD + HD],
                                        hid[:, hb, NWIN * sg:NWIN * sg + NWIN], w2[:, hb, :], start=(hb == 0), stop=(hb == 1))
                    if sg % 4 == 3 or sg == SEQS - 1:
                        ins.then_inc(kc_mm, 1)
        for s in range(4):
            ins = pe.matmul(bank[1][:, GATES * s:GATES * s + GATES], cst[0:64, C_SELG + 128 * s:C_SELG + 128 * s + 128],
                            gate[0:64, 2, :], start=True, stop=True)
        ins.then_inc(gs_mm, 1)
        pe.wait_ge(cmp_done, 7)

        def scores(u):
            t, hh, par = u // NH, u % NH, u % 2
            g = hh // HPG
            nk = 128 * (t + 1)
            if u >= 2:
                pe.wait_ge(biased, u - 1)
            q = qkT[:, hh, 128 * t:128 * t + 128]
            pe.matmul(bank[par][:, 0:nk], q, qkT[:, 12 + g, 0:nk], start=True, stop=True)
            pe.matmul(bank[par][:, 256:256 + nk], q, qkT[:, 14 + g, 0:nk], start=True, stop=True)
            ncmp = NWIN if t else 7
            pe.matmul(bank[2 + par][:, 0:ncmp], q, kcT[:, g * NWIN:g * NWIN + ncmp], start=True, stop=True).then_inc(s_mm, 1)

        def values(u):
            t, hh, par = u // NH, u % NH, u % 2
            g = hh // HPG
            ncmp = NWIN if t else 7
            pe.wait_ge(p_scaled, u + 1)
            if u >= 2:
                pe.wait_ge(pt_ev, u - 1)
            for w in range(2):
                for k in range(t + 1):
                    pe.transpose(bank[4 + par][:, 256 * w + 128 * k:256 * w + 128 * k + 128],
                                 pb[:, par, 256 * w + 128 * k:256 * w + 128 * k + 128], ident)
            pe.transpose(bank[2 + par][0:ncmp, 128:256], pb[:, par, 512:512 + ncmp], ident).then_inc(pt_mm, 1)
            pe.wait_ge(pt_ev, u + 1)
            if u >= 2:
                pe.wait_ge(o_ev, u - 1)
            first = True
            for w in range(2):
                for k in range(t + 1):
                    pe.matmul(bank[6 + par][:, 0:HD], pT[:, par, 256 * w + 128 * k:256 * w + 128 * k + 128],
                              z[:, k, (1792, 2304)[w] + g * HD:(1792, 2304)[w] + g * HD + HD], start=first, stop=False)
                    first = False
            pe.matmul(bank[6 + par][:, 0:HD], pT[0:ncmp, par, 512:640], vc[0:ncmp, g, :], start=False, stop=True)\
              .then_inc(o_mm, 1)

        for u in range(17):
            if u < 16:
                scores(u)
            if u:
                values(u - 1)
        pe.wait_ge(o_ev, 16)

        for s in range(4):
            u = 16 + s
            pe.wait_ge(past_in[s % 2], 96 * (s // 2 + 1))

            transposes(4, lambda c: [(128 * (2 * a + g), past_rows(s, c // 2, c % 2, a)[:, g * HD:g * HD + HD], 128)
                                     for a in range(2) for g in range(2)])
            pe.wait_ge(t_ev[0], evs[0])
            pe.wait_ge(t_ev[1], evs[1])
            pe.wait_ge(biased, u)
            for bb in range(2):
                b = 2 * s + bb
                for g in range(NG):
                    p0 = 64 * bb + 32 * g
                    q = qsT[:, b, HPG * g:HPG * g + HPG, :].rearrange("p h t -> p (h t)")
                    for br in range(2):
                        for a in range(2):
                            pe.matmul(bank[br][p0:p0 + 32, 128 * a:128 * a + 128], q, pastT[:, bb, br, a, g, :],
                                      start=True, stop=True)
                        pe.matmul(bank[br][p0:p0 + 32, 256:264], q, qkT[:, 12 + 2 * br + g, 256 + b * NT:256 + b * NT + NT],
                                  start=True, stop=True)
                    sg = 2 * (1 + b) + g
                    ins = pe.matmul(bank[0][p0:p0 + 32, 264:264 + NWIN], q, kcT[:, sg * NWIN:sg * NWIN + NWIN],
                                    start=True, stop=True)
            ins.then_inc(s_mm, 1)
            pe.wait_ge(p_scaled, u + 1)
            for w in range(2):
                for k in range(2):
                    pe.transpose(bank[4][:, 256 * w + 128 * k:256 * w + 128 * k + 128],
                                 pb[:, 0, 264 * w + 128 * k:264 * w + 128 * k + 128], ident)
                pe.transpose(bank[5][0:NT, 128 * w:128 * w + 128], pb[:, 0, 264 * w + 256:264 * w + 264], ident)
            pe.transpose(bank[5][0:NWIN, 256:384], pb[:, 0, 528:528 + NWIN], ident).then_inc(pt_mm, 1)
            pe.wait_ge(pt_ev, u + 1)
            if s == 0:
                pe.wait_ge(vn_in, 16 * 2 * NB)
            for bb in range(2):
                b = 2 * s + bb
                for g in range(NG):
                    r = slice(64 * bb + 32 * g, 64 * bb + 32 * g + 32)
                    o = bank[5][:, 384 + r.start:384 + r.stop]
                    for w in range(2):
                        for k in range(2):
                            pe.matmul(o, past_rows(s, bb, w, k)[:, 256 + g * HD:256 + g * HD + HD],
                                      pT[:, 0, 256 * w + 128 * k + r.start:256 * w + 128 * k + r.stop],
                                      start=(w == 0 and k == 0), stop=False)
                        pe.matmul(o, vn[0:NT, b, w, g * HD:g * HD + HD],
                                  pT[0:NT, 0, 512 + 128 * w + r.start:512 + 128 * w + r.stop], start=False, stop=False)
                    ins = pe.matmul(o, vc[0:NWIN, 2 * (1 + b) + g, :], pT[0:NWIN, 0, 768 + r.start:768 + r.stop],
                                    start=False, stop=True)
            ins.then_inc(o_mm, 1)
            pe.wait_ge(o_ev, u + 1)
        for i in range(2):
            for j in range(4):
                ins = pe.transpose(bank[i][0:64, 128 * j:128 * j + 128], attT[:, 4 * i + j, :], ident)
            ins.then_inc(attT_mm, 1)

        pe.wait_ge(hn_ready, 2)
        pe.sem_inc(merged, 1)
        transposes(KC, tok_tiles(lambda t, c: (att if c < 8 else bg)[:, t, 128 * (c % 8):128 * (c % 8) + 128]))
        pe.wait_ge(t_ev[0], evs[0])
        pe.wait_ge(t_ev[1], evs[1])
        blocks(N_OUT, 4)

        pe.wait_ge(hn_ready, 3)
        transposes(KC, tok_tiles(lambda t, c: n_tok[:, t, 128 * c:128 * c + 128], (128, 128, 128)))
        pe.wait_ge(t_ev[0], evs[0])
        pe.wait_ge(t_ev[1], evs[1])
        for blk in range(4):
            if blk >= 2:
                pe.wait_ge(qT_done, blk - 1)
            n = N_WQ + blk
            for half in range(2):
                slot = (2 * blk + half) % 4
                pe.wait_ge(w_in[slot], 16 * (n // 2) + 16)
                for sub in range(4):
                    for k in range(8):
                        ins = pe.matmul(bank[4 * (blk % 2) + sub][:, 0:384], ring[slot][:, k, 128 * sub:128 * sub + 128],
                                        xT[:, 8 * half + k, :], start=(half == 0 and k == 0), stop=(half == 1 and k == 7))
                ins.then_inc(w_used, 1)
            pe.wait_ge(w_used, 4 + 2 * (n + 1))
            pe.sem_inc(mm_done, 1)
        pe.wait_ge(qT_done, 4)
        pe.wait_ge(keys_s, 16)
        for a in range(2):
            ins = pe.transpose(bank[0][:, 128 * a:128 * a + 128], keys_in[:, a, :], ident)
        ins.then_inc(keys_mm, 1)
        pe.wait_ge(keys_ev, 1)
        for t in range(3):
            for q in range(4):
                if t == 2:
                    pe.wait_ge(sc_ev, q + 1)
                for j in range(4):
                    c = 4 * q + j
                    ins = pe.matmul(bank[4 * (t % 2) + q][:, 128 * j:128 * j + 128], qT[:, c, 128 * t:128 * t + 128],
                                    keysT[:, c % 2, :], start=True, stop=True)
                ins.then_inc(sc_mm, 1)
        pe.wait_ge(sc_ev, 12)
        pe.wait_ge(p_in_s, 48)
        for c in range(2):
            for t in range(3):
                ins = pe.transpose(bank[c][:, 128 * t:128 * t + ROWS[t]], p_in[0:ROWS[t], t, 128 * c:128 * c + 128],
                                   ident[0:ROWS[t], 0:ROWS[t]])
        ins.then_inc(pleT_mm, 1)
        pe.wait_ge(pleT_ev, 1)

        def weighted_rows(k, par, t, first, last):
            m = 128 if t < 2 else 64
            pe.wait_ge(diag_ready, k + 1)
            for j in range(4):
                pe.wait_ge(v_in[j], (k + 1) * 16)
                for q in range(4):
                    ins = pe.matmul(bank[4 * (t % 2) + q][0:m, :], diag[:, par, j, 0:m], v_row[j][:, 512 * q:512 * q + 512],
                                    start=(first and j == 0), stop=(last and j == 3))
                ins.then_inc(v_used, 1)

        def tile_done(n):
            pe.wait_ge(v_used, 4 * n + 4)
            pe.sem_inc(peer_mm, 1)

        end0, end1 = GROUPS[0], LAST
        weighted_rows(0, 0, 0, True, False)
        with pe.Fori(0, (GROUPS[0] - 2) // 2) as i:
            for jj in range(2):
                weighted_rows(i * 2 + (1 + jj), (1 + jj) % 2, 0, False, False)
        weighted_rows(end0 - 1, 1, 0, False, True)
        tile_done(end0)
        weighted_rows(end0, 0, 1, True, False)
        with pe.Fori(0, (GROUPS[1] - 2) // 2) as i:
            for jj in range(2):
                weighted_rows(i * 2 + (end0 + 1 + jj), (1 + jj) % 2, 1, False, False)
        weighted_rows(end1 - 1, 1, 1, False, True)
        tile_done(end1)

        for i in range(GROUPS[2]):
            if i == 0:
                pe.wait_ge(h_seen, 1)
            weighted_rows(end1 + i, i % 2, 2, i == 0, i == GROUPS[2] - 1)
            if i in (2, 3):
                pe.wait_ge(h_seen, 2)
                if i == 3:
                    pe.wait_ge(hT_ev, 2)
                for j in range(8):
                    c = 8 * (i - 2) + j
                    for t in range(2):
                        ins = pe.transpose(bank[4 + j // 2][:, 256 * (j % 2) + 128 * t:256 * (j % 2) + 128 * t + 128],
                                           h[:, t, 128 * c:128 * c + 128], ident)
                ins.then_inc(hT_mm, 1)
            for q in gate_quarters(i):
                blk, part = divmod(q, 4)
                if part == 0:
                    if blk == 0:
                        pe.wait_ge(hT_ev, 4)
                        pe.wait_ge(ple_in, 16)
                    else:
                        pe.wait_ge(y_ready, blk)
                    for t in range(2):
                        for c in range(2):
                            pe.matmul(bank[6 + t][:, :], pleT[:, c, 128 * t:128 * t + 128], ple_w[:, c, 512 * blk:512 * blk + 512],
                                      start=(c == 0), stop=(c == 1))
                pe.wait_ge(gw_in[q % 3], 16 * (q // 3 + 1))
                for t in range(2):
                    for k in range(4):
                        ins = pe.matmul(bank[4 + t][:, :], hT[:, 4 * part + k, 128 * t:128 * t + 128], gate_w[q % 3][:, k, :],
                                        start=(part == 0 and k == 0), stop=(part == 3 and k == 3))
                ins.then_inc(gw_used, 1)
                if part == 3:
                    pe.wait_ge(gw_used, q + 1)
                    pe.sem_inc(gate_mm, 1)
        tile_done(end1 + GROUPS[2])

        pe.wait_ge(h_ready, 2)
        pe.wait_ge(y_ready, 4)
        transposes(KC, lambda c: [(0, h[0:64, 2, 128 * c:128 * c + 128], 64)])
        pe.wait_ge(t_ev[0], evs[0])
        pe.wait_ge(t_ev[1], evs[1])
        for blk in range(4):
            n = N_GATE + blk
            if blk >= 2:
                pe.wait_ge(ple_mm, blk - 1)
                pe.wait_ge(sig_ready, 4 + blk - 1)
            for c in range(2):
                pe.matmul(bank[2 + blk % 2][0:64, :], pleT[:, c, 256:TOK], ple_w[:, c, 512 * blk:512 * blk + 512],
                          start=(c == 0), stop=(c == 1))
            for half in range(2):
                slot = (2 * blk + half) % 4
                pe.wait_ge(w_in[slot], 16 * (n // 2) + 16)
                for k in range(8):
                    ins = pe.matmul(bank[blk % 2][0:64, :], hT_s[:, 8 * half + k, :], ring[slot][:, k, :],
                                    start=(half == 0 and k == 0), stop=(half == 1 and k == 7))
                ins.then_inc(w_used, 1)
            pe.wait_ge(w_used, 4 + 2 * (n + 1))
            pe.sem_inc(mm_done, 1)

    ctx.close()


_INS = ["x_prompt", "x_sample", "p_prompt", "p_sample", "cache_kv", "state_win", "state_conv", "page_table", "rel_bias",
        "norm1", "w_in", "qk_gain", "cmp_pe", "cmp_w1", "cmp_w2", "conv_w", "conv_b", "out_gain", "w_out", "norm2",
        "peer_wq", "peer_keys", "peer_u", "peer_v", "norm3", "ple_gate", "ple_proj"]
_OUTS = [(1, NP, D), (NB, NT, D), (1, 1, NP, 4, NG, HD), (1, 1, NP, 2, NG, HD), (1, 1, 2, CONV),
         (1, NB, NT, 4, NG, HD), (1, NB, PAST, 2, NG, HD), (1, NB, 2, CONV)]


def kernel(**inputs):
    import concourse.bacc as bacc
    from concourse.bass_utils import run_bass_kernel_spmd

    nc = bacc.Bacc("TRN2", target_bir_lowering=False, num_devices=1)
    arrays, ins = {}, {}
    for name in _INS:
        a = np.ascontiguousarray(inputs[name])
        arrays[f"in_{name}"] = a
        ins[name] = nc.dram_tensor(f"in_{name}", a.shape, mybir.dt.from_np(a.dtype), kind="ExternalInput").ap()
    arrays["in_cst"] = shape_constants()
    ins["cst"] = nc.dram_tensor("in_cst", (128, NCST), mybir.dt.float32, kind="ExternalInput").ap()
    outs = [nc.dram_tensor(f"out_{i}", s, mybir.dt.float32, kind="ExternalOutput").ap() for i, s in enumerate(_OUTS)]
    build(nc, ins, outs)
    r = run_bass_kernel_spmd(nc, [arrays], core_ids=[0])
    return tuple(r.results[0][f"out_{i}"] for i in range(len(_OUTS)))
```

```python
import math
from contextlib import ExitStack

import numpy as np
import concourse.bass as bass
from concourse import mybir

D = 2048
KC = D // 128
NP, NB, NT = 256, 8, 8
PAST, PAGE = 256, 128
HD, NH, NG = 128, 8, 2
HPG = NH // NG
ATT = NH * HD
CONV = D - ATT
KVC = 6 * NG * HD
QKV = ATT + KVC
GATES = 3 * NH
BLK, STRIDE, HID = 32, 16, 256
NWIN = PAST // STRIDE - 1
SEQS = (1 + NB) * NG
PH, PK, NKEY = 8, 16, 128
PLE = 256
EPS, NEG = 1e-6, -1e30
ROWS = (128, 128, NB * NT)
TOK = sum(ROWS)
NBUCKET, MAXDIST = 32, 128
DMAX = PAST + NT - 1
NBIAS = DMAX + 128

C_ID = 0
C_IOTA = C_ID + 128
C_PAIR = C_IOTA + PK * PK
C_SELG = C_PAIR + 64
C_HM = C_SELG + 4 * 128
C_VM = C_HM + GATES
C_OH = C_VM + 1
NCST = C_OH + NBIAS


def shape_constants():
    c = np.zeros((128, NCST), np.float32)
    p = np.arange(128)
    c[:, C_ID:C_ID + 128] = np.eye(128, dtype=np.float32)
    c[:, C_IOTA:C_IOTA + PK * PK] = np.arange(PK * PK) % PK
    c[p, C_PAIR + p % 64] = 1.0
    for s in range(4):
        tok = (2 * s + p // 64) * NT + p % NT
        c[tok, C_SELG + s * 128 + p] = 1.0
    for br in range(3):
        c[p, C_HM + br * NH + (p % 64) // NT] = 1.0
    c[BLK - 1:, C_VM] = 1.0
    dist = DMAX - np.arange(NBIAS)
    n = np.maximum(dist, 0)
    exact = NBUCKET // 2
    nf = np.maximum(n, 1).astype(np.float32)
    large = exact + (np.log(nf / np.float32(exact)) / np.float32(math.log(MAXDIST / exact))
                     * np.float32(NBUCKET - exact)).astype(np.int32)
    bucket = np.where(n < exact, n, np.minimum(large, NBUCKET - 1))
    bucket = np.where(dist >= 0, bucket, NBUCKET)
    c[bucket, C_OH + np.arange(NBIAS)] = 1.0
    return c


def build(nc, I, O):
    fp32, i32, u32 = mybir.dt.float32, mybir.dt.int32, mybir.dt.uint32
    ALU, ACT, AX = mybir.AluOpType, mybir.ActivationFunctionType, mybir.AxisListType
    ctx = ExitStack()
    PITCH = 53200
    arena = ctx.enter_context(nc.sbuf_tensor("arena", [128, PITCH], fp32))
    bank = [ctx.enter_context(nc.psum_tensor(f"bank{i}", [128, 512], fp32)) for i in range(8)]
    bias_dram = nc.dram_tensor("bias_rows", (NH, 128, NBIAS), fp32, kind="Internal").ap()

    def sem(name):
        return ctx.enter_context(nc.semaphore(name))

    def buf(off, *dims):
        n = math.prod(dims)
        assert off + n <= PITCH
        a = arena[:, off:off + n]
        if len(dims) == 1:
            return a
        names = "abcde"[:len(dims)]
        return a.rearrange(f"p ({' '.join(names)}) -> p {' '.join(names)}",
                           **{x: d for x, d in zip(names[1:], dims[1:])})

    def rep(ap, *dims):
        return bass.AP(ap.tensor, ap.offset, [list(ap.ap[0])] + [list(d) for d in dims])

    T0 = 0
    W0 = T0 + KC * 384
    Z0 = W0 + 4 * 8 * 512
    ZC0 = Z0 + 3 * 2560
    X0 = ZC0 + 9 * 1024
    K0 = X0 + 3 * 1024

    xT = buf(T0, KC, 384)
    ring = [buf(W0 + s * 4096, 8, 512) for s in range(4)]
    z = buf(Z0, 3, 2560)
    h = buf(Z0, 3, D)
    n_tok = buf(Z0 + 3 * D, 3, D)
    bg, cu, sh1 = (buf(ZC0 + i * 3072, 3, 1024) for i in range(3))
    sh2 = buf(X0, 3, 1024)
    att = buf(X0, 3, 1024)

    cst = buf(K0, NCST)
    ident = cst[:, C_ID:C_ID + 128]
    gT = buf(K0 + NCST, 4, KC)
    qg = buf(K0 + NCST + 64, 4, HD)
    gate = buf(K0 + NCST + 576, 3, GATES)
    bias_s = buf(K0 + NCST + 648, DMAX + 1)
    bias_p = buf(K0 + NCST + 912, NH, 256)
    g2 = buf(K0 + NCST + 912, D)
    cw = buf(K0 + NCST + 912 + 2048, 4, CONV)
    S0 = K0 + NCST + 912 + 2048 + 4096
    stats = buf(S0, 256)
    tab = buf(S0 + 256, NH)
    bias_row = buf(S0 + 264, NBIAS)
    g24 = buf(S0 + 264, 4, 3, NH)
    gs = buf(S0 + 368, 4, 3)
    pages = buf(S0 + 656, 2 * NB).bitcast(i32)
    w4 = buf(S0 + 672, 2, 4)
    a4 = buf(S0 + 680, 2, 4)
    idx4 = buf(S0 + 688, 2, 4).bitcast(i32)
    diag = buf(S0 + 700, 2, 4, 128)
    vn = buf(K0 + NCST + 912 + 2048, NB, 2, 256)
    qsT = buf(S0 + 1724, NB, NH, NT)

    qkT = buf(W0, 12, TOK)
    w1 = buf(W0 + 5120, BLK, HID)
    page_in = buf(W0, NB, 2, 256)
    hid = buf(W0 + 13312 + 1024, 2, SEQS * NWIN)
    w2 = [buf(W0 + 14880, 2, HD), buf(W0 + 16128, 2, HD)]
    kcT = buf(W0 + 15136, SEQS * NWIN)
    kct = buf(W0 + 15408, 3, HD)
    pe_in = [buf(W0 + 15792, HD), buf(W0 + 16000, HD)]
    pecol = buf(W0 + 15920, 2)
    raw = [buf(T0, SEQS + 1, 256), buf(ZC0 + 3072, SEQS + 1, 256)]
    vc = buf(T0 + 3840, SEQS, HD)

    def past_rows(s, bb, br, a):
        return buf(W0 + 5120 + (((s % 2) * 2 + bb) * 2 + br) * 1024 + a * 512, 512)

    pastT = [buf(ZC0 + 3072 + 2048 * par, 2, 2, 2, 2, HD) for par in range(2)]
    pb = [buf(T0, 544), buf(T0 + 544, 544), buf(W0 + 13312, 544)]
    pT = buf(T0 + 1088, 2, 896)
    attT = buf(T0 + 2880, NH, NB * NT)
    mx, nm, sm, cf = (buf(S0 + 200 + 6 * i, 2, 3) for i in range(4))
    hT_in = buf(Z0 + 3 * D, KC, 384)
    hT_g2 = buf(Z0 + 6 * D, KC, TOK)
    qT = buf(T0, KC, 384)
    keys_in = buf(K0 + NCST + 2960, 2, 128)
    keysT = buf(K0 + NCST + 2960 + 256, 2, 128)
    sv = buf(K0 + NCST + 2960 + 512, 16, PK)
    si = buf(K0 + NCST + 2960 + 768, 16, PK)
    fv = buf(K0 + NCST + 2960 + 1024, PH, PK)
    fi = buf(K0 + NCST + 2960 + 1152, PH, PK)
    fh = buf(K0 + NCST + 2960 + 1280, PH, PK)
    fl = buf(K0 + NCST + 2960 + 1408, PH, PK)
    e0 = buf(K0 + NCST + 2960 + 1536, PH, PK)
    e1 = buf(K0 + NCST + 2960 + 1664, PH, PK)
    wgt = buf(K0 + NCST + 2960 + 1792, 3, 128)
    idx = buf(K0 + NCST + 2960 + 2176, 3, 128).bitcast(i32)
    score = buf(Z0 + 6 * D, 3, D)
    cands = [buf(W0, PH, PK, PK), buf(T0, PH, PK, PK), buf(T0, PH, PK, PK)]
    cuts = [buf(W0 + D, D), buf(T0 + D, D), buf(T0 + D, D)]
    u_row = [buf(W0 + j * D, D) for j in range(4)]
    v_row = [buf(W0 + (4 + j) * D, D) for j in range(4)]
    ple_w = buf(Z0 + 6 * D, 2, D)
    p_in = buf(K0 + NCST + 5520, 3, PLE)
    pleT = buf(K0 + NCST + 6288, 2, TOK)
    sig = buf(K0 + NCST + 912, 2, 512)
    hT = buf(T0, KC, 256)
    hT_s = buf(T0, KC, 64)
    gate_w = [n_tok[:, 0, :], n_tok[:, 1, :], buf(T0 + KC * 256, D)]
    gate_w = [g.rearrange("p (k n) -> p k n", k=4) for g in gate_w]

    x_in, cst_in, small_in, first_in, cw_in, dve_step, hn_ready = map(sem, ("x_in", "cst_in", "small_in", "first_in", "cw_in", "dve_step", "hn_ready"))
    v_ready, root_ready = sem("v_ready"), sem("root_ready")
    t_mm, t_ev = sem("t_mm"), [sem("t_ev_bank6"), sem("t_ev_bank7")]
    bias_mm, bias_sb, bias_out, bias_in = map(sem, ("bias_mm", "bias_sb", "bias_out", "bias_in"))
    w_in = [sem(f"w_in{s}") for s in range(4)]
    w_used, mm_done, mm_ev = map(sem, ("w_used", "mm_done", "mm_ev"))
    u_ready, shift_a, shift_b, out_done = map(sem, ("u_ready", "shift_a", "shift_b", "out_done"))
    qkv_ready, vn_in = sem("qkv_ready"), sem("vn_in")
    w1_in, w2_in, pe_in_s, conv_done, u_out = [sem("w1_in0"), sem("w1_in1")], sem("w2_in"), sem("pe_in"), sem("conv_done"), sem("u_out")
    page_s = [sem(f"page_in{b}") for b in range(NB)]
    cmp_mm, hid_ready, kc_mm, kc_ready, kcT_mm, cmp_done = map(sem, (
        "cmp_mm", "hid_ready", "kc_mm", "kc_ready", "kcT_mm", "cmp_done"))
    s_mm, biased, exp_done, p_scaled, pt_mm, pt_ev, o_mm, o_ev = map(sem, (
        "s_mm", "biased", "exp_done", "p_scaled", "pt_mm", "pt_ev", "o_mm", "o_ev"))
    past_k, past_v = [sem("past_k0"), sem("past_k1")], [sem("past_v0"), sem("past_v1")]
    gs_mm = sem("gs_mm")
    attT_mm, attT_ev = sem("attT_mm"), sem("attT_ev")
    merged, g2_in, n1_ready, n2_ready = sem("merged"), sem("g2_in"), sem("n1_ready"), sem("n2_ready")
    hT_raw, hT_scaled = sem("hT_raw"), sem("hT_scaled")
    h_ready = sem("h_ready")
    keys_s, keys_mm, keys_ev, sc_mm, sc_ev, qT_done = map(sem, ("keys_in", "keys_mm", "keys_ev", "sc_mm", "sc_ev", "qT_done"))
    e_in, e_out, idx_ready = sem("e_in"), sem("e_out"), sem("idx_ready")
    idx_set, u_used, v_used = sem("idx_set"), sem("u_used"), sem("v_used")
    u_in = [sem(f"u_in{j}") for j in range(4)]
    v_in = [sem(f"v_in{j}") for j in range(4)]
    dots, gelu_done, diag_ready, peer_mm = map(sem, ("dots", "gelu_done", "diag_ready", "peer_mm"))
    ple_in, pleT_mm, pleT_ev, ple_mm, sig_ready, y_ready = map(sem, ("ple_in", "pleT_mm", "pleT_ev", "ple_mm", "sig_ready", "y_ready"))
    loop_step, slot_seen = sem("loop_step"), sem("slot_seen")
    h_seen = sem("h_seen")
    gw_in = [sem(f"gate_w_in{j}") for j in range(3)]
    gw_used, p_in_s, hT_mm, hT_ev, gate_mm = map(sem, ("gate_w_used", "p_in", "hT_mm", "hT_ev", "gate_mm"))

    N_OUT, N_WQ, N_GATE = 12, 16, 20
    W1_CUT = (8192 - 5120) // HID
    w_in_cols = [QKV + GATES + 512 * i for i in range(6)] + [512 * i for i in range(5)] + [QKV]
    TBLOCKS = [HD * i for i in range(NH)] + [1536, 1664, 2048, 2176]
    GROUPS = (PH * PK // 4, PH * PK // 4, PH * PK // 8)
    LAST = GROUPS[0] + GROUPS[1]
    PICKING = 20

    def gate_quarters(i):
        if i < 3 or i == 15:
            return []
        b, j = divmod(i - 3, 3)
        return [4 * b + q for q in ((0,), (1,), (2, 3))[j]]

    w_view = {
        "in": I["w_in"][0].rearrange("(k p) n -> p k n", p=128),
        "out": I["w_out"][0].rearrange("(k p) n -> p k n", p=128),
        "wq": I["peer_wq"][0].rearrange("(k p) n -> p k n", p=128),
        "gate": I["ple_gate"][0].rearrange("(k p) n -> p k n", p=128),
    }
    xp = I["x_prompt"][0].rearrange("(t p) d -> t p d", p=128)
    xs = I["x_sample"].rearrange("b t d -> (b t) d")
    cache = I["cache_kv"][0].rearrange("n p s g d -> n p (s g d)")
    swin = I["state_win"][0].rearrange("b (a p) s g d -> b p a (s g d)", p=128)
    kv_p = O[2][0].rearrange("b (t p) s g d -> (b t) p (s g d)", p=128)
    win_p = O[3][0].rearrange("b (t p) s g d -> (b t) p (s g d)", p=128)
    kv_s = O[5][0].rearrange("b t s g d -> (b t) (s g d)")
    win_s = O[6][0].rearrange("b t s g d -> b t (s g d)")

    block = ctx.enter_context(nc.Block())

    @block.sync
    def _(sp):
        def tiles_of(src_p, src_s, dst, s):
            for t in range(2):
                sp.dma_start(dst[:, t, :], src_p[t]).then_inc(s, 16)
            sp.dma_start(dst[0:64, 2, :], src_s).then_inc(s, 16)

        sp.dma_start(cst, I["cst"]).then_inc(cst_in, 16)
        tiles_of(xp, xs, h, x_in)
        def channel_gain(i, name, s):
            with nc.allow_non_contiguous_dma(reason="a gain by channel"):
                sp.dma_start(gT[:, i, :], I[name][0].rearrange("(k p) -> p k", p=128)).then_inc(s, 16)

        def fill(f, src, n=512):
            sp.wait_ge(w_used, f + 1)
            sp.dma_start(ring[f % 4][:, :, 0:n], src).then_inc(w_in[f % 4], 16)

        def fill_z(blk):
            c0, n = w_in_cols[blk], GATES if blk == 11 else 512
            for half in range(2):
                fill(2 * blk + half, w_view["in"][:, 8 * half:8 * half + 8, c0:c0 + n], n)

        channel_gain(0, "norm1", first_in)
        sp.dma_start(tab[0:NBUCKET, :], I["rel_bias"]).then_inc(first_in, 16)
        for blk in range(2):
            fill_z(blk)
        for i, name in ((1, "norm2"), (2, "norm3"), (3, "out_gain")):
            channel_gain(i, name, small_in)
        sp.dma_start(pages[0:1, :], I["page_table"].rearrange("(o b) n -> o (b n)", o=1)).then_inc(small_in, 16)
        sp.dma_start(qg, bass.AP(I["qk_gain"].tensor, 0, [[0, 128], [HD, 4], [1, HD]])).then_inc(small_in, 16)
        sp.dma_start(cw[:, 0:3, :], bass.AP(I["conv_w"].tensor, 0, [[0, 128], [CONV, 3], [1, CONV]])).then_inc(cw_in, 16)
        sp.dma_start(cw[:, 3, :], bass.AP(I["conv_b"].tensor, 0, [[0, 128], [1, CONV]])).then_inc(cw_in, 16)

        for blk in range(2, 12):
            fill_z(blk)
        sp.dma_start(win_s[:, 0:PAST - NT, :], I["state_win"][0].rearrange("b t s g d -> b t (s g d)")[:, NT:, :])\
          .then_inc(out_done, 16)

        sp.wait_ge(bias_sb, 1)
        sp.dma_start(bias_dram, rep(bias_row[0:NH, :], [0, 128], [1, NBIAS])).then_inc(bias_out, 16)
        sp.wait_ge(bias_out, 16)
        bt = bias_dram.tensor
        sp.dma_start(bias_p, bass.AP(bt, DMAX - 128, [[NBIAS - 1, 128], [128 * NBIAS, NH], [1, 256]])).then_inc(bias_in, 16)
        for r in range(2 * NH):
            sp.dma_start(bias_s[NT * r:NT * r + NT, :],
                         bass.AP(bt, (r % NH) * 128 * NBIAS + DMAX - PAST, [[NBIAS - 1, NT], [1, DMAX + 1]])).then_inc(bias_in, 16)

        sp.wait_ge(u_ready, 1)
        sp.dma_start(O[4][0, 0], cu[126:128, 1, :]).then_inc(u_out, 16)
        for w in range(2):
            sp.dma_start(O[7][0][:, w, :], cu[NT - 2 + w:64:NT, 2, :]).then_inc(u_out, 16)
        for d, dst in ((1, sh1), (2, sh2)):
            for t in range(3):
                sp.dma_start(dst[d:ROWS[t], t, :], cu[0:ROWS[t] - d, t, :]).then_inc(shift_a, 16)
            sp.dma_start(dst[0:d, 1, :], cu[128 - d:128, 0, :]).then_inc(shift_a, 16)
        sp.wait_ge(shift_a, 8 * 16)
        sc = I["state_conv"][0]
        sp.dma_start(sh1[0:64:NT, 2, :], sc[:, 1, :]).then_inc(shift_b, 16)
        sp.dma_start(sh2[0:64:NT, 2, :], sc[:, 0, :]).then_inc(shift_b, 16)
        sp.dma_start(sh2[1:64:NT, 2, :], sc[:, 1, :]).then_inc(shift_b, 16)

        def page(b, a):
            return sp.value_load(pages[0:1, 2 * b + a:2 * b + a + 1], min_val=0, max_val=I["cache_kv"].shape[1] - 1)

        def page_rows(kind, b):
            for a in range(2):
                sp.dma_start(page_in[:, b, a, :],
                             cache[bass.ds(page(b, a), 1), :, 256 * kind:256 * kind + 256]
                             .rearrange("o p n -> p (o n)")).then_inc(page_s[b], 16)

        def compress_weights(kind, part):
            rows = slice(0, W1_CUT) if part == 0 else slice(W1_CUT, BLK)
            sp.dma_start(w1[:, rows, :], I["cmp_w1"][0, kind].rearrange("(m d) h -> d m h", d=HD)[:, rows, :])\
              .then_inc(w1_in[part], 16)

        sp.wait_ge(small_in, 16 * 5)
        sp.wait_ge(mm_done, 11)
        for b in range(NB):
            page_rows(0, b)
        compress_weights(0, 0)
        sp.wait_ge(mm_done, 12)
        compress_weights(0, 1)
        for kind in range(2):
            sp.dma_start(w2[kind], I["cmp_w2"][0, kind].rearrange("(a p) h -> p a h", p=128)).then_inc(w2_in, 16)
            sp.dma_start(pe_in[kind][0:BLK, :], I["cmp_pe"][0, kind]).then_inc(pe_in_s, 16)
        for b in range(NB):
            sp.wait_ge(t_mm, KC + 1 + b + 1)
            page_rows(1, b)
        sp.wait_ge(cmp_mm, 2)
        compress_weights(1, 0)
        compress_weights(1, 1)

        sp.wait_ge(qkv_ready, 1)
        for t in range(2):
            sp.dma_start(kv_p[t], z[:, t, 1024:2048]).then_inc(out_done, 16)
            sp.dma_start(win_p[t], z[:, t, 2048:2560]).then_inc(out_done, 16)
        sp.dma_start(kv_s, z[0:64, 2, 1024:2048]).then_inc(out_done, 16)
        for b in range(NB):
            sp.dma_start(win_s[b, PAST - NT:PAST, :], z[b * NT:b * NT + NT, 2, 2048:2560]).then_inc(out_done, 16)
            for i, c0 in enumerate((1792, 2304)):
                sp.dma_start(vn[0:NT, b, i, :], z[b * NT:b * NT + NT, 2, c0:c0 + 256]).then_inc(vn_in, 16)

        sp.wait_ge(cmp_mm, 4)
        for s in range(NB // 2):
            for kv in range(2):
                if s >= 2:
                    sp.wait_ge((s_mm, o_mm)[kv], 16 + s - 1)
                for bb in range(2):
                    b = 2 * s + bb
                    for a in range(2):
                        sp.dma_start(past_rows(s, bb, 0, a)[:, 256 * kv:256 * kv + 256],
                                     cache[bass.ds(page(b, a), 1), :, 512 + 256 * kv:768 + 256 * kv]
                                     .rearrange("o p n -> p (o n)")).then_inc((past_k, past_v)[kv][s % 2], 16)
                    sp.dma_start(buf(W0 + 5120 + (((s % 2) * 2 + bb) * 2 + 1) * 1024, 2, 512)[:, :, 256 * kv:256 * kv + 256],
                                 swin[b][:, :, 256 * kv:256 * kv + 256]).then_inc((past_k, past_v)[kv][s % 2], 16)

        sp.wait_ge(merged, 1)
        tiles_of(xp, xs, h, x_in)
        for blk in range(4):
            for half in range(2):
                fill(2 * (N_OUT + blk) + half, w_view["out"][:, 8 * half:8 * half + 8, 512 * blk:512 * blk + 512])
        sp.dma_start(g2, bass.AP(I["norm2"].tensor, 0, [[0, 128], [1, D]])).then_inc(g2_in, 16)
        sp.dma_start(keys_in, I["peer_keys"][0].rearrange("a n k -> n a k")).then_inc(keys_s, 16)
        for blk in range(4):
            for half in range(2):
                fill(2 * (N_WQ + blk) + half, w_view["wq"][:, 8 * half:8 * half + 8, 512 * blk:512 * blk + 512])
        tiles_of(I["p_prompt"][0, 0].rearrange("(t p) d -> t p d", p=128),
                 I["p_sample"][0].rearrange("b t d -> (b t) d"), p_in, p_in_s)
        sp.wait_ge(idx_ready, 3)
        sp.dma_start(ple_w, I["ple_proj"][0].rearrange("(k p) n -> p k n", p=128)).then_inc(ple_in, 16)
        sp.wait_ge(u_used, 4 + 4 * LAST)
        yp = O[0][0].rearrange("(t p) d -> t p d", p=128)
        ys = O[1].rearrange("b t d -> (b t) d")

        def y_out(b):
            sp.wait_ge(y_ready, b + 1)
            cols = slice(512 * b, 512 * b + 512)
            for t in range(2):
                sp.dma_start(yp[t][:, cols], h[:, t, cols]).then_inc(out_done, 16)

        for q in range(16):
            if q >= 3:
                sp.wait_ge(gw_used, q - 2)
            sp.dma_start(gate_w[q % 3], w_view["gate"][:, 4 * (q % 4):4 * (q % 4) + 4, 512 * (q // 4):512 * (q // 4) + 512])\
              .then_inc(gw_in[q % 3], 16)
            if q >= 8 and q % 4 == 0:
                y_out(q // 4 - 2)
        y_out(2)
        for blk in range(4):
            if blk == 0:
                sp.wait_ge(u_used, 4 + 4 * (LAST + GROUPS[2]))
            elif blk == 1:
                sp.wait_ge(v_used, 4 + 4 * (LAST + GROUPS[2]))
            for half in range(2):
                fill(2 * (N_GATE + blk) + half, w_view["gate"][:, 8 * half:8 * half + 8, 512 * blk:512 * blk + 512])
        y_out(3)
        for blk in range(4):
            sp.wait_ge(y_ready, 4 + blk + 1)
            cols = slice(512 * blk, 512 * blk + 512)
            sp.dma_start(ys[:, cols], h[0:64, 2, cols]).then_inc(out_done, 16)
        sp.wait_ge(u_out, 16 * 3)
        sp.wait_ge(out_done, 16 * (1 + 5 + NB + 12))

    @block.gpsimd
    def _(pool):
        def gathers(k, par):
            pool.wait_ge(idx_set, k + 1)
            for j in range(4):
                pool.wait_ge(u_used, 4 * k + j + 1)
                pool.sem_inc(slot_seen, 1)
                pool.indirect_dma_start(u_row[j], None, I["peer_u"][0],
                                        bass.IndirectOffsetOnAxis(idx4[:, par, j:j + 1], 0)).then_inc(u_in[j], 16)
            for j in range(4):
                pool.wait_ge(v_used, 4 * k + j + 1)
                pool.sem_inc(slot_seen, 1)
                pool.indirect_dma_start(v_row[j], None, I["peer_v"][0],
                                        bass.IndirectOffsetOnAxis(idx4[:, par, j:j + 1], 0)).then_inc(v_in[j], 16)

        with pool.Fori(0, sum(GROUPS) // 2) as i:
            for par in range(2):
                gathers(i * 2 + par, par)

    @block.scalar
    def _(act):
        act.sem_inc(mm_ev, 2)
        roots = [0]

        def root(src, dst):
            roots[0] += 1
            act.wait_ge(v_ready, roots[0])
            act.activation(dst, src, ACT.Sqrt).then_inc(root_ready, 1)

        tcount = [0]

        def odd_transposes(n, put):
            for c in range(1, n, 2):
                act.wait_ge(t_mm, tcount[0] + c + 1)
                put(act, c).then_inc(t_ev[1], 1)
            tcount[0] += n

        act.wait_ge(first_in, 32)
        odd_transposes(KC, lambda e, c: e.activation(xT[:, c, 0:TOK], bank[7][:, 0:TOK], ACT.Copy, scale=gT[:, 0, c:c + 1]))

        root(stats[:, 0:3], stats[:, 3:6])
        act.wait_ge(n1_ready, 1)

        def z_out(n, wait, dst):
            act.wait_ge(mm_done, wait)
            for t in range(3):
                ins = act.activation(dst(t), bank[3 * (n % 2) + t][0:ROWS[t], :], ACT.Copy, scale=stats[0:ROWS[t], 3 + t:4 + t])
            ins.then_inc(mm_ev, 1)

        for part, region in enumerate((bg, cu, sh1)):
            for j in range(2):
                z_out(j, 2 * part + j + 1, lambda t: region[0:ROWS[t], t, 512 * j:512 * j + 512])
        with act.Fori(0, 2) as i:
            for j in range(2):
                z_out(j, i * 2 + 6 + j + 1, lambda t: z[0:ROWS[t], t, bass.ds(i * 1024 + 512 * j, 512)])
        z_out(10, 11, lambda t: z[0:ROWS[t], t, 2048:2560])
        act.wait_ge(mm_done, 12)
        for t in range(3):
            ins = act.activation(gate[0:ROWS[t], t, :], bank[3 + t][0:ROWS[t], 0:GATES], ACT.Sigmoid,
                                 scale=stats[0:ROWS[t], 3 + t:4 + t])
        ins.then_inc(mm_ev, 1)

        def raw_out(kind):
            for c in range(NB + 2):
                act.wait_ge(t_mm, tcount[0] + c + 1)
                src = bank[6 + c % 2]
                if c == 0:
                    ins = act.activation(raw[kind][:, 0:NG, :], src[:, :].rearrange("p (g x) -> p g x", g=2), ACT.Copy)
                elif c <= NB:
                    ins = act.activation(raw[kind][:, 2 * c:2 * c + 2, :].rearrange("p g (a x) -> p a g x", a=2),
                                         src[:, :].rearrange("p (a g x) -> p a g x", a=2, g=2), ACT.Copy)
                else:
                    ins = act.activation(raw[kind][:, SEQS, 0:BLK], src[:, 0:BLK], ACT.Copy)
                ins.then_inc(t_ev[c % 2], 1)
            tcount[0] += NB + 2

        def hidden(kind):
            for hb in range(2):
                act.wait_ge(cmp_mm, 2 * kind + hb + 1)
                act.activation(pecol[:, hb:hb + 1], bank[hb][:, SEQS * NWIN:SEQS * NWIN + 1], ACT.Copy).then_inc(e_out, 1)
                act.wait_ge(e_out, 2 * kind + hb + 1)
                act.activation(hid[:, hb, :], bank[hb][:, 0:SEQS * NWIN], ACT.Gelu_apprx_tanh,
                               bias=pecol[:, hb:hb + 1]).then_inc(hid_ready, 1)

        def heads_out(e, c):
            ins = e.activation(qkT[:, c, :], bank[7][:, 0:TOK], ACT.Copy)
            if c < NH:
                ins = e.activation(qsT[:, :, c, :], bank[7][:, 256:TOK].rearrange("p (b t) -> p b t", b=NB), ACT.Copy)
            return ins

        raw_out(0)
        root(stats[:, 36:72], stats[:, 72:108])
        hidden(0)
        act.wait_ge(conv_done, 1)
        act.wait_ge(u_out, 16 * 3)
        raw_out(1)
        odd_transposes(12, heads_out)
        root(stats[:, 108:111], stats[:, 111:114])
        root(stats[:, 123:126], stats[:, 129:132])
        hidden(1)
        act.wait_ge(kcT_mm, 1)
        act.activation(kcT, bank[3][:, 0:SEQS * NWIN], ACT.Copy).then_inc(cmp_done, 1)
        for q in range(5):
            act.wait_ge(kc_mm, 2 + q)
            n = min(4, SEQS - 4 * q)
            act.activation(vc[0:NWIN, 4 * q:4 * q + n, :],
                           bank[(2, 4, 5, 6, 0)[q]][0:NWIN, 0:n * HD].rearrange("p (a b) -> p a b", a=n), ACT.Copy)\
               .then_inc(cmp_done, 1)

        def softmax_exp(u, rows_list, par):
            act.wait_ge(biased, u + 1)
            for br, ap in rows_list:
                ins = act.activation(ap, ap, ACT.Exp, bias=nm[:, par, br:br + 1], accum_out=sm[:, par, br:br + 1])
            ins.then_inc(exp_done, 1)

        def prompt_pt(u):
            t = u // NH
            act.wait_ge(pt_mm, u + 1)
            if t:
                act.activation(pT[:, u % 2, 0:512], bank[4 + u % 2][:, :], ACT.Copy)
            else:
                act.activation(pT[:, u % 2, 0:512].rearrange("p (a b) -> p a b", a=2)[:, :, 0:128],
                               bank[4 + u % 2][:, :].rearrange("p (a b) -> p a b", a=2)[:, :, 0:128], ACT.Copy)
            nc_ = NWIN if t else 7
            act.activation(pT[0:nc_, u % 2, 512:640], bank[6 + u % 2][0:nc_, 128:256], ACT.Copy).then_inc(pt_ev, 1)

        def prompt_o(u):
            t, hh = u // NH, u % NH
            act.wait_ge(o_mm, u + 1)
            act.activation(att[:, t, hh * HD:hh * HD + HD], bank[6 + u % 2][:, 0:HD], ACT.Copy).then_inc(o_ev, 1)

        def prompt_rows(u):
            t = u // NH
            nk = 128 * (t + 1)
            p = pb[u % 3]
            return [(0, p[:, 512:512 + (NWIN if t else 7)]), (1, p[:, 0:nk]), (2, p[:, 256:256 + nk])]

        for u in range(17):
            if u < 16:
                softmax_exp(u, prompt_rows(u), u % 2)
            if u:
                prompt_pt(u - 1)
            if u > 1:
                prompt_o(u - 2)
        prompt_o(15)

        def sample_keys(s):
            odd_transposes(4, lambda e, c: e.activation(
                pastT[s % 2][:, c // 2, c % 2].rearrange("p a b d -> p (a b d)"), bank[7][:, :], ACT.Copy))

        def sample_exp(s):
            p = pb[s % 2]
            softmax_exp(16 + s, [(0, p[:, 528:528 + NWIN]), (1, p[:, 0:264]), (2, p[:, 264:528])], s % 2)

        def sample_pt(s):
            act.wait_ge(pt_mm, 16 + s + 1)
            act.activation(pT[:, 0, 0:512], bank[4][:, :], ACT.Copy)
            act.activation(pT[0:NT, 0, 512:768], bank[5][0:NT, 0:256], ACT.Copy)
            act.activation(pT[0:NWIN, 0, 768:896], bank[5][0:NWIN, 256:384], ACT.Copy).then_inc(pt_ev, 1)

        def sample_o(s):
            act.wait_ge(o_mm, 16 + s + 1)
            for bb in range(2):
                ins = act.activation(attT[:, :, (2 * s + bb) * NT:(2 * s + bb) * NT + NT],
                                     bank[5][:, 384 + 64 * bb:448 + 64 * bb].rearrange("p (h t) -> p h t", h=NH), ACT.Copy)
            ins.then_inc(o_ev, 1)

        sample_keys(0)
        sample_exp(0)
        sample_keys(1)
        for s in range(4):
            sample_pt(s)
            if s < 3:
                sample_exp(s + 1)
            sample_o(s)
            if s < 2:
                sample_keys(s + 2)
        for i in range(2):
            act.wait_ge(attT_mm, i + 1)
            act.activation(att[0:64, 2, 512 * i:512 * i + 512], bank[i][0:64, :], ACT.Copy).then_inc(attT_ev, 1)
        root(stats[:, 120:123], stats[:, 126:129])
        act.wait_ge(small_in, 16 * 5)
        odd_transposes(KC, lambda e, c: e.activation(xT[:, c, 0:TOK], bank[7][:, 0:TOK], ACT.Copy, scale=gT[:, 3, c:c + 1]))

        def doubled_out(dst, src):
            act.activation(dst[:, 0:TOK], src[:, 0:TOK], ACT.Copy)
            return act.activation(dst[:, TOK:384], src[:, 256:TOK], ACT.Copy)

        for blk in range(4):
            act.wait_ge(mm_done, N_OUT + blk + 1)
            for sub in range(4):
                doubled_out(hT_in[:, 4 * blk + sub, :], bank[4 * (blk % 2) + sub]).then_inc(hT_raw, 1)

        for blk in range(4):
            act.wait_ge(mm_done, N_WQ + blk + 1)
            for sub in range(4):
                ins = doubled_out(qT[:, 4 * blk + sub, :], bank[4 * (blk % 2) + sub])
            ins.then_inc(qT_done, 1)
            if blk == 0:
                odd_transposes(12, lambda e, c: e.activation(h[:, c // 4, 512 * (c % 4):512 * (c % 4) + 512], bank[7][:, :], ACT.Copy))
            if blk == 1:
                root(stats[:, 136:139], stats[:, 139:142])
        act.wait_ge(keys_mm, 1)
        act.activation(keysT, bank[0][:, 0:256].rearrange("p (a b) -> p a b", a=2), ACT.Copy).then_inc(keys_ev, 1)
        act.wait_ge(n2_ready, 1)
        for t in range(3):
            for q in range(4):
                act.wait_ge(sc_mm, 4 * t + q + 1)
                act.activation(score[:, t, 512 * q:512 * q + 512], bank[4 * (t % 2) + q][:, :], ACT.Copy,
                               scale=stats[:, 139 + t:140 + t]).then_inc(sc_ev, 1)
        act.wait_ge(pleT_mm, 1)
        for c in range(2):
            ins = act.activation(pleT[:, c, :], bank[c][:, 0:TOK], ACT.Copy)
        ins.then_inc(pleT_ev, 1)

        def pick_exp(t):
            act.wait_ge(e_in, t + 1)
            act.activation(fv, fv, ACT.Exp).then_inc(e_out, 1)

        def gate_sigmoid(b):
            act.wait_ge(gate_mm, b + 1)
            if b:
                act.wait_ge(y_ready, b)
            for t in range(2):
                ins = act.activation(sig[:, t, :], bank[4 + t][:, :], ACT.Sigmoid, scale=stats[:, 147 + t:148 + t])
            ins.then_inc(sig_ready, 1)

        def gelu(k, par):
            act.wait_ge(dots, k + 1)
            act.activation(w4[:, par, :], a4[:, par, :], ACT.Gelu_apprx_tanh).then_inc(gelu_done, 1)

        pick_exp(0)
        for i in range(PICKING):
            if i == 10:
                pick_exp(1)
            if i == 19:
                pick_exp(2)
            gelu(i, i % 2)
        with act.Fori(0, (GROUPS[0] - PICKING) // 2) as i:
            for jj in range(2):
                gelu(i * 2 + (PICKING + jj), jj)
        with act.Fori(0, GROUPS[1] // 2) as i:
            for jj in range(2):
                gelu(i * 2 + (GROUPS[0] + jj), jj)
        for i in range(GROUPS[2]):
            if i == 2:
                root(stats[:, 144:146], stats[:, 147:149])
            if i in (2, 3):
                act.wait_ge(hT_mm, i - 1)
                for j in range(4):
                    c = 8 * (i - 2) + 4 + j
                    ins = act.activation(hT[:, c, :], bank[6 + j // 2][:, 256 * (j % 2):256 * (j % 2) + 256], ACT.Copy,
                                         scale=gT[:, 2, c:c + 1])
                ins.then_inc(hT_ev, 1)
            if i in (6, 9, 12):
                gate_sigmoid((i - 6) // 3)
            gelu(LAST + i, i % 2)
        gate_sigmoid(3)
        odd_transposes(KC, lambda e, c: e.activation(hT_s[:, c, :], bank[7][:, 0:64], ACT.Copy, scale=gT[:, 2, c:c + 1]))
        root(stats[:, 146:147], stats[:, 149:150])
        act.wait_ge(h_ready, 1)
        for blk in range(4):
            act.wait_ge(mm_done, N_GATE + blk + 1)
            if blk >= 2:
                act.wait_ge(y_ready, 4 + blk - 1)
            act.activation(sig[0:64, blk % 2, :], bank[blk % 2][0:64, :], ACT.Sigmoid, scale=stats[0:64, 149:150])\
               .then_inc(sig_ready, 1)

    @block.vector
    def _(dve):
        steps = [0]

        def step(ins):
            steps[0] += 1
            ins.then_inc(dve_step, 1)
            dve.wait_ge(dve_step, steps[0])

        roots = [0]

        def inv_rms(ss, v, y, t, width):
            step(dve.tensor_scalar(v, ss, 1.0 / width, EPS, ALU.mult, ALU.add))
            dve.sem_inc(v_ready, 1)
            roots[0] += 1
            dve.wait_ge(root_ready, roots[0])
            step(dve.reciprocal(y, y))
            step(dve.tensor_tensor(t, y, y, ALU.mult))
            step(dve.tensor_tensor(t, t, v, ALU.mult))
            step(dve.tensor_scalar(t, t, -0.5, 1.5, ALU.mult, ALU.add))
            step(dve.tensor_tensor(y, y, t, ALU.mult))

        tcount = [0]

        evens, odds = [0], [0]

        def even_transposes(n, put):
            evens[0] += (n + 1) // 2
            odds[0] += n // 2
            for c in range(0, n, 2):
                dve.wait_ge(t_mm, tcount[0] + c + 1)
                put(dve, c).then_inc(t_ev[0], 1)
            tcount[0] += n

        def squares(src, junk, acc):
            return dve.tensor_tensor_reduce(out=junk, in0=src, in1=src, scale=1.0, scalar=0.0,
                                            op0=ALU.mult, op1=ALU.add, accum_out=acc)

        step(dve.memset(stats, 1.0))
        step(dve.memset(tab[NBUCKET:NBUCKET + 1, :], NEG))
        dve.wait_ge(bias_mm, 1)
        dve.tensor_copy(bias_row[0:NH, :], bank[0][0:NH, 0:NBIAS]).then_inc(bias_sb, 1)
        dve.wait_ge(first_in, 32)
        even_transposes(KC, lambda e, c: e.tensor_scalar(xT[:, c, 0:TOK], bank[6][:, 0:TOK], gT[:, 0, c:c + 1], None, ALU.mult))
        dve.wait_ge(x_in, 48)
        for t in range(3):
            ins = squares(h[0:ROWS[t], t, :], n_tok[0:ROWS[t], t, :], stats[0:ROWS[t], t:t + 1])
        step(ins)
        inv_rms(stats[:, 0:3], stats[:, 0:3], stats[:, 3:6], stats[:, 6:9], D)
        dve.sem_inc(n1_ready, 1)

        dve.wait_ge(mm_ev, 2 + 6)
        for t in range(3):
            r = ROWS[t]
            ins = dve.tensor_tensor(cu[0:r, t, :], cu[0:r, t, :], sh1[0:r, t, :], ALU.mult)
        step(ins)
        dve.memset(sh2[0:2, 0, :], 0.0)
        step(dve.memset(sh1[0:1, 0, :], 0.0))
        dve.sem_inc(u_ready, 1)
        dve.wait_ge(shift_a, 8 * 16)
        dve.wait_ge(shift_b, 3 * 16)
        dve.wait_ge(cw_in, 32)
        for op in range(7):
            for t in range(3):
                r = ROWS[t]
                a, b, c, g = sh1[0:r, t, :], sh2[0:r, t, :], cu[0:r, t, :], bg[0:r, t, :]
                out, x, y, alu = ((a, a, cw[0:r, 1, :], ALU.mult), (b, b, cw[0:r, 0, :], ALU.mult), (a, a, b, ALU.add),
                                  (b, c, cw[0:r, 2, :], ALU.mult), (a, a, b, ALU.add), (a, a, cw[0:r, 3, :], ALU.add),
                                  (g, g, a, ALU.mult))[op]
                ins = dve.tensor_tensor(out, x, y, alu)
            step(ins)
        for t in range(3):
            r = ROWS[t]
            ins = squares(bg[0:r, t, :], sh1[0:r, t, :], stats[0:r, 123 + t:124 + t])
        step(ins)
        dve.sem_inc(conv_done, 1)

        dve.wait_ge(small_in, 16 * 5)
        dve.wait_ge(mm_ev, 2 + 12)
        HEADS = ((0, 8, 0, 0), (1536, 2, 8, 2), (2048, 2, 10, 3))
        for t in range(3):
            r = ROWS[t]
            for c0, nh, s0, _ in HEADS:
                v = z[0:r, t, c0:c0 + nh * HD]
                step(dve.tensor_tensor(sh2[0:r, t, 0:nh * HD], v, v, ALU.mult))
                step(dve.tensor_reduce(stats[0:r, 36 + 12 * t + s0:36 + 12 * t + s0 + nh],
                                       sh2[0:r, t, 0:nh * HD].rearrange("p (n d) -> p n d", d=HD), AX.X, ALU.add))
        inv_rms(stats[:, 36:72], stats[:, 36:72], stats[:, 72:108], stats[:, 160:196], HD)
        qs = stats[:, 72:108].rearrange("p (t n) -> p t n", t=3)[:, :, 0:NH]
        step(dve.tensor_scalar(qs, qs, HD ** -0.5, None, ALU.mult))
        for t in range(3):
            r = ROWS[t]
            for c0, nh, s0, gi in HEADS:
                for n in range(nh):
                    v = z[0:r, t, c0 + n * HD:c0 + n * HD + HD]
                    k = 72 + 12 * t + s0 + n
                    ins = dve.scalar_tensor_tensor(out=v, in0=v, scalar=stats[0:r, k:k + 1], in1=qg[0:r, gi, :],
                                                   op0=ALU.mult, op1=ALU.mult)
        step(ins)
        dve.sem_inc(qkv_ready, 1)

        def heads_out(e, c):
            ins = e.tensor_copy(qkT[:, c, :], bank[6][:, 0:TOK])
            if c < NH:
                ins = e.tensor_copy(qsT[:, :, c, :], bank[6][:, 256:TOK].rearrange("p (b t) -> p b t", b=NB))
            return ins
        tcount[0] += 2 * (NB + 2)
        evens[0] += NB + 2
        odds[0] += NB + 2
        even_transposes(12, heads_out)

        dve.wait_ge(kc_mm, 1)
        for i in range(3):
            ins = dve.tensor_copy(kct[0:90, i, :], bank[2][0:90, i * HD:i * HD + HD])
        step(ins)
        for i in range(3):
            ins = squares(kct[0:90, i, :], buf(Z0 + 8 * D, HD)[0:90, :], stats[0:90, 108 + i:109 + i])
            step(ins)
        inv_rms(stats[:, 108:111], stats[:, 108:111], stats[:, 111:114], stats[:, 114:117], HD)
        for i in range(3):
            ins = dve.scalar_tensor_tensor(out=kct[0:90, i, :], in0=kct[0:90, i, :], scalar=stats[0:90, 111 + i:112 + i],
                                           in1=qg[0:90, 1, :], op0=ALU.mult, op1=ALU.mult)
        ins.then_inc(kc_ready, 1)
        inv_rms(stats[:, 123:126], stats[:, 123:126], stats[:, 129:132], stats[:, 160:163], CONV)
        for t in range(3):
            r = ROWS[t]
            ins = dve.tensor_scalar(bg[0:r, t, :], bg[0:r, t, :], stats[0:r, 129 + t:130 + t], None, ALU.mult)
        step(ins)
        dve.wait_ge(gs_mm, 1)
        step(dve.tensor_tensor(g24, bank[1][:, 0:96].rearrange("p (s c h) -> p s c h", s=4, c=3),
                               rep(cst[:, C_HM:], [0, 4], [NH, 3], [1, NH]), ALU.mult))
        dve.sem_inc(cmp_done, 1)
        step(dve.tensor_reduce(gs, g24, AX.X, ALU.add))

        def bias_max(u, par, parts):
            dve.wait_ge(s_mm, u + 1)
            for br, out, src, bias in parts:
                ins = dve.tensor_tensor_reduce(out=out, in0=src, in1=bias, scale=1.0, scalar=-3.0e38,
                                               op0=ALU.add, op1=ALU.max, accum_out=mx[:, par, br:br + 1])
            step(ins)
            step(dve.tensor_scalar(nm[:, par, :], mx[:, par, :], -1.0, None, ALU.mult))
            dve.sem_inc(biased, 1)

        def weigh(u, par, parts, gates_, mask):
            dve.wait_ge(exp_done, u + 1)
            step(dve.reciprocal(cf[:, par, :], sm[:, par, :]))
            step(dve.tensor_tensor(cf[:, par, :], cf[:, par, :], gates_, ALU.mult))
            if mask:
                step(dve.tensor_tensor(cf[:, par, 0:1], cf[:, par, 0:1], cst[:, C_VM:C_VM + 1], ALU.mult))
            for br, out, _, _ in parts:
                ins = dve.tensor_scalar(out, out, cf[:, par, br:br + 1], None, ALU.mult)
            step(ins)
            dve.sem_inc(p_scaled, 1)

        def prompt_parts(u):
            t, hh, par = u // NH, u % NH, u % 2
            nk = 128 * (t + 1)
            s, c = bank[par], bank[2 + par]
            ncmp = NWIN if t else 7
            c0 = BLK - 1 if t else BLK - 1 + 128
            p = pb[u % 3]
            return [(0, p[:, 512:512 + ncmp], c[:, 0:ncmp], bias_p[:, hh, c0:256:STRIDE][:, 0:ncmp]),
                    (1, p[:, 0:nk], s[:, 0:nk], bias_p[:, hh, 256 - nk:256]),
                    (2, p[:, 256:256 + nk], s[:, 256:256 + nk], bias_p[:, hh, 256 - nk:256])]

        dve.wait_ge(bias_in, 17 * 16)
        for u in range(17):
            if u < 16:
                if u >= 3:
                    dve.wait_ge(pt_mm, u - 2)
                bias_max(u, u % 2, prompt_parts(u))
            if u:
                v = u - 1
                weigh(v, v % 2, prompt_parts(v), gate[:, v // NH, v % NH:GATES:NH], v < NH)

        def sample_keys(s):
            if s >= 2:
                dve.wait_ge(s_mm, 16 + s - 1)
            even_transposes(4, lambda e, c: e.tensor_copy(
                pastT[s % 2][:, c // 2, c % 2].rearrange("p a b d -> p (a b d)"), bank[6][:, :]))

        def att_squares(t):
            r = ROWS[t]
            return squares(att[0:r, t, :], buf(K0 + NCST + 912 + ATT * (t % 2), ATT)[0:r, :], stats[0:r, 120 + t:121 + t])

        sample_keys(0)
        for s in range(4):
            u, par = 16 + s, s % 2
            if s == 2:
                dve.wait_ge(o_ev, 16)
                att_squares(0)
                step(att_squares(1))
            dve.wait_ge(pt_mm, 16 if s < 2 else u - 1)
            p, b0, b1 = pb[par], bank[2 * par], bank[2 * par + 1]
            parts = [(0, p[:, 528:528 + NWIN], b0[:, 264:264 + NWIN], bias_s[:, BLK - 1:256:STRIDE]),
                     (1, p[:, 0:264], b0[:, 0:264], bias_s),
                     (2, p[:, 264:528], b1[:, 0:264], bias_s)]
            bias_max(u, par, parts)
            if s < 3:
                sample_keys(s + 1)
            weigh(u, par, parts, gs[:, s, :], False)

        dve.wait_ge(attT_ev, 2)
        dve.wait_ge(o_ev, 20)
        step(att_squares(2))
        inv_rms(stats[:, 120:123], stats[:, 120:123], stats[:, 126:129], stats[:, 160:163], ATT)
        for t in range(3):
            r = ROWS[t]
            ins = dve.tensor_scalar(att[0:r, t, :], att[0:r, t, :], stats[0:r, 126 + t:127 + t], None, ALU.mult)
        ins.then_inc(hn_ready, 1)
        even_transposes(KC, lambda e, c: e.tensor_scalar(xT[:, c, 0:TOK], bank[6][:, 0:TOK], gT[:, 3, c:c + 1], None, ALU.mult))

        for c in range(KC):
            dve.wait_ge(hT_raw, c + 1)
            dve.tensor_scalar(hT_g2[:, c, :], hT_in[:, c, 0:TOK], gT[:, 1, c:c + 1], None, ALU.mult).then_inc(hT_scaled, 1)
        step(dve.memset(stats[:, 136:139], 0.0))
        even_transposes(12, lambda e, c: e.tensor_copy(h[:, c // 4, 512 * (c % 4):512 * (c % 4) + 512], bank[6][:, :]))
        dve.wait_ge(t_ev[0], evens[0])
        dve.wait_ge(t_ev[1], odds[0])
        dve.wait_ge(g2_in, 16)
        for t in range(3):
            ins = squares(h[:, t, :], n_tok[:, t, :], stats[:, 136 + t:137 + t])
        step(ins)
        inv_rms(stats[:, 136:139], stats[:, 136:139], stats[:, 139:142], stats[:, 160:163], D)
        dve.sem_inc(n2_ready, 1)
        for t in range(3):
            ins = dve.scalar_tensor_tensor(out=n_tok[:, t, :], in0=h[:, t, :], scalar=stats[:, 139 + t:140 + t],
                                           in1=g2, op0=ALU.mult, op1=ALU.mult)
        step(ins)

        iota = cst[:, C_IOTA:C_IOTA + PK * PK]

        class Best16:

            def __init__(self, n, width, src, cut, val, ix):
                self.n, self.width, self.src, self.cut, self.val, self.ix = n, width, src, cut, val, ix

            def row(self, buf_, r):
                return buf_[:, r * self.width:r * self.width + self.width]

            def values(self, half):
                for r in range(self.n):
                    ins = dve.max(self.val[:, r, 8 * half:8 * half + 8], self.row(self.cut if half else self.src, r))
                step(ins)

            def places(self, half):
                for r in range(self.n):
                    o = slice(8 * half, 8 * half + 8)
                    ins = dve.max_index(self.ix[:, r, o].bitcast(u32), self.val[:, r, o],
                                        self.row(self.cut if half else self.src, r))
                step(ins)

            def cut_out(self):
                for r in range(self.n):
                    ins = dve.match_replace(self.row(self.cut, r), self.val[:, r, 0:8], self.row(self.src, r), -3.0e38)
                step(ins)

        PARTS = 9

        def pick(t, part):
            cand, cut = cands[t], cuts[t]
            halves = Best16(16, NKEY, score[:, t, :], cut, sv, si)
            pairs = Best16(PH, PK * PK, cand.rearrange("p a b c -> p (a b c)"), cut, fv, fi)
            fiu = fi.bitcast(u32)
            if part == 0:
                halves.values(0)
                halves.places(0)
            elif part == 1:
                halves.cut_out()
                halves.values(1)
            elif part == 2:
                halves.places(1)
                step(dve.tensor_copy(si, si.bitcast(u32)))
                for r in range(PH):
                    ins = dve.tensor_tensor(cand[:, r], rep(sv[:, 2 * r, :], [1, PK], [0, PK]),
                                            rep(sv[:, 2 * r + 1, :], [0, PK], [1, PK]), ALU.add)
                step(ins)
            elif part == 3:
                pairs.values(0)
                pairs.places(0)
            elif part == 4:
                pairs.cut_out()
                pairs.values(1)
            elif part == 5:
                pairs.places(1)
                dve.tensor_scalar(fh.bitcast(u32), fiu, 4, None, ALU.logical_shift_right)
                step(dve.tensor_scalar(fl.bitcast(u32), fiu, PK - 1, None, ALU.bitwise_and))
                dve.tensor_copy(fh, fh.bitcast(u32))
                step(dve.tensor_copy(fl, fl.bitcast(u32)))
            elif part < 8:
                side = part - 6
                pos, e = ((fh, e0), (fl, e1))[side]
                step(dve.tensor_tensor(cand, rep(pos, [PK, PH], [1, PK], [0, PK]),
                                       rep(iota, [0, PH], [PK, PK], [1, PK]), ALU.is_equal))
                step(dve.tensor_tensor(cand, cand, rep(si[:, side, :], [2 * PK, PH], [0, PK], [1, PK]), ALU.mult))
                step(dve.tensor_reduce(e, cand, AX.X, ALU.add))
            else:
                step(dve.scalar_tensor_tensor(out=e0, in0=e0, scalar=float(NKEY), in1=e1, op0=ALU.mult, op1=ALU.add))
                step(dve.tensor_copy(idx[:, t, :], e0.rearrange("p a b -> p (a b)")))
                step(dve.tensor_copy(e1[:, :, 0], fv[:, :, 0]))
                step(dve.tensor_tensor(fv, fv, rep(e1, [PK, PH], [0, PK]), ALU.subtract))
                dve.sem_inc(e_in, 1)
                dve.wait_ge(e_out, 4 + t + 1)
                step(dve.tensor_reduce(e1[:, :, 0], fv, AX.X, ALU.add))
                step(dve.reciprocal(e1[:, :, 1], e1[:, :, 0]))
                step(dve.tensor_tensor(wgt[:, t, :].rearrange("p (a b) -> p a b", a=PH), fv,
                                       rep(e1[:, :, 1], [PK, PH], [0, PK]), ALU.mult))
                if t == 2:
                    step(dve.tensor_copy(wgt[64:128, 2, 0:64], wgt[64:128, 2, 64:128]))
                    step(dve.tensor_copy(idx[64:128, 2, 0:64], idx[64:128, 2, 64:128]))
                dve.sem_inc(idx_ready, 1)

        dve.wait_ge(sc_ev, 4)
        for part in range(PARTS):
            pick(0, part)
        dve.sem_inc(u_used, 4)
        dve.sem_inc(v_used, 4)

        dve.wait_ge(sc_ev, 12)

        def group(k, par, t, c0, between=None, after=None):
            dve.tensor_copy(idx4[:, par, :], idx[:, t, c0]).then_inc(idx_set, 1)
            for j in range(4):
                dve.wait_ge(u_in[j], (k + 1) * 16)
                ins = dve.tensor_tensor_reduce(out=u_row[j], in0=u_row[j], in1=n_tok[:, t, :], scale=1.0, scalar=0.0,
                                               op0=ALU.mult, op1=ALU.add, accum_out=a4[:, par, j:j + 1])
                ins.then_inc(u_used, 1)
            dve.wait_ge(u_used, k * 4 + 8)
            dve.sem_inc(dots, 1)
            if between:
                between()
            dve.wait_ge(gelu_done, k + 1)
            dve.tensor_tensor(w4[:, par, :], w4[:, par, :], wgt[:, t, c0], ALU.mult).then_inc(loop_step, 1)
            dve.wait_ge(loop_step, k + 1)
            for j in range(4):
                src = ident if t < 2 else cst[:, C_PAIR:C_PAIR + 64]
                ins = dve.tensor_scalar(diag[:, par, j, 0:(128 if t < 2 else 64)], src, w4[:, par, j:j + 1], None, ALU.mult)
            ins.then_inc(diag_ready, 1)
            if after:
                after()

        def add_peer(t):
            dve.wait_ge(peer_mm, t + 1)
            for q in range(4):
                v = h[0:ROWS[t], t, 512 * q:512 * q + 512]
                ins = dve.tensor_tensor(v, bank[4 * (t % 2) + q][0:ROWS[t], :], v, ALU.add)
            step(ins)
            dve.sem_inc(h_seen, 1)

        def gate_rms():
            for t in range(2):
                step(squares(h[:, t, :], buf(Z0 + 8 * D, D), stats[:, 144 + t:145 + t]))
            inv_rms(stats[:, 144:146], stats[:, 144:146], stats[:, 147:149], stats[:, 160:162], D)

        def prompt_y(b):
            dve.wait_ge(sig_ready, b + 1)
            for t in range(2):
                ins = dve.tensor_tensor(sig[:, t, :], sig[:, t, :], bank[6 + t][:, :], ALU.mult)
            step(ins)
            for t in range(2):
                v = h[:, t, 512 * b:512 * b + 512]
                ins = dve.tensor_tensor(v, v, sig[:, t, :], ALU.add)
            step(ins)
            dve.sem_inc(y_ready, 1)

        def hT_out(rnd):
            dve.wait_ge(hT_mm, rnd + 1)
            for j in range(4):
                c = 8 * rnd + j
                ins = dve.tensor_scalar(hT[:, c, :], bank[4 + j // 2][:, 256 * (j % 2):256 * (j % 2) + 256],
                                        gT[:, 2, c:c + 1], None, ALU.mult)
            ins.then_inc(hT_ev, 1)

        def diag_free(k):
            dve.wait_ge(v_used, 4 * k)

        for i in range(PICKING):
            if i >= 2:
                diag_free(i)
            group(i, i % 2, 0, slice(4 * i, 4 * i + 4),
                  after=(lambda: pick(1 + (i - 1) // PARTS, (i - 1) % PARTS)) if 1 <= i <= 2 * PARTS else None)
        with dve.Fori(0, (GROUPS[0] - PICKING) // 2) as i:
            for jj in range(2):
                diag_free(i * 2 + (PICKING + jj))
                group(i * 2 + (PICKING + jj), jj, 0, bass.ds(i * 8 + 4 * (PICKING + jj), 4))
        with dve.Fori(0, GROUPS[1] // 2) as i:
            for jj in range(2):
                diag_free(i * 2 + (GROUPS[0] + jj))
                group(i * 2 + (GROUPS[0] + jj), jj, 1, bass.ds(i * 8 + 4 * jj, 4))
        extra = {0: lambda: add_peer(0), 1: lambda: add_peer(1), 
                 2: lambda: (gate_rms(), hT_out(0)), 3: lambda: hT_out(1),
                 6: lambda: prompt_y(0), 9: lambda: prompt_y(1), 12: lambda: prompt_y(2)}
        for i in range(GROUPS[2]):
            diag_free(LAST + i)
            group(LAST + i, i % 2, 2, slice(4 * i, 4 * i + 4), extra.get(i))
        prompt_y(3)
        add_peer(2)
        even_transposes(KC, lambda e, c: e.tensor_scalar(hT_s[:, c, :], bank[6][:, 0:64], gT[:, 2, c:c + 1], None, ALU.mult))
        step(squares(h[0:64, 2, :], n_tok[0:64, 2, :], stats[0:64, 146:147]))
        inv_rms(stats[:, 146:147], stats[:, 146:147], stats[:, 149:150], stats[:, 160:161], D)
        dve.sem_inc(h_ready, 1)
        for blk in range(4):
            dve.wait_ge(sig_ready, 4 + blk + 1)
            s = sig[0:64, blk % 2, :]
            step(dve.tensor_tensor(s, s, bank[4 + blk % 2][0:64, :], ALU.mult))
            dve.sem_inc(ple_mm, 1)
            v = h[0:64, 2, 512 * blk:512 * blk + 512]
            step(dve.tensor_tensor(v, v, s, ALU.add))
            dve.sem_inc(y_ready, 1)

    @block.tensor
    def _(pe):
        pe.sem_inc(w_used, 4)
        runs = [0]
        evs = [0, 0]

        def transposes(n, src_of):
            for c in range(n):
                par = c % 2
                if evs[par] >= 1:
                    pe.wait_ge(t_ev[par], evs[par])
                for dst, src, rows in src_of(c):
                    ins = pe.transpose(bank[6 + par][0:src.shape[1], dst:dst + rows], src, ident[0:rows, 0:rows])
                ins.then_inc(t_mm, 1)
                evs[par] += 1

        def tok_tiles(src, rows=ROWS):
            return lambda c: [(128 * t, src(t, c)[0:rows[t], :], rows[t]) for t in range(3)]

        pe.wait_ge(cst_in, 16)
        pe.wait_ge(first_in, 32)
        pe.wait_ge(dve_step, 2)
        pe.matmul(bank[0][0:NH, 0:NBIAS], tab[0:NBUCKET + 1, :], cst[0:NBUCKET + 1, C_OH:C_OH + NBIAS],
                  start=True, stop=True).then_inc(bias_mm, 1)
        pe.wait_ge(x_in, 48)
        transposes(KC, tok_tiles(lambda t, c: h[:, t, 128 * c:128 * c + 128]))
        pe.wait_ge(t_ev[0], 8)
        pe.wait_ge(t_ev[1], 8)
        pe.wait_ge(bias_sb, 1)

        def product(n, done, f, par, width=512):
            pe.wait_ge(mm_ev, done)
            for half in range(2):
                slot = (2 * par + half) % 4
                pe.wait_ge(w_in[slot], f)
                for t in range(3):
                    for k in range(8):
                        ins = pe.matmul(bank[3 * par + t][0:ROWS[t], 0:width], xT[:, 8 * half + k, 128 * t:128 * t + ROWS[t]],
                                        ring[slot][:, k, 0:width], start=(half == 0 and k == 0), stop=(half == 1 and k == 7))
                ins.then_inc(w_used, 1)

        def blocks(first, count):
            with pe.Fori(0, count // 2) as i:
                for par in range(2):
                    product(None, i * 2 + (first + par + 1), i * 16 + (8 * first + 16), par)
                    pe.wait_ge(w_used, i * 4 + (4 + 2 * (first + par + 1)))
                    pe.sem_inc(mm_done, 1)

        blocks(0, 6)
        blocks(6, 4)
        for n in (10, 11):
            product(None, n + 1, 16 * (n // 2) + 16, n % 2, 512 if n == 10 else GATES)
            pe.wait_ge(w_used, 4 + 2 * (n + 1))
            pe.sem_inc(mm_done, 1)

        def raw_rows(kind):
            def src(c):
                if c == 0:
                    c0 = ATT + 256 * kind
                    return [(256 * g + 128 * t, z[:, t, c0 + g * HD:c0 + g * HD + HD], 128) for g in range(2) for t in range(2)]
                if c <= NB:
                    pe.wait_ge(page_s[c - 1], 32 * (kind + 1))
                    return [(128 * (2 * a + g), page_in[:, c - 1, a, g * HD:g * HD + HD], 128) for a in range(2) for g in range(2)]
                pe.wait_ge(pe_in_s, 32)
                return [(0, pe_in[kind][0:BLK, :], BLK)]
            transposes(NB + 2, src)

        def first_layer(kind):
            pe.wait_ge(t_ev[0], evs[0])
            pe.wait_ge(t_ev[1], evs[1])
            for hb in range(2):
                if kind:
                    pe.wait_ge(hid_ready, hb + 1)
                for m in range(BLK):
                    if hb == 0 and m in (0, W1_CUT):
                        pe.wait_ge(w1_in[m // W1_CUT], 16 * (kind + 1))
                    view = raw[kind][:, :, m:m + STRIDE * (NWIN - 1) + 1:STRIDE]
                    ins = pe.matmul(bank[hb][:, 0:(SEQS + 1) * NWIN], w1[:, m, hb * 128:hb * 128 + 128], view,
                                    start=(m == 0), stop=(m == BLK - 1))
                ins.then_inc(cmp_mm, 1)

        pe.wait_ge(mm_ev, 2 + 12)
        raw_rows(0)
        first_layer(0)
        raw_rows(1)
        pe.wait_ge(hid_ready, 2)
        pe.wait_ge(w2_in, 32)
        for i in range(3):
            for hb in range(2):
                ins = pe.matmul(bank[2][0:90, i * HD:i * HD + HD], hid[:, hb, 90 * i:90 * i + 90], w2[0][:, hb, :],
                                start=(hb == 0), stop=(hb == 1))
        ins.then_inc(kc_mm, 1)
        pe.wait_ge(qkv_ready, 1)
        transposes(12, tok_tiles(lambda t, c: z[:, t, TBLOCKS[c]:TBLOCKS[c] + 128]))
        first_layer(1)
        pe.wait_ge(kc_ready, 1)
        for i in range(3):
            ins = pe.transpose(bank[3][:, 90 * i:90 * i + 90], kct[0:90, i, :], ident[0:90, 0:90])
        ins.then_inc(kcT_mm, 1)
        pe.wait_ge(hid_ready, 4)
        for sg in range(SEQS):
            q = sg // 4
            for hb in range(2):
                ins = pe.matmul(bank[(2, 4, 5, 6, 0)[q]][0:NWIN, (sg % 4) * HD:(sg % 4) * HD + HD],
                                hid[:, hb, NWIN * sg:NWIN * sg + NWIN], w2[1][:, hb, :], start=(hb == 0), stop=(hb == 1))
            if sg % 4 == 3 or sg == SEQS - 1:
                ins.then_inc(kc_mm, 1)
        for s in range(4):
            ins = pe.matmul(bank[1][:, GATES * s:GATES * s + GATES], cst[0:64, C_SELG + 128 * s:C_SELG + 128 * s + 128],
                            gate[0:64, 2, :], start=True, stop=True)
        ins.then_inc(gs_mm, 1)
        pe.wait_ge(cmp_done, 7)

        def scores(u):
            t, hh, par = u // NH, u % NH, u % 2
            g = hh // HPG
            nk = 128 * (t + 1)
            if u >= 2:
                pe.wait_ge(biased, u - 1)
            q = qkT[:, hh, 128 * t:128 * t + 128]
            pe.matmul(bank[par][:, 0:nk], q, qkT[:, 8 + g, 0:nk], start=True, stop=True)
            pe.matmul(bank[par][:, 256:256 + nk], q, qkT[:, 10 + g, 0:nk], start=True, stop=True)
            ncmp = NWIN if t else 7
            pe.matmul(bank[2 + par][:, 0:ncmp], q, kcT[:, g * NWIN:g * NWIN + ncmp], start=True, stop=True).then_inc(s_mm, 1)

        def turn_probs(u):
            t, par = u // NH, u % 2
            ncmp = NWIN if t else 7
            pe.wait_ge(p_scaled, u + 1)
            if u >= 2:
                pe.wait_ge(o_ev, u - 1)
            for w in range(2):
                for k in range(t + 1):
                    pe.transpose(bank[4 + par][:, 256 * w + 128 * k:256 * w + 128 * k + 128],
                                 pb[u % 3][:, 256 * w + 128 * k:256 * w + 128 * k + 128], ident)
            pe.transpose(bank[6 + par][0:ncmp, 128:256], pb[u % 3][:, 512:512 + ncmp], ident).then_inc(pt_mm, 1)

        def values(u):
            t, hh, par = u // NH, u % NH, u % 2
            g = hh // HPG
            ncmp = NWIN if t else 7
            pe.wait_ge(pt_ev, u + 1)
            first = True
            for w in range(2):
                for k in range(t + 1):
                    pe.matmul(bank[6 + par][:, 0:HD], pT[:, par, 256 * w + 128 * k:256 * w + 128 * k + 128],
                              z[:, k, (1792, 2304)[w] + g * HD:(1792, 2304)[w] + g * HD + HD], start=first, stop=False)
                    first = False
            pe.matmul(bank[6 + par][:, 0:HD], pT[0:ncmp, par, 512:640], vc[0:ncmp, g, :], start=False, stop=True)\
              .then_inc(o_mm, 1)

        scores(0)
        scores(1)
        for u in range(16):
            if u < 14:
                scores(u + 2)
            turn_probs(u)
            values(u)
        pe.wait_ge(o_ev, 16)

        def sample_scores(s):
            pe.wait_ge(past_k[s % 2], 96 * (s // 2 + 1))
            transposes(4, lambda c: [(128 * (2 * a + g), past_rows(s, c // 2, c % 2, a)[:, g * HD:g * HD + HD], 128)
                                     for a in range(2) for g in range(2)])
            pe.wait_ge(t_ev[0], evs[0])
            pe.wait_ge(t_ev[1], evs[1])
            pe.wait_ge(biased, 16 if s < 2 else 16 + s - 1)
            for bb in range(2):
                b = 2 * s + bb
                for g in range(NG):
                    p0 = 64 * bb + 32 * g
                    q = qsT[:, b, HPG * g:HPG * g + HPG, :].rearrange("p h t -> p (h t)")
                    for br in range(2):
                        for a in range(2):
                            pe.matmul(bank[2 * (s % 2) + br][p0:p0 + 32, 128 * a:128 * a + 128], q, pastT[s % 2][:, bb, br, a, g, :],
                                      start=True, stop=True)
                        pe.matmul(bank[2 * (s % 2) + br][p0:p0 + 32, 256:264], q, qkT[:, 8 + 2 * br + g, 256 + b * NT:256 + b * NT + NT],
                                  start=True, stop=True)
                    sg = 2 * (1 + b) + g
                    ins = pe.matmul(bank[2 * (s % 2)][p0:p0 + 32, 264:264 + NWIN], q, kcT[:, sg * NWIN:sg * NWIN + NWIN],
                                    start=True, stop=True)
            ins.then_inc(s_mm, 1)

        def sample_values(s):
            u = 16 + s
            p = pb[s % 2]
            pe.wait_ge(past_v[s % 2], 96 * (s // 2 + 1))
            pe.wait_ge(p_scaled, u + 1)
            pe.wait_ge(o_ev, u)
            for w in range(2):
                for k in range(2):
                    pe.transpose(bank[4][:, 256 * w + 128 * k:256 * w + 128 * k + 128],
                                 p[:, 264 * w + 128 * k:264 * w + 128 * k + 128], ident)
                pe.transpose(bank[5][0:NT, 128 * w:128 * w + 128], p[:, 264 * w + 256:264 * w + 264], ident)
            pe.transpose(bank[5][0:NWIN, 256:384], p[:, 528:528 + NWIN], ident).then_inc(pt_mm, 1)
            pe.wait_ge(pt_ev, u + 1)
            if s == 0:
                pe.wait_ge(vn_in, 16 * 2 * NB)
            for bb in range(2):
                b = 2 * s + bb
                for g in range(NG):
                    r = slice(64 * bb + 32 * g, 64 * bb + 32 * g + 32)
                    o = bank[5][:, 384 + r.start:384 + r.stop]
                    for w in range(2):
                        for k in range(2):
                            pe.matmul(o, past_rows(s, bb, w, k)[:, 256 + g * HD:256 + g * HD + HD],
                                      pT[:, 0, 256 * w + 128 * k + r.start:256 * w + 128 * k + r.stop],
                                      start=(w == 0 and k == 0), stop=False)
                        pe.matmul(o, vn[0:NT, b, w, g * HD:g * HD + HD],
                                  pT[0:NT, 0, 512 + 128 * w + r.start:512 + 128 * w + r.stop], start=False, stop=False)
                    ins = pe.matmul(o, vc[0:NWIN, 2 * (1 + b) + g, :], pT[0:NWIN, 0, 768 + r.start:768 + r.stop],
                                    start=False, stop=True)
            ins.then_inc(o_mm, 1)

        sample_scores(0)
        for s in range(4):
            if s < 3:
                sample_scores(s + 1)
            sample_values(s)
        pe.wait_ge(o_ev, 20)
        for i in range(2):
            for j in range(4):
                ins = pe.transpose(bank[i][0:64, 128 * j:128 * j + 128], attT[:, 4 * i + j, :], ident)
            ins.then_inc(attT_mm, 1)

        pe.wait_ge(hn_ready, 1)
        pe.sem_inc(merged, 1)
        transposes(KC, tok_tiles(lambda t, c: (att if c < 8 else bg)[:, t, 128 * (c % 8):128 * (c % 8) + 128]))
        pe.wait_ge(t_ev[0], evs[0])
        pe.wait_ge(t_ev[1], evs[1])

        def channels_down(n, src, last):
            for half in range(2):
                slot = (2 * n + half) % 4
                pe.wait_ge(w_in[slot], 16 * (n // 2) + 16)
                for sub in range(4):
                    for k in range(8):
                        ins = pe.matmul(bank[4 * (n % 2) + sub][:, 0:TOK], ring[slot][:, k, 128 * sub:128 * sub + 128],
                                        src[:, 8 * half + k, 0:TOK], start=(half == 0 and k == 0),
                                        stop=(last and half == 1 and k == 7))
                ins.then_inc(w_used, 1)

        for blk in range(4):
            if blk >= 2:
                pe.wait_ge(hT_raw, 4 * (blk - 1))
            channels_down(N_OUT + blk, xT, False)
            if blk == 0:
                pe.wait_ge(x_in, 96)
            for sub in range(4):
                for t in range(3):
                    c = 4 * blk + sub
                    ins = pe.matmul(bank[4 * (blk % 2) + sub][:, 128 * t:128 * t + ROWS[t]], h[0:ROWS[t], t, 128 * c:128 * c + 128],
                                    ident[0:ROWS[t], 0:ROWS[t]], start=False, stop=(t == 2))
            ins.then_inc(mm_done, 1)

        pe.wait_ge(hT_raw, KC)
        pe.wait_ge(hT_scaled, KC)
        for blk in range(4):
            if blk >= 2:
                pe.wait_ge(qT_done, blk - 1)
            n = N_WQ + blk
            channels_down(n, hT_g2, True)
            pe.wait_ge(w_used, 4 + 2 * (n + 1))
            pe.sem_inc(mm_done, 1)
            if blk == 0:
                transposes(12, lambda c: [(128 * j, hT_in[:, 4 * (c % 4) + j, 128 * (c // 4):128 * (c // 4) + 128], 128)
                                          for j in range(4)])
                pe.wait_ge(t_ev[0], evs[0])
                pe.wait_ge(t_ev[1], evs[1])
        pe.wait_ge(qT_done, 4)
        pe.wait_ge(keys_s, 16)
        for a in range(2):
            ins = pe.transpose(bank[0][:, 128 * a:128 * a + 128], keys_in[:, a, :], ident)
        ins.then_inc(keys_mm, 1)
        pe.wait_ge(keys_ev, 1)
        for t in range(3):
            for q in range(4):
                if t == 2:
                    pe.wait_ge(sc_ev, q + 1)
                for j in range(4):
                    c = 4 * q + j
                    ins = pe.matmul(bank[4 * (t % 2) + q][:, 128 * j:128 * j + 128], qT[:, c, 128 * t:128 * t + 128],
                                    keysT[:, c % 2, :], start=True, stop=True)
                ins.then_inc(sc_mm, 1)
        pe.wait_ge(sc_ev, 12)
        pe.wait_ge(p_in_s, 48)
        for c in range(2):
            for t in range(3):
                ins = pe.transpose(bank[c][:, 128 * t:128 * t + ROWS[t]], p_in[0:ROWS[t], t, 128 * c:128 * c + 128],
                                   ident[0:ROWS[t], 0:ROWS[t]])
        ins.then_inc(pleT_mm, 1)
        pe.wait_ge(pleT_ev, 1)

        def weighted_rows(k, par, t, first, last):
            m = 128 if t < 2 else 64
            pe.wait_ge(diag_ready, k + 1)
            for j in range(4):
                pe.wait_ge(v_in[j], (k + 1) * 16)
                for q in range(4):
                    ins = pe.matmul(bank[4 * (t % 2) + q][0:m, :], diag[:, par, j, 0:m], v_row[j][:, 512 * q:512 * q + 512],
                                    start=(first and j == 0), stop=(last and j == 3))
                ins.then_inc(v_used, 1)

        def tile_done(n):
            pe.wait_ge(v_used, 4 * n + 4)
            pe.sem_inc(peer_mm, 1)

        end0, end1 = GROUPS[0], LAST
        weighted_rows(0, 0, 0, True, False)
        with pe.Fori(0, (GROUPS[0] - 2) // 2) as i:
            for jj in range(2):
                weighted_rows(i * 2 + (1 + jj), (1 + jj) % 2, 0, False, False)
        weighted_rows(end0 - 1, 1, 0, False, True)
        tile_done(end0)
        weighted_rows(end0, 0, 1, True, False)
        with pe.Fori(0, (GROUPS[1] - 2) // 2) as i:
            for jj in range(2):
                weighted_rows(i * 2 + (end0 + 1 + jj), (1 + jj) % 2, 1, False, False)
        weighted_rows(end1 - 1, 1, 1, False, True)
        tile_done(end1)

        for i in range(GROUPS[2]):
            if i == 0:
                pe.wait_ge(h_seen, 1)
            weighted_rows(end1 + i, i % 2, 2, i == 0, i == GROUPS[2] - 1)
            if i in (1, 2):
                pe.wait_ge(h_seen, 2)
                if i == 2:
                    pe.wait_ge(hT_ev, 2)
                for j in range(8):
                    c = 8 * (i - 1) + j
                    for t in range(2):
                        ins = pe.transpose(bank[4 + j // 2][:, 256 * (j % 2) + 128 * t:256 * (j % 2) + 128 * t + 128],
                                           h[:, t, 128 * c:128 * c + 128], ident)
                ins.then_inc(hT_mm, 1)
            for q in gate_quarters(i):
                blk, part = divmod(q, 4)
                if part == 0:
                    if blk == 0:
                        pe.wait_ge(hT_ev, 4)
                        pe.wait_ge(ple_in, 16)
                    else:
                        pe.wait_ge(y_ready, blk)
                    for t in range(2):
                        for c in range(2):
                            pe.matmul(bank[6 + t][:, :], pleT[:, c, 128 * t:128 * t + 128], ple_w[:, c, 512 * blk:512 * blk + 512],
                                      start=(c == 0), stop=(c == 1))
                pe.wait_ge(gw_in[q % 3], 16 * (q // 3 + 1))
                for t in range(2):
                    for k in range(4):
                        ins = pe.matmul(bank[4 + t][:, :], hT[:, 4 * part + k, 128 * t:128 * t + 128], gate_w[q % 3][:, k, :],
                                        start=(part == 0 and k == 0), stop=(part == 3 and k == 3))
                ins.then_inc(gw_used, 1)
                if part == 3:
                    pe.wait_ge(gw_used, q + 1)
                    pe.sem_inc(gate_mm, 1)
        tile_done(end1 + GROUPS[2])

        def sample_ple(blk):
            for c in range(2):
                pe.matmul(bank[4 + blk % 2][0:64, :], pleT[:, c, 256:TOK], ple_w[:, c, 512 * blk:512 * blk + 512],
                          start=(c == 0), stop=(c == 1))

        pe.wait_ge(y_ready, 4)
        sample_ple(0)
        sample_ple(1)
        pe.wait_ge(h_seen, 3)
        transposes(KC, lambda c: [(0, h[0:64, 2, 128 * c:128 * c + 128], 64)])
        pe.wait_ge(t_ev[0], evs[0])
        pe.wait_ge(t_ev[1], evs[1])
        for blk in range(4):
            n = N_GATE + blk
            if blk >= 2:
                pe.wait_ge(ple_mm, blk - 1)
                pe.wait_ge(sig_ready, 4 + blk - 1)
                sample_ple(blk)
            for half in range(2):
                slot = (2 * blk + half) % 4
                pe.wait_ge(w_in[slot], 16 * (n // 2) + 16)
                for k in range(8):
                    ins = pe.matmul(bank[blk % 2][0:64, :], hT_s[:, 8 * half + k, :], ring[slot][:, k, :],
                                    start=(half == 0 and k == 0), stop=(half == 1 and k == 7))
                ins.then_inc(w_used, 1)
            pe.wait_ge(w_used, 4 + 2 * (n + 1))
            pe.sem_inc(mm_done, 1)

    ctx.close()


_INS = ["x_prompt", "x_sample", "p_prompt", "p_sample", "cache_kv", "state_win", "state_conv", "page_table", "rel_bias",
        "norm1", "w_in", "qk_gain", "cmp_pe", "cmp_w1", "cmp_w2", "conv_w", "conv_b", "out_gain", "w_out", "norm2",
        "peer_wq", "peer_keys", "peer_u", "peer_v", "norm3", "ple_gate", "ple_proj"]
_OUTS = [(1, NP, D), (NB, NT, D), (1, 1, NP, 4, NG, HD), (1, 1, NP, 2, NG, HD), (1, 1, 2, CONV),
         (1, NB, NT, 4, NG, HD), (1, NB, PAST, 2, NG, HD), (1, NB, 2, CONV)]


def kernel(**inputs):
    import concourse.bacc as bacc
    from concourse.bass_utils import run_bass_kernel_spmd

    nc = bacc.Bacc("TRN2", target_bir_lowering=False, num_devices=1)
    arrays, ins = {}, {}
    for name in _INS:
        a = np.ascontiguousarray(inputs[name])
        arrays[f"in_{name}"] = a
        ins[name] = nc.dram_tensor(f"in_{name}", a.shape, mybir.dt.from_np(a.dtype), kind="ExternalInput").ap()
    arrays["in_cst"] = shape_constants()
    ins["cst"] = nc.dram_tensor("in_cst", (128, NCST), mybir.dt.float32, kind="ExternalInput").ap()
    outs = [nc.dram_tensor(f"out_{i}", s, mybir.dt.float32, kind="ExternalOutput").ap() for i, s in enumerate(_OUTS)]
    build(nc, ins, outs)
    r = run_bass_kernel_spmd(nc, [arrays], core_ids=[0])
    return tuple(r.results[0][f"out_{i}"] for i in range(len(_OUTS)))
```
